# Optimizing a Trainium2 kernel written in Bass

```python
import jax, jax.numpy as jnp
from jax import lax
import numpy as np
import math
import jax
import jax.numpy as jnp

D_MODEL = 1024
BATCH = 1
SEQ = 256
DEPTH = 2

N_MEM = 256
EPS = 1e-6
A_WIDTH = D_MODEL // 2
A_CONV = 3
B_HEADS = 8
B_HEAD_DIM = D_MODEL // (2 * B_HEADS)
DILATED_PATTERN = ((128, 1), (512, 4), (2048, 16))
C_HEADS = 8
C_HEAD_DIM = D_MODEL // C_HEADS
C_CONV = 4
C_CHUNK = 64
X_HEADS = 4
X_HEAD_DIM = 64
D_FF = 2816
N_EXPERTS = 8
TOP_K = 2
D_FF_EXPERT = D_FF // 2
N_EVEN = (DEPTH + 1) // 2
N_ODD = DEPTH // 2


def rms_norm(x, g):
    xf = x.astype(jnp.float32)
    y = xf * lax.rsqrt(jnp.mean(xf * xf, axis=-1, keepdims=True) + EPS)
    return (y * g.astype(jnp.float32)).astype(x.dtype)

def l2_norm(x):
    xf = x.astype(jnp.float32)
    return xf * lax.rsqrt(jnp.sum(xf * xf, axis=-1, keepdims=True) + EPS)

def causal_dwconv(x, w):
    k = w.shape[0]
    return lax.conv_general_dilated(x, w[:, None, :], window_strides=(1,), padding=[(k - 1, 0)],
                                    dimension_numbers=('NWC', 'WIO', 'NWC'),
                                    feature_group_count=x.shape[-1])

def banded_attention(q, k, v, w):
    n, L, h, hd = q.shape
    nb = -(-L // w)
    pad = nb * w - L
    q = jnp.pad(q, ((0, 0), (0, pad), (0, 0), (0, 0))).reshape(n, nb, w, h, hd)
    k = jnp.pad(k, ((0, 0), (w, pad), (0, 0), (0, 0))).reshape(n, nb + 1, w, h, hd)
    v = jnp.pad(v, ((0, 0), (w, pad), (0, 0), (0, 0))).reshape(n, nb + 1, w, h, hd)
    k2 = jnp.concatenate([k[:, :-1], k[:, 1:]], axis=2)
    v2 = jnp.concatenate([v[:, :-1], v[:, 1:]], axis=2)
    s = jnp.einsum('nbqhd,nbkhd->nbhqk', q, k2).astype(jnp.float32) * (hd ** -0.5)
    qi = jnp.arange(w)[:, None]
    kj = jnp.arange(2 * w)[None, :]
    dist = qi + w - kj
    kpos = jnp.arange(nb)[:, None, None] * w + kj[None] - w
    valid = (dist >= 0) & (dist <= w) & (kpos >= 0)
    s = jnp.where(valid[None, :, None], s, -jnp.inf)
    m = jnp.max(s, axis=-1, keepdims=True)
    p = jnp.exp(s - m)
    den = jnp.sum(p, axis=-1)
    o = jnp.einsum('nbhqk,nbkhd->nbqhd', p, v2.astype(jnp.float32))
    o = o / jnp.moveaxis(den, 2, 3)[..., None]
    lse = m[..., 0] + jnp.log(den)
    o = o.reshape(n, nb * w, h, hd)[:, :L]
    lse = jnp.moveaxis(lse, 2, 3).reshape(n, nb * w, h)[:, :L]
    return o, lse

def dilated_attention(q, k, v):
    b, s, h, hd = q.shape
    outs, lses = [], []
    for window, d in DILATED_PATTERN:
        L = s // d
        def to_sub(t):
            return t.reshape(b, L, d, h, hd).transpose(0, 2, 1, 3, 4).reshape(b * d, L, h, hd)
        o, lse = banded_attention(to_sub(q), to_sub(k), to_sub(v), window // d)
        outs.append(o.reshape(b, d, L, h, hd).transpose(0, 2, 1, 3, 4).reshape(b, s, h, hd))
        lses.append(lse.reshape(b, d, L, h).transpose(0, 2, 1, 3).reshape(b, s, h))
    wts = jax.nn.softmax(jnp.stack(lses), axis=0)
    return jnp.einsum('gbsh,gbshd->bshd', wts, jnp.stack(outs))

def conv_dilated_mixer(u, w_in, conv_w, q_g, k_g, w_out):
    b, s, _ = u.shape
    gb, gc, xc, q, k, v = jnp.split(u @ w_in, 6, axis=-1)
    a = gb * causal_dwconv(gc * xc, conv_w)
    q = rms_norm(q.reshape(b, s, B_HEADS, B_HEAD_DIM), q_g)
    k = rms_norm(k.reshape(b, s, B_HEADS, B_HEAD_DIM), k_g)
    v = v.reshape(b, s, B_HEADS, B_HEAD_DIM)
    o = dilated_attention(q, k, v).astype(u.dtype).reshape(b, s, B_HEADS * B_HEAD_DIM)
    return jnp.concatenate([a, o], axis=-1) @ w_out

def gated_delta_rule(q, k, v, beta, g):
    b, s, h, dk = q.shape
    dv = v.shape[-1]
    nc = s // C_CHUNK
    def chunk(t):
        t = t.astype(jnp.float32).reshape((b, nc, C_CHUNK) + t.shape[2:])
        return jnp.moveaxis(t, 3, 2)
    q = chunk(l2_norm(q)) * (dk ** -0.5)
    k = chunk(l2_norm(k))
    v = chunk(v)
    beta = chunk(beta)
    gc = jnp.cumsum(chunk(g), axis=-1)
    causal = jnp.tril(jnp.ones((C_CHUNK, C_CHUNK), dtype=bool))
    strict = jnp.tril(jnp.ones((C_CHUNK, C_CHUNK), dtype=bool), -1)
    decay = jnp.exp(jnp.where(causal, gc[..., :, None] - gc[..., None, :], -jnp.inf))
    kk = jnp.einsum('bnhid,bnhjd->bnhij', k, k)
    a_mat = jnp.where(strict, beta[..., :, None] * kk * decay, 0.0) + jnp.eye(C_CHUNK, dtype=jnp.float32)
    u = lax.linalg.triangular_solve(a_mat, v * beta[..., None], left_side=True, lower=True, unit_diagonal=True)
    w = lax.linalg.triangular_solve(a_mat, k * (beta * jnp.exp(gc))[..., None], left_side=True, lower=True,
                                    unit_diagonal=True)
    attn = jnp.einsum('bnhid,bnhjd->bnhij', q, k) * decay
    q_dec = q * jnp.exp(gc)[..., None]
    k_dec = k * jnp.exp(gc[..., -1:] - gc)[..., None]
    g_last = jnp.exp(gc[..., -1])

    def step(state, inp):
        qd, kd, uc, wc, at, gl = inp
        v_new = uc - jnp.einsum('bhcd,bhde->bhce', wc, state)
        o = jnp.einsum('bhcd,bhde->bhce', qd, state) + jnp.einsum('bhij,bhje->bhie', at, v_new)
        state = state * gl[..., None, None] + jnp.einsum('bhcd,bhce->bhde', kd, v_new)
        return state, o

    xs = (jnp.moveaxis(q_dec, 1, 0), jnp.moveaxis(k_dec, 1, 0), jnp.moveaxis(u, 1, 0),
          jnp.moveaxis(w, 1, 0), jnp.moveaxis(attn, 1, 0), jnp.moveaxis(g_last, 1, 0))
    state0 = jnp.zeros((b, h, dk, dv), jnp.float32)
    _, o = lax.scan(step, state0, xs)
    return jnp.moveaxis(jnp.moveaxis(o, 0, 1), 2, 3).reshape(b, s, h, dv)

def deltanet_mixer(u, w_in, conv_w, a_log, dt_bias, o_g, w_out):
    b, s, _ = u.shape
    proj = u @ w_in
    qkv, gate, bb, aa = jnp.split(proj, [3 * D_MODEL, 4 * D_MODEL, 4 * D_MODEL + C_HEADS], axis=-1)
    qkv = jax.nn.silu(causal_dwconv(qkv, conv_w))
    q, k, v = [t.reshape(b, s, C_HEADS, C_HEAD_DIM) for t in jnp.split(qkv, 3, axis=-1)]
    beta = jax.nn.sigmoid(bb.astype(jnp.float32))
    g = -jnp.exp(a_log.astype(jnp.float32)) * jax.nn.softplus(aa.astype(jnp.float32) + dt_bias.astype(jnp.float32))
    o = gated_delta_rule(q, k, v, beta, g)
    o = rms_norm(o, o_g).astype(u.dtype) * jax.nn.silu(gate.reshape(b, s, C_HEADS, C_HEAD_DIM))
    return o.reshape(b, s, C_HEADS * C_HEAD_DIM) @ w_out

def memory_cross_attention(u, mem_n, w_q, w_kv, q_g, k_g, w_o):
    b, s, _ = u.shape
    m = mem_n.shape[1]
    q = rms_norm((u @ w_q).reshape(b, s, X_HEADS, X_HEAD_DIM), q_g)
    k, v = jnp.split(mem_n @ w_kv, 2, axis=-1)
    k = rms_norm(k.reshape(b, m, X_HEADS, X_HEAD_DIM), k_g)
    v = v.reshape(b, m, X_HEADS, X_HEAD_DIM)
    sc = jnp.einsum('bshd,bmhd->bhsm', q, k).astype(jnp.float32) * (X_HEAD_DIM ** -0.5)
    p = jax.nn.softmax(sc, axis=-1).astype(v.dtype)
    o = jnp.einsum('bhsm,bmhd->bshd', p, v).reshape(b, s, X_HEADS * X_HEAD_DIM)
    return o @ w_o

def swiglu(u, w_gu, w_down):
    gt, up = jnp.split(u @ w_gu, 2, axis=-1)
    return (jax.nn.silu(gt) * up) @ w_down

def moe_swiglu(u, router, w_gu, w_down):
    logits = (u @ router).astype(jnp.float32)
    top_val, top_idx = lax.top_k(logits, TOP_K)
    top_w = jax.nn.softmax(top_val, axis=-1)
    combine = jnp.sum(jax.nn.one_hot(top_idx, N_EXPERTS, dtype=jnp.float32) * top_w[..., None], axis=-2)
    y = jnp.zeros_like(u)
    for e in range(N_EXPERTS):
        y = y + combine[..., e:e + 1].astype(u.dtype) * swiglu(u, w_gu[e], w_down[e])
    return y

def first_inputs(seed: int = 0) -> dict:
    key = jax.random.key(seed)
    ks = iter(jax.random.split(key, 40))
    def nrm(shape, scale):
        return jax.random.normal(next(ks), shape, jnp.float32) * scale
    def gain(shape):
        return 1.0 + 0.02 * jax.random.normal(next(ks), shape, jnp.float32)
    d = D_MODEL
    dt = jnp.exp(jax.random.uniform(next(ks), (N_ODD, C_HEADS), jnp.float32, np.log(1e-3), np.log(1e-1)))
    return {
        'x': nrm((BATCH, SEQ, d), 1.0),
        'mem': nrm((BATCH, N_MEM, d), 1.0),
        'norm_mix': gain((DEPTH, d)),
        'norm_xattn': gain((DEPTH, d)),
        'norm_mem': gain((DEPTH, d)),
        'norm_ffn': gain((DEPTH, d)),
        'ev_w_in': nrm((N_EVEN, d, 3 * A_WIDTH + 3 * B_HEADS * B_HEAD_DIM), d ** -0.5),
        'ev_conv': nrm((N_EVEN, A_CONV, A_WIDTH), A_CONV ** -0.5),
        'ev_q_norm': gain((N_EVEN, B_HEAD_DIM)),
        'ev_k_norm': gain((N_EVEN, B_HEAD_DIM)),
        'ev_w_out': nrm((N_EVEN, A_WIDTH + B_HEADS * B_HEAD_DIM, d), (A_WIDTH + B_HEADS * B_HEAD_DIM) ** -0.5),
        'od_w_in': nrm((N_ODD, d, 4 * C_HEADS * C_HEAD_DIM + 2 * C_HEADS), d ** -0.5),
        'od_conv': nrm((N_ODD, C_CONV, 3 * C_HEADS * C_HEAD_DIM), C_CONV ** -0.5),
        'od_a_log': jnp.log(jax.random.uniform(next(ks), (N_ODD, C_HEADS), jnp.float32, 1.0, 16.0)),
        'od_dt_bias': jnp.log(jnp.expm1(dt)),
        'od_o_norm': gain((N_ODD, C_HEAD_DIM)),
        'od_w_out': nrm((N_ODD, C_HEADS * C_HEAD_DIM, d), (C_HEADS * C_HEAD_DIM) ** -0.5),
        'xa_w_q': nrm((DEPTH, d, X_HEADS * X_HEAD_DIM), d ** -0.5),
        'xa_w_kv': nrm((DEPTH, d, 2 * X_HEADS * X_HEAD_DIM), d ** -0.5),
        'xa_q_norm': gain((DEPTH, X_HEAD_DIM)),
        'xa_k_norm': gain((DEPTH, X_HEAD_DIM)),
        'xa_w_o': nrm((DEPTH, X_HEADS * X_HEAD_DIM, d), (X_HEADS * X_HEAD_DIM) ** -0.5),
        'ff_w_gu': nrm((N_EVEN, d, 2 * D_FF), d ** -0.5),
        'ff_w_down': nrm((N_EVEN, D_FF, d), D_FF ** -0.5),
        'moe_router': nrm((N_ODD, d, N_EXPERTS), d ** -0.5),
        'moe_w_gu': nrm((N_ODD, N_EXPERTS, d, 2 * D_FF_EXPERT), d ** -0.5),
        'moe_w_down': nrm((N_ODD, N_EXPERTS, D_FF_EXPERT, d), D_FF_EXPERT ** -0.5),
    }

def first_block(x, mem, norm_mix, norm_xattn, norm_mem, norm_ffn,
              ev_w_in, ev_conv, ev_q_norm, ev_k_norm, ev_w_out,
              od_w_in, od_conv, od_a_log, od_dt_bias, od_o_norm, od_w_out,
              xa_w_q, xa_w_kv, xa_q_norm, xa_k_norm, xa_w_o,
              ff_w_gu, ff_w_down, moe_router, moe_w_gu, moe_w_down):
    h = x
    for layer in range(DEPTH):
        i = layer // 2
        u = rms_norm(h, norm_mix[layer])
        if layer % 2 == 0:
            h = h + conv_dilated_mixer(u, ev_w_in[i], ev_conv[i], ev_q_norm[i], ev_k_norm[i], ev_w_out[i])
        else:
            h = h + deltanet_mixer(u, od_w_in[i], od_conv[i], od_a_log[i], od_dt_bias[i], od_o_norm[i], od_w_out[i])
        h = h + memory_cross_attention(rms_norm(h, norm_xattn[layer]), rms_norm(mem, norm_mem[layer]),
                                       xa_w_q[layer], xa_w_kv[layer], xa_q_norm[layer], xa_k_norm[layer],
                                       xa_w_o[layer])
        u = rms_norm(h, norm_ffn[layer])
        if layer % 2 == 0:
            h = h + swiglu(u, ff_w_gu[i], ff_w_down[i])
        else:
            h = h + moe_swiglu(u, moe_router[i], moe_w_gu[i], moe_w_down[i])
    return h


N_META = 16
BLOCK = 128
D_INNER = 2 * D_MODEL
SSD_HEAD_DIM = 64
SSD_HEADS = D_INNER // SSD_HEAD_DIM
SSD_GROUPS = 8
SSD_HEADS_PER_GROUP = SSD_HEADS // SSD_GROUPS
SSD_STATE = 128
CONV_WIDTH = 4
CONV_DIM = D_INNER + 2 * SSD_GROUPS * SSD_STATE
ATTN_HEAD_DIM = 64
ATTN_Q_HEADS = D_MODEL // ATTN_HEAD_DIM
ATTN_KV_HEADS = ATTN_Q_HEADS // 4
ATTN_REP = ATTN_Q_HEADS // ATTN_KV_HEADS
D_ATTN = ATTN_Q_HEADS * ATTN_HEAD_DIM
D_KV = ATTN_KV_HEADS * ATTN_HEAD_DIM
WINDOW = 128
ROPE_THETA = 10000.0
N_BRANCH = 2
D_FF_2 = 4 * D_MODEL
D_IN_PROJ = D_INNER + CONV_DIM + SSD_HEADS + D_ATTN + 2 * D_KV + N_BRANCH * D_MODEL


def rms_norm_2(x, g):
    xf = x.astype(jnp.float32)
    xf = xf * lax.rsqrt(jnp.mean(xf * xf, axis=-1, keepdims=True) + EPS)
    return (xf * g.astype(jnp.float32)).astype(x.dtype)

def left_pad(t, pad):
    return jnp.pad(t, [(0, 0), (pad, 0)] + [(0, 0)] * (t.ndim - 2))

def segsum(a):
    t = a.shape[-1]
    cs = jnp.cumsum(a, axis=-1)
    diff = cs[..., :, None] - cs[..., None, :]
    mask = jnp.tril(jnp.ones((t, t), dtype=bool))
    return jnp.where(mask, diff, -jnp.inf)

def causal_depthwise_conv(u, w, bias):
    k, c = w.shape
    out = lax.conv_general_dilated(
        u, w[:, None, :].astype(u.dtype), window_strides=(1,), padding=[(k - 1, 0)],
        dimension_numbers=('NWC', 'WIO', 'NWC'), feature_group_count=c)
    return out + bias.astype(u.dtype)

def ssd_chunked(xs, dt, a_log, bm, cm):
    bsz, L, _, _ = xs.shape
    dtype = xs.dtype
    pad = (-L) % BLOCK
    xs, dt, bm, cm = left_pad(xs, pad), left_pad(dt, pad), left_pad(bm, pad), left_pad(cm, pad)
    nc = (L + pad) // BLOCK
    g, r, p, n = SSD_GROUPS, SSD_HEADS_PER_GROUP, SSD_HEAD_DIM, SSD_STATE
    a = -jnp.exp(a_log.astype(jnp.float32))
    adt = (dt.astype(jnp.float32) * a).reshape(bsz, nc, BLOCK, g, r)
    adt = jnp.transpose(adt, (0, 1, 3, 4, 2))
    a_cum = jnp.cumsum(adt, axis=-1)
    xdt = (xs * dt[..., None]).reshape(bsz, nc, BLOCK, g, r, p)
    bc = bm.reshape(bsz, nc, BLOCK, g, n)
    cc = cm.reshape(bsz, nc, BLOCK, g, n)
    lmat = jnp.exp(segsum(adt)).astype(dtype)
    cb = jnp.einsum('bclgn,bcsgn->bcgls', cc, bc)
    y_diag = jnp.einsum('bcgls,bcgrls,bcsgrp->bclgrp', cb, lmat, xdt)
    decay_states = jnp.exp(a_cum[..., -1:] - a_cum).astype(dtype)
    states = jnp.einsum('bclgn,bcgrl,bclgrp->bcgrpn', bc, decay_states, xdt)
    chunk_tot = jnp.pad(a_cum[..., -1], ((0, 0), (1, 0), (0, 0), (0, 0)))
    decay_chunk = jnp.exp(segsum(jnp.transpose(chunk_tot, (0, 2, 3, 1)))).astype(dtype)
    states = jnp.concatenate([jnp.zeros_like(states[:, :1]), states], axis=1)
    states = jnp.einsum('bgrzc,bcgrpn->bzgrpn', decay_chunk, states)[:, :-1]
    y_off = jnp.einsum('bclgn,bcgrpn,bcgrl->bclgrp', cc, states, jnp.exp(a_cum).astype(dtype))
    y = (y_diag + y_off).reshape(bsz, nc * BLOCK, SSD_HEADS, p)
    return y[:, pad:]

def ssd_mixer(z, xbc, dt_raw, conv_w, conv_b, dt_bias, a_log, d_skip, norm_g):
    bsz, L, _ = xbc.shape
    xbc = jax.nn.silu(causal_depthwise_conv(xbc, conv_w, conv_b))
    xs, bm, cm = jnp.split(xbc, [D_INNER, D_INNER + SSD_GROUPS * SSD_STATE], axis=-1)
    xs = xs.reshape(bsz, L, SSD_HEADS, SSD_HEAD_DIM)
    bm = bm.reshape(bsz, L, SSD_GROUPS, SSD_STATE)
    cm = cm.reshape(bsz, L, SSD_GROUPS, SSD_STATE)
    dt = jax.nn.softplus(dt_raw + dt_bias.astype(dt_raw.dtype))
    y = ssd_chunked(xs, dt, a_log, bm, cm) + xs * d_skip.astype(xs.dtype)[:, None]
    y = y.reshape(bsz, L, D_INNER) * jax.nn.silu(z)
    y = rms_norm_2(y.reshape(bsz, L, SSD_GROUPS, D_INNER // SSD_GROUPS),
                 norm_g.reshape(SSD_GROUPS, D_INNER // SSD_GROUPS))
    return y.reshape(bsz, L, D_INNER)

def rotary(t, pos):
    half = t.shape[-1] // 2
    inv_freq = ROPE_THETA ** (-jnp.arange(half, dtype=jnp.float32) / half)
    ang = pos.astype(jnp.float32)[:, None] * inv_freq[None, :]
    cos = jnp.cos(ang)[None, :, None, :].astype(t.dtype)
    sin = jnp.sin(ang)[None, :, None, :].astype(t.dtype)
    t1, t2 = t[..., :half], t[..., half:]
    return jnp.concatenate([t1 * cos - t2 * sin, t2 * cos + t1 * sin], axis=-1)

def sliding_window_attention(q, k, v, q_norm_g, k_norm_g, sinks):
    bsz, L = q.shape[:2]
    pos = jnp.arange(L)
    q = rotary(rms_norm_2(q, q_norm_g), pos)
    k = rotary(rms_norm_2(k, k_norm_g), pos)
    k_meta, v_meta = k[:, :N_META], v[:, :N_META]
    pad = (-L) % BLOCK
    nb = (L + pad) // BLOCK
    qb = left_pad(q, pad).reshape(bsz, nb, BLOCK, ATTN_KV_HEADS, ATTN_REP, ATTN_HEAD_DIM)
    kb = left_pad(k, pad).reshape(bsz, nb, BLOCK, ATTN_KV_HEADS, ATTN_HEAD_DIM)
    vb = left_pad(v, pad).reshape(bsz, nb, BLOCK, ATTN_KV_HEADS, ATTN_HEAD_DIM)

    def with_prev(t):
        prev = jnp.pad(t, [(0, 0), (1, 0)] + [(0, 0)] * (t.ndim - 2))[:, :-1]
        return jnp.concatenate([prev, t], axis=2)

    kb2, vb2 = with_prev(kb), with_prev(vb)
    blk_pos = (jnp.arange(nb * BLOCK) - pad).reshape(nb, BLOCK)
    k_pos = jnp.concatenate([blk_pos - BLOCK, blk_pos], axis=1)
    rel = blk_pos[:, :, None] - k_pos[:, None, :]
    band_mask = (rel >= 0) & (rel < WINDOW) & (k_pos[:, None, :] >= N_META)
    meta_mask = jnp.arange(N_META)[None, None, :] <= blk_pos[:, :, None]
    scale = ATTN_HEAD_DIM ** -0.5
    s_meta = jnp.einsum('bnqhrd,bmhd->bnhrqm', qb, k_meta).astype(jnp.float32) * scale
    s_band = jnp.einsum('bnqhrd,bnkhd->bnhrqk', qb, kb2).astype(jnp.float32) * scale
    s_meta = jnp.where(meta_mask[None, :, None, None], s_meta, -jnp.inf)
    s_band = jnp.where(band_mask[None, :, None, None], s_band, -jnp.inf)
    sink = jnp.broadcast_to(
        sinks.astype(jnp.float32).reshape(1, 1, ATTN_KV_HEADS, ATTN_REP, 1, 1),
        s_meta.shape[:-1] + (1,))
    probs = jax.nn.softmax(jnp.concatenate([s_meta, s_band, sink], axis=-1), axis=-1).astype(v.dtype)
    out = (jnp.einsum('bnhrqm,bmhd->bnqhrd', probs[..., :N_META], v_meta)
           + jnp.einsum('bnhrqk,bnkhd->bnqhrd', probs[..., N_META:N_META + 2 * BLOCK], vb2))
    return out.reshape(bsz, nb * BLOCK, D_ATTN)[:, pad:]

def second_inputs(seed: int = 0) -> dict:
    key = jax.random.key(seed)
    ks = jax.random.split(key, 20)
    f32 = jnp.float32

    def normal(k, shape, scale):
        return jax.random.normal(k, shape, f32) * scale

    dt0 = jnp.exp(jax.random.uniform(ks[7], (DEPTH, SSD_HEADS), f32, math.log(1e-3), math.log(1e-1)))
    return {
        'x': normal(ks[0], (BATCH, SEQ, D_MODEL), 1.0),
        'meta_tokens': normal(ks[1], (N_META, D_MODEL), 1.0),
        'norm1_g': 1.0 + normal(ks[2], (DEPTH, D_MODEL), 0.02),
        'w_in': normal(ks[3], (DEPTH, D_MODEL, D_IN_PROJ), D_MODEL ** -0.5),
        'b_gate': normal(ks[4], (DEPTH, N_BRANCH * D_MODEL), 0.01),
        'conv_w': normal(ks[5], (DEPTH, CONV_WIDTH, CONV_DIM), CONV_WIDTH ** -0.5),
        'conv_b': normal(ks[6], (DEPTH, CONV_DIM), 0.01),
        'dt_bias': dt0 + jnp.log(-jnp.expm1(-dt0)),
        'a_log': jnp.log(jax.random.uniform(ks[8], (DEPTH, SSD_HEADS), f32, 1.0, 16.0)),
        'd_skip': 1.0 + normal(ks[9], (DEPTH, SSD_HEADS), 0.02),
        'ssd_norm_g': 1.0 + normal(ks[10], (DEPTH, D_INNER), 0.02),
        'q_norm_g': 1.0 + normal(ks[11], (DEPTH, ATTN_HEAD_DIM), 0.02),
        'k_norm_g': 1.0 + normal(ks[12], (DEPTH, ATTN_HEAD_DIM), 0.02),
        'sinks': normal(ks[13], (DEPTH, ATTN_Q_HEADS), 1.0),
        'w_ssd_down': normal(ks[14], (DEPTH, D_INNER, D_MODEL), D_INNER ** -0.5),
        'w_attn_down': normal(ks[15], (DEPTH, D_ATTN, D_MODEL), D_ATTN ** -0.5),
        'w_o': normal(ks[16], (DEPTH, D_MODEL, D_MODEL), D_MODEL ** -0.5),
        'norm2_g': 1.0 + normal(ks[17], (DEPTH, D_MODEL), 0.02),
        'w_mlp_up': normal(ks[18], (DEPTH, D_MODEL, D_FF_2), D_MODEL ** -0.5),
        'w_mlp_down': normal(ks[19], (DEPTH, D_FF_2, D_MODEL), D_FF_2 ** -0.5),
    }

def second_block(x, meta_tokens, norm1_g, w_in, b_gate, conv_w, conv_b, dt_bias, a_log, d_skip,
              ssd_norm_g, q_norm_g, k_norm_g, sinks, w_ssd_down, w_attn_down, w_o, norm2_g,
              w_mlp_up, w_mlp_down):
    bsz = x.shape[0]
    meta = jnp.broadcast_to(meta_tokens[None].astype(x.dtype), (bsz, N_META, D_MODEL))
    h = jnp.concatenate([meta, x], axis=1)
    L = h.shape[1]
    split_at = [D_INNER, D_INNER + CONV_DIM, D_INNER + CONV_DIM + SSD_HEADS,
                D_INNER + CONV_DIM + SSD_HEADS + D_ATTN,
                D_INNER + CONV_DIM + SSD_HEADS + D_ATTN + D_KV,
                D_INNER + CONV_DIM + SSD_HEADS + D_ATTN + 2 * D_KV]
    for l in range(DEPTH):
        xn = rms_norm_2(h, norm1_g[l])
        proj = xn @ w_in[l]
        z, xbc, dt_raw, q, k, v, gate_logits = jnp.split(proj, split_at, axis=-1)
        y_ssd = ssd_mixer(z, xbc, dt_raw, conv_w[l], conv_b[l], dt_bias[l], a_log[l],
                          d_skip[l], ssd_norm_g[l])
        y_attn = sliding_window_attention(
            q.reshape(bsz, L, ATTN_Q_HEADS, ATTN_HEAD_DIM),
            k.reshape(bsz, L, ATTN_KV_HEADS, ATTN_HEAD_DIM),
            v.reshape(bsz, L, ATTN_KV_HEADS, ATTN_HEAD_DIM),
            q_norm_g[l], k_norm_g[l], sinks[l])
        gates = jax.nn.sigmoid(gate_logits + b_gate[l].astype(gate_logits.dtype))
        g_ssd, g_attn = jnp.split(gates, 2, axis=-1)
        merged = g_ssd * (y_ssd @ w_ssd_down[l]) + g_attn * (y_attn @ w_attn_down[l])
        h = h + merged @ w_o[l]
        hn = rms_norm_2(h, norm2_g[l])
        h = h + jnp.square(jax.nn.relu(hn @ w_mlp_up[l])) @ w_mlp_down[l]
    return h[:, N_META:]


def setup_inputs(seed=0):
    out = dict(first_inputs(seed))
    for name, value in second_inputs(seed + 1).items():
        if name != "x":
            out[name + "_2"] = value
    return out


def reference(
    x, mem, norm_mix, norm_xattn, norm_mem, norm_ffn, ev_w_in, ev_conv, ev_q_norm, ev_k_norm,
    ev_w_out, od_w_in, od_conv, od_a_log, od_dt_bias, od_o_norm, od_w_out, xa_w_q, xa_w_kv,
    xa_q_norm, xa_k_norm, xa_w_o, ff_w_gu, ff_w_down, moe_router, moe_w_gu, moe_w_down,
    meta_tokens_2, norm1_g_2, w_in_2, b_gate_2, conv_w_2, conv_b_2, dt_bias_2, a_log_2,
    d_skip_2, ssd_norm_g_2, q_norm_g_2, k_norm_g_2, sinks_2, w_ssd_down_2, w_attn_down_2, w_o_2,
    norm2_g_2, w_mlp_up_2, w_mlp_down_2,
):
    x = first_block(
        x, mem, norm_mix, norm_xattn, norm_mem, norm_ffn, ev_w_in, ev_conv, ev_q_norm,
        ev_k_norm, ev_w_out, od_w_in, od_conv, od_a_log, od_dt_bias, od_o_norm, od_w_out,
        xa_w_q, xa_w_kv, xa_q_norm, xa_k_norm, xa_w_o, ff_w_gu, ff_w_down, moe_router, moe_w_gu,
        moe_w_down,
    )
    return second_block(
        x, meta_tokens_2, norm1_g_2, w_in_2, b_gate_2, conv_w_2, conv_b_2, dt_bias_2, a_log_2,
        d_skip_2, ssd_norm_g_2, q_norm_g_2, k_norm_g_2, sinks_2, w_ssd_down_2, w_attn_down_2,
        w_o_2, norm2_g_2, w_mlp_up_2, w_mlp_down_2,
    )


_drawn_inputs = setup_inputs


def setup_inputs(seed=0):
    import zlib

    import numpy as np

    out = dict(_drawn_inputs(seed))
    spreads = {}
    factors = {'norm_xattn': 8.0,
     'ev_k_norm': 2.894,
     'xa_q_norm': 2.935,
     'norm1_g_2': 3.955,
     'b_gate_2': 8.0,
     'conv_b_2': 8.0,
     'd_skip_2': 64.0,
     'ssd_norm_g_2': 5.996,
     'q_norm_g_2': 8.0,
     'k_norm_g_2': 8.0,
     'sinks_2': 26.243,
     'norm2_g_2': 2.953}
    for name, (base, spread) in spreads.items():
        noise = np.random.default_rng([zlib.crc32(name.encode()), seed]).standard_normal(out[name].shape)
        drawn = base * np.exp(spread * noise) if base else spread * noise
        out[name] = jnp.asarray(drawn.astype(out[name].dtype))
    for name, factor in factors.items():
        out[name] = (out[name] * factor).astype(out[name].dtype)
    return out
```

```python
from contextlib import ExitStack

import numpy as np
import concourse.bass as bass
from concourse import mybir

F32 = mybir.dt.float32
U32 = mybir.dt.uint32
ALU = mybir.AluOpType
ACT = mybir.ActivationFunctionType
AX_X = mybir.AxisListType.X

P = 128
D = 1024
KD = D // P
SEQ = 256
EPS = 1e-6
NEG = -1e30

B_HEADS, B_DIM = 8, 64
C_HEADS, C_DIM, C_CONV = 8, 128, 4
X_HEADS = 4
A_CONV = 3
D_FF = 2816
N_EXPERTS = 8
D_FFE = D_FF // 2
DELTA_CHUNK = 128
DELTA_LEVELS = 7

N_META = 16
L2 = SEQ + N_META
CHUNKS2 = ((0, 16), (16, 128), (144, 128))
SSD_HEADS, SSD_GROUPS, SSD_R, SSD_P = 32, 8, 4, 64
ATTN_HEADS, KV_HEADS, ATTN_DIM = 16, 4, 64
WINDOW = 128
FF2 = 4 * D
CONV2 = 4
CONV_CHUNKS2 = 32

RING = 4
SLOT = 2048

STREAM = (
    [("xa_kv0", "wide", 2), ("xa_kv1", "wide", 2)]
    + [("ev_in", "wide", 12), ("ev_out", "wide", 4), ("xa_q0", "wide", 1), ("xa_o0", "flat", 4)]
    + [("ff_gu", "wide", 22), ("ff_down", "deep", 22)]
    + [("od_in", "wide", 16), ("od_out", "wide", 4), ("xa_q1", "wide", 1), ("xa_o1", "flat", 4)]
    + [("moe", "moe", 8)]
    + [
        (f"{n}{l}", kind, size)
        for l in range(2)
        for n, kind, size in (
            ("z", "wide", 8), ("xbc", "wide", 16), ("q", "wide", 4), ("kv", "wide", 2), ("gate", "wide", 8),
            ("ssd_down", "deep", 16), ("attn_down", "wide", 4), ("w_o", "wide", 4),
            ("up", "wide", 16), ("down", "deep", 32),
        )
    ]
)


class Segment:

    def __init__(self, name, iters, slots, units, unit0):
        self.name, self.iters, self.slots, self.units, self.unit0 = name, iters, slots, units, unit0
        self.last_unit = [0] * len(slots)
        for j, unit in enumerate(units):
            for chunk in unit:
                for s, *_ in chunk:
                    self.last_unit[s] = j + 1


def wide_unit(s):
    return [[(s, k, k * 256 + c * P, k, 0) for k in range(KD)] for c in range(2)]


def plan_stream():
    plan, order = {}, []
    for name, kind, size in STREAM:
        segs = []
        if kind == "wide":
            n = size // 4 if size >= 8 else 0
            if n:
                segs.append(Segment(name, n, [SLOT] * 4, [wide_unit(s) for s in range(4)], 0))
            if size - 4 * n:
                rest = size - 4 * n
                segs.append(Segment(name, 1, [SLOT] * rest, [wide_unit(s) for s in range(rest)], 4 * n))
        elif kind == "deep":
            parts = 1 if size <= 16 else 2
            kt = size // parts
            per = 4 // parts
            units = [[[(u * parts + k // kt, k % kt, (k % kt) * P, k, 0) for k in range(size)]] for u in range(per)]
            segs.append(Segment(name, 8 // per, [kt * P] * 4, units, 0))
        elif kind == "flat":
            units = [[[(0, k, k * D + (2 * u + c) * P, k, 0) for k in range(2)] for c in range(2)] for u in range(4)]
            segs.append(Segment(name, 1, [SLOT], units, 0))
        else:
            kt = D_FFE // P
            units = [wide_unit(s) for s in range(kt)]
            units += [[[(kt + c, k, k * P, k, 1) for k in range(kt)]] for c in range(8)]
            segs.append(Segment(name, N_EXPERTS, [SLOT] * kt + [kt * P] * 8, units, 0))
        plan[name] = segs
        order += segs
    position, units_before, slots_before = 0, 0, 0
    fills = [0] * RING
    occupant = [0] * RING
    for seg in order:
        looped = seg.iters > 1
        if looped:
            position = -(-position // RING) * RING
        seg.unit_base, seg.slot_base = units_before, slots_before
        n, nu = len(seg.slots), len(seg.units)
        seg.ring = [(position + j) % RING for j in range(n)]
        per = [seg.ring.count(s) for s in range(RING)]
        seen = list(fills)
        seg.full0, seg.full_step, seg.free0 = [], [], []
        for j, s in enumerate(seg.ring):
            seen[s] += 1
            seg.full0.append(16 * seen[s])
            seg.full_step.append(16 * per[s])
            before = [i for i in range(j) if seg.ring[i] == s]
            if before:
                seg.free0.append(units_before + seg.last_unit[before[-1]])
            elif looped:
                again = [i for i in range(n) if seg.ring[i] == s][-1]
                seg.free0.append(max(units_before + seg.last_unit[again] - nu, occupant[s]))
            else:
                seg.free0.append(occupant[s])
        for s in range(RING):
            used = [j for j in range(n) if seg.ring[j] == s]
            if used:
                fills[s] += seg.iters * per[s]
                occupant[s] = units_before + (seg.iters - 1) * nu + seg.last_unit[used[-1]]
        position = -(-(position + n) // RING) * RING if looped else position + n
        units_before += seg.iters * nu
        slots_before += seg.iters * n
    return plan, order, slots_before


PARAMS = [
    ("norm_mix", 2 * KD), ("norm_xattn", 2 * KD), ("norm_mem", 2 * KD), ("norm_ffn", 2 * KD),
    ("ev_conv", A_CONV * 4), ("ev_q_norm", 1), ("ev_k_norm", 1),
    ("od_conv", C_CONV * 24), ("od_o_norm", 1), ("od_a_log", 1), ("od_dt_bias", 1),
    ("xa_q_norm", 2), ("xa_k_norm", 2),
    ("od_small", KD * 16), ("router", KD * 8),
    ("norm1", 2 * KD), ("norm2", 2 * KD), ("conv_w", 2 * CONV2 * 32), ("conv_b", 2 * 32), ("b_gate", 2 * 16),
    ("d_skip", 2 * 16), ("ssd_norm", 2 * 16), ("q_norm", 2), ("k_norm", 2), ("dt_bias", 2), ("a_log", 2),
    ("w_dt", 2 * KD * 32), ("sinks", 2 * 16),
]
CONSTS = [
    ("ident", P), ("ones", P), ("pair_ones", P), ("swap", P), ("dilated", 2 * SEQ), ("zero_mask", 2 * SEQ),
    ("window", 3 * L2), ("cos", L2), ("sin", L2), ("levels", DELTA_LEVELS * P), ("below", P), ("iota", 8),
]


def offsets(spec):
    at, out = 0, {}
    for name, n in spec:
        out[name] = (at, n)
        at += n
    return out, at


class Counted:

    def __init__(self, sem):
        self.sem, self.base = sem, 0

    def at(self, n):
        return self.base + n

    def close(self, n):
        self.base += n


class Steps:

    def __init__(self, sem):
        self.sem, self.count = sem, 0

    def link(self, eng, ins):
        self.count += 1
        ins.then_inc(self.sem, 1)
        eng.wait_ge(self.sem, self.count)


class Program:
    def __init__(self, nc, ctx, block, upto):
        self.nc, self.ctx, self.block, self.upto = nc, ctx, block, upto
        self.counts = {}
        self.plan, self.order, self.n_slots = plan_stream()
        self.stage_done = self.sem("stage_done")
        self.stages = 0
        self.unit_done = self.sem("unit_done")
        self.unit_free = self.sem("unit_free")
        self.full = [self.sem(f"slot_full{s}") for s in range(RING)]
        self.loaded = self.sem("inputs_loaded")
        self.stored = self.sem("output_stored")
        self.act_steps = Steps(self.sem("act_step"))
        self.dve_steps = Steps(self.sem("dve_step"))
        sb = lambda name, shape, dt=F32: ctx.enter_context(nc.sbuf_tensor(name, shape, dt))
        self.ring = sb("ring", [P, RING, SLOT])
        self.par_at, n_par = offsets(PARAMS)
        self.con_at, n_con = offsets(CONSTS)
        self.params = sb("params", [P, n_par])
        self.consts = sb("consts", [P, n_con])
        self.h = sb("h", [P, KD, L2])
        self.u = sb("u", [P, KD, L2])
        self.work = sb("work", [P, KD * L2])
        self.rstd = sb("rstd", [P, L2])
        self.arena_cols = 29000
        self.arena = sb("arena", [P, self.arena_cols])
        self.indices = sb("indices", [P, 2, 8], U32)
        self.ps = ctx.enter_context(nc.psum_tensor("ps", [P, 8, 512], F32))

    def sem(self, name):
        return self.ctx.enter_context(self.nc.semaphore(name))

    def counted(self, name):
        if name not in self.counts:
            self.counts[name] = Counted(self.sem(name))
        return self.counts[name]

    def par(self, name, first=0, n=1):
        at = self.par_at[name][0] + first
        return self.params[:, at:at + n]

    def par_dyn(self, name, first):
        return self.params[:, bass.ds(self.par_at[name][0] + first, 1)]

    def con(self, name, first=0, n=None, rows=P):
        at, size = self.con_at[name]
        return self.consts[0:rows, at + first:at + first + (size if n is None else n)]

    def area(self, at, *dims):
        n = int(np.prod(dims))
        assert at + n <= self.arena_cols, (at, n)
        v = self.arena[:, at:at + n]
        if len(dims) == 2:
            v = v.rearrange("p (a b) -> p a b", b=dims[1])
        elif len(dims) == 3:
            v = v.rearrange("p (a b c) -> p a b c", b=dims[1], c=dims[2])
        return v, at + n

    def stage_end(self):
        self.stages += 1
        goal = 3 * self.stages
        for start in (self.block.tensor, self.block.scalar, self.block.vector):
            @start
            def _(eng):
                eng.drain().then_inc(self.stage_done, 1)
                eng.wait_ge(self.stage_done, goal)


def repeat(eng, n, body):
    if n == 1:
        body(0)
    else:
        with eng.Fori(0, n) as i:
            body(i)


def at_dyn(view, first, n, size=None):
    return view[:, first:first + n] if isinstance(first, int) else view[:, bass.ds(first, n)]


def is_register(i):
    return not isinstance(i, int)


def gemm(p, name, xs, T, act_unit=None, dve_unit=None, signals=()):
    for seg in p.plan[name]:
        nu = len(seg.units)

        @p.block.tensor
        def _(pe):
            def body(i):
                seen = set()
                for j, unit in enumerate(seg.units):
                    for s in sorted({c[0] for chunk in unit for c in chunk} - seen):
                        seen.add(s)
                        pe.wait_ge(p.full[seg.ring[s]], i * seg.full_step[s] + seg.full0[s])
                    number = seg.unit_base + j + 1
                    if number > 2 or is_register(i):
                        pe.wait_ge(p.unit_free, i * nu + (number - 2))
                    for c, chunk in enumerate(unit):
                        for n, (s, k, col, xk, which) in enumerate(chunk):
                            mm = pe.matmul(p.ps[:, 2 * (j % 2) + c, 0:T], p.ring[:, seg.ring[s], col:col + P],
                                           xs[which][:, xk, 0:T], start=(n == 0), stop=(n == len(chunk) - 1))
                    mm.then_inc(p.unit_done, 1)
            repeat(pe, seg.iters, body)

        for unit_fn, start in ((act_unit, p.block.scalar), (dve_unit, p.block.vector)):
            if unit_fn is None:
                continue

            @start
            def _(eng):
                def body(i):
                    for j, unit in enumerate(seg.units):
                        eng.wait_ge(p.unit_done, i * nu + (seg.unit_base + j + 1))
                        unit_fn(eng, i * nu + (seg.unit0 + j), j, p.ps[:, 2 * (j % 2):2 * (j % 2) + len(unit), 0:T])
                repeat(eng, seg.iters, body)
    for name, n in signals:
        p.counted(name).close(n)


def take_copy(p, dst, T, per=2, func=ACT.Copy):
    def unit(act, u, j, bank):
        act.activation(at_dyn(dst, per * u, per)[:, :, 0:T], bank, func).then_inc(p.unit_free, 1)
    return unit


def take_add(p, dst, T, per):
    def unit(dve, u, j, bank):
        out = at_dyn(dst, per * u, per)[:, :, 0:T]
        dve.tensor_tensor(out, bank, out, ALU.add).then_inc(p.unit_free, 1)
    return unit


def norm(p, src, dst, gain, gain0, T, chunks=KD):
    sq = p.work[:, 0:chunks * T].rearrange("p (k t) -> p k t", t=T)
    half = chunks // 2
    squares, sums, means, roots = (p.counted(n) for n in ("squares_ready", "sums_ready", "means_ready", "roots_ready"))

    @p.block.scalar
    def _(act):
        act.activation(sq[:, 0:half], src[:, 0:half, 0:T], ACT.Square).then_inc(squares.sem, 1)
        act.wait_ge(means.sem, means.at(1))
        act.activation(p.rstd[:, 0:T], p.rstd[:, 0:T], ACT.Sqrt).then_inc(roots.sem, 1)

    @p.block.tensor
    def _(pe):
        pe.wait_ge(squares.sem, squares.at(2))
        for k in range(chunks):
            mm = pe.matmul(p.ps[:, 7, 0:T], p.con("ones"), sq[:, k], start=(k == 0), stop=(k == chunks - 1))
        mm.then_inc(sums.sem, 1)

    @p.block.vector
    def _(dve):
        dve.tensor_tensor(sq[:, half:], src[:, half:chunks, 0:T], src[:, half:chunks, 0:T], ALU.mult).then_inc(squares.sem, 1)
        dve.wait_ge(sums.sem, sums.at(1))
        dve.tensor_scalar(p.rstd[:, 0:T], p.ps[:, 7, 0:T], 1.0 / (chunks * P), EPS, ALU.mult, ALU.add).then_inc(means.sem, 1)
        dve.wait_ge(roots.sem, roots.at(1))
        p.dve_steps.link(dve, dve.reciprocal(p.rstd[:, 0:T], p.rstd[:, 0:T]))
        for k in range(chunks):
            dve.scalar_tensor_tensor(dst[:, k, 0:T], src[:, k, 0:T], p.par(gain, gain0 + k), p.rstd[:, 0:T], ALU.mult, ALU.mult)

    for s, n in ((squares, 2), (sums, 1), (means, 1), (roots, 1)):
        s.close(n)
    p.stage_end()


def head_norm(p, x, n, T, ones, scale, eps, gain=None, factor=1.0, group=1, extra=None):
    sq = p.work[:, 0:n * T].rearrange("p (k t) -> p k t", t=T)
    squares, sums, means, roots = (p.counted(s) for s in ("squares_ready", "sums_ready", "means_ready", "roots_ready"))
    ng = n // group
    assert ng <= 8

    @p.block.scalar
    def _(act):
        act.activation(sq, x, ACT.Square).then_inc(squares.sem, 1)
        act.wait_ge(means.sem, means.at(1))
        act.activation(sq[:, 0:ng], sq[:, 0:ng], ACT.Sqrt).then_inc(roots.sem, 1)

    @p.block.tensor
    def _(pe):
        pe.wait_ge(squares.sem, squares.at(1))
        for g in range(ng):
            for k in range(group):
                mm = pe.matmul(p.ps[:, g, 0:T], p.con(ones), sq[:, g * group + k], start=(k == 0), stop=(k == group - 1))
        mm.then_inc(sums.sem, 1)

    @p.block.vector
    def _(dve):
        dve.wait_ge(sums.sem, sums.at(1))
        dve.tensor_scalar(sq[:, 0:ng], p.ps[:, 0:ng, 0:T], scale, eps, ALU.mult, ALU.add).then_inc(means.sem, 1)
        dve.wait_ge(roots.sem, roots.at(1))
        p.dve_steps.link(dve, dve.reciprocal(sq[:, 0:ng], sq[:, 0:ng]))
        if group == 1:
            dve.scalar_tensor_tensor(x, x, factor if gain is None else gain[0], sq, ALU.mult, ALU.mult)
        else:
            for c in range(n):
                dve.scalar_tensor_tensor(x[:, c], x[:, c], gain[c], sq[:, c // group], ALU.mult, ALU.mult)

    for s in (squares, sums, means, roots):
        s.close(1)
    p.stage_end()


def to_tokens(p, src, n_chunks, tiles, dst, T):
    groups = [(i, o, n, c, min(4, n_chunks - c)) for i, (o, n) in enumerate(tiles) for c in range(0, n_chunks, 4)]
    turned, moved = p.counted("turned"), p.counted("moved")

    @p.block.tensor
    def _(pe):
        for g, (i, o, n, c0, m) in enumerate(groups):
            if g >= 4:
                pe.wait_ge(moved.sem, moved.at(g - 3))
            for c in range(m):
                mm = pe.transpose(p.ps[0:n, 4 + g % 4, c * P:(c + 1) * P], src[:, c0 + c, o:o + n], p.con("ident"))
            mm.then_inc(turned.sem, 1)

    @p.block.scalar
    def _(act):
        for g, (i, o, n, c0, m) in enumerate(groups):
            act.wait_ge(turned.sem, turned.at(g + 1))
            act.activation(dst[0:n, i, c0 * P:(c0 + m) * P], p.ps[0:n, 4 + g % 4, 0:m * P], ACT.Copy).then_inc(moved.sem, 1)

    turned.close(len(groups))
    moved.close(len(groups))
    p.stage_end()


def from_tokens(p, src, dst, tiles):
    groups = [(i, o, n, c) for i, (o, n) in enumerate(tiles) for c in (0, 4)]
    turned, moved = p.counted("turned"), p.counted("moved")

    @p.block.tensor
    def _(pe):
        pe.wait_ge(p.loaded, p.n_loads)
        for g, (i, o, n, c0) in enumerate(groups):
            if g >= 4:
                pe.wait_ge(moved.sem, moved.at(g - 3))
            for c in range(4):
                mm = pe.transpose(p.ps[:, 4 + g % 4, c * P:c * P + n], src[0:n, i, (c0 + c) * P:(c0 + c + 1) * P],
                                  p.con("ident", n=n, rows=n))
            mm.then_inc(turned.sem, 1)

    @p.block.scalar
    def _(act):
        for g, (i, o, n, c0) in enumerate(groups):
            act.wait_ge(turned.sem, turned.at(g + 1))
            bank = p.ps[:, 4 + g % 4, :].rearrange("p (c t) -> p c t", t=P)
            act.activation(dst[:, c0:c0 + 4, o:o + n], bank[:, :, 0:n], ACT.Copy).then_inc(moved.sem, 1)

    turned.close(len(groups))
    moved.close(len(groups))
    p.stage_end()


def attention(p, items, scale, at):
    masked, at = p.area(at, 3, L2)
    probs, at = p.area(at, 3, L2)
    turned_p, at = p.area(at, 2, 3, P)
    small, at = p.area(at, 3, 8)
    names = ("scores_ready", "masked_ready", "exp_ready", "probs_ready", "probs_turned", "turned_ready", "heads_ready", "heads_moved")
    scores, mask_ok, exp_ok, prob_ok, turn_ok, tcopy_ok, head_ok, moved = (p.counted(n) for n in names)
    N = len(items)

    @p.block.tensor
    def _(pe):
        def do_scores(i):
            t = items[i]
            if i >= 2:
                pe.wait_ge(mask_ok.sem, mask_ok.at(i - 1))
            pe.matmul(p.ps[0:t["nq"], i % 2, 0:t["nk"]], t["q"], t["k"], start=True, stop=True).then_inc(scores.sem, 1)

        def do_turn(i):
            t = items[i]
            pe.wait_ge(prob_ok.sem, prob_ok.at(i + 1))
            if i >= 2:
                pe.wait_ge(tcopy_ok.sem, tcopy_ok.at(i - 1))
            for n, (o, rows) in enumerate(t["tiles"]):
                mm = pe.transpose(p.ps[0:rows, 2 + i % 2, n * P:n * P + t["nq"]], probs[0:t["nq"], i % 3, o:o + rows],
                                  p.con("ident", n=t["nq"], rows=t["nq"]))
            mm.then_inc(turn_ok.sem, 1)

        def do_heads(i):
            t = items[i]
            pe.wait_ge(tcopy_ok.sem, tcopy_ok.at(i + 1))
            if i >= 2:
                pe.wait_ge(moved.sem, moved.at(i - 1))
            for n, (o, rows) in enumerate(t["tiles"]):
                mm = pe.matmul(p.ps[t["part"]:t["part"] + 64, 4 + i % 2, 0:t["nq"]], t["v"][n], turned_p[0:rows, i % 2, n, 0:t["nq"]],
                               start=(n == 0), stop=(n == len(t["tiles"]) - 1))
            mm.then_inc(head_ok.sem, 1)

        for i in range(N + 2):
            if i < N:
                do_scores(i)
            if 1 <= i <= N:
                do_turn(i - 1)
            if i >= 2:
                do_heads(i - 2)

    @p.block.vector
    def _(dve):
        def do_mask(i):
            t = items[i]
            nq, nk = t["nq"], t["nk"]
            dve.wait_ge(scores.sem, scores.at(i + 1))
            if i >= 3:
                dve.wait_ge(exp_ok.sem, exp_ok.at(i - 2))
            m, sm = masked[0:nq, i % 3, 0:nk], small[0:nq, i % 3]
            p.dve_steps.link(dve, dve.scalar_tensor_tensor(m, p.ps[0:nq, i % 2, 0:nk], scale, t["mask"], ALU.mult, ALU.add))
            p.dve_steps.link(dve, dve.tensor_reduce(sm[:, 0:1], m, AX_X, ALU.max))
            other = t["sink"] if t["sink"] is not None else sm[:, 0:1]
            dve.tensor_scalar(sm[:, 1:2], sm[:, 0:1], other, -1.0, ALU.max, ALU.mult).then_inc(mask_ok.sem, 1)

        def do_divide(i):
            t = items[i]
            nq, nk = t["nq"], t["nk"]
            sm = small[0:nq, i % 3]
            dve.wait_ge(exp_ok.sem, exp_ok.at(i + 1))
            if t["sink"] is not None:
                p.dve_steps.link(dve, dve.tensor_tensor(sm[:, 2:3], sm[:, 2:3], sm[:, 3:4], ALU.add))
            p.dve_steps.link(dve, dve.reciprocal(sm[:, 4:5], sm[:, 2:3]))
            dve.tensor_scalar(probs[0:nq, i % 3, 0:nk], probs[0:nq, i % 3, 0:nk], sm[:, 4:5], None, ALU.mult).then_inc(prob_ok.sem, 1)

        for i in range(N + 1):
            if i < N:
                do_mask(i)
            if i >= 1:
                do_divide(i - 1)

    @p.block.scalar
    def _(act):
        def do_exp(i):
            t = items[i]
            nq, nk = t["nq"], t["nk"]
            sm = small[0:nq, i % 3]
            act.wait_ge(mask_ok.sem, mask_ok.at(i + 1))
            if i >= 3:
                act.wait_ge(turn_ok.sem, turn_ok.at(i - 2))
            if t["sink"] is not None:
                p.act_steps.link(act, act.activation(sm[:, 3:4], t["sink"], ACT.Exp, bias=sm[:, 1:2]))
            act.activation(probs[0:nq, i % 3, 0:nk], masked[0:nq, i % 3, 0:nk], ACT.Exp, bias=sm[:, 1:2],
                           accum_out=sm[:, 2:3]).then_inc(exp_ok.sem, 1)

        def do_copy(i):
            t = items[i]
            act.wait_ge(turn_ok.sem, turn_ok.at(i + 1))
            if i >= 2:
                act.wait_ge(head_ok.sem, head_ok.at(i - 1))
            bank = p.ps[:, 2 + i % 2, 0:3 * P].rearrange("p (n t) -> p n t", t=P)
            runs, n = [], 0
            while n < len(t["tiles"]):
                m = n + 1
                while m < len(t["tiles"]) and t["tiles"][m][1] == t["tiles"][n][1]:
                    m += 1
                runs.append((n, m, t["tiles"][n][1]))
                n = m
            for r, (n, m, rows) in enumerate(runs):
                ins = act.activation(turned_p[0:rows, i % 2, n:m, 0:t["nq"]], bank[0:rows, n:m, 0:t["nq"]], ACT.Copy)
                if r == len(runs) - 1:
                    ins.then_inc(tcopy_ok.sem, 1)

        def do_out(i):
            t = items[i]
            act.wait_ge(head_ok.sem, head_ok.at(i + 1))
            act.activation(t["out"], p.ps[t["part"]:t["part"] + 64, 4 + i % 2, 0:t["nq"]], ACT.Copy).then_inc(moved.sem, 1)

        for i in range(N + 2):
            if i < N:
                do_exp(i)
            if 1 <= i <= N:
                do_copy(i - 1)
            if i >= 2:
                do_out(i - 2)

    for s in (scores, mask_ok, exp_ok, prob_ok, turn_ok, tcopy_ok, head_ok, moved):
        s.close(N)
    p.stage_end()


TILES1 = ((0, 128), (128, 128))


def heads_256(q, k, v_tok, heads, mask, out, out0):
    items = []
    for h in range(heads):
        lo = 64 * (h % 2)
        for qt in range(2):
            items.append(dict(
                nq=P, nk=SEQ, tiles=TILES1, part=lo, sink=None, mask=mask[:, qt * SEQ:(qt + 1) * SEQ],
                q=q[lo:lo + 64, h // 2, qt * P:(qt + 1) * P], k=k[lo:lo + 64, h // 2, 0:SEQ],
                v=[v_tok[:, n, 64 * h:64 * h + 64] for n in range(2)],
                out=out[lo:lo + 64, out0 + h // 2, qt * P:(qt + 1) * P]))
    return items


def layer_even(p):
    T = SEQ
    proj, at = p.area(p.a0, 24, T)
    padded, at = p.area(at, 4, T + A_CONV - 1)
    cat, at = p.area(at, 8, T)
    v_tok, at = p.area(at, 2, 512)
    norm(p, p.h, p.u, "norm_mix", 0, T)
    gemm(p, "ev_in", [p.u], T, act_unit=take_copy(p, proj, T))
    p.stage_end()
    gb, gc, xc, q, k, v = (proj[:, 4 * i:4 * i + 4] for i in range(6))

    @p.block.vector
    def _(dve):
        dve.memset(padded[:, :, 0:A_CONV - 1], 0.0)
        p.dve_steps.link(dve, dve.tensor_tensor(padded[:, :, A_CONV - 1:], gc, xc, ALU.mult))
        for c in range(4):
            w = lambda j: p.par("ev_conv", j * 4 + c)
            p.dve_steps.link(dve, dve.tensor_scalar(cat[:, c], padded[:, c, 0:T], w(0), None, ALU.mult))
            for j in range(1, A_CONV):
                p.dve_steps.link(dve, dve.scalar_tensor_tensor(cat[:, c], padded[:, c, j:j + T], w(j), cat[:, c], ALU.mult, ALU.add))
        dve.tensor_tensor(cat[:, 0:4], cat[:, 0:4], gb, ALU.mult)

    head_norm(p, q, 4, T, "pair_ones", 1.0 / B_DIM, EPS, [p.par("ev_q_norm")])
    head_norm(p, k, 4, T, "pair_ones", 1.0 / B_DIM, EPS, [p.par("ev_k_norm")])
    to_tokens(p, v, 4, TILES1, v_tok, T)
    attention(p, heads_256(q, k, v_tok, B_HEADS, p.con("dilated"), cat, 4), B_DIM ** -0.5, at)
    gemm(p, "ev_out", [cat], T, dve_unit=take_add(p, p.h, T, 2))
    p.stage_end()


def memory_heads(p, layer):
    T = SEQ
    mem_n, _ = p.area(p.a0, KD, T)
    kv, at = p.area(p.a0 + KD * T, 4, T)
    norm(p, p.mem, mem_n, "norm_mem", KD * layer, T)
    gemm(p, f"xa_kv{layer}", [mem_n], T, act_unit=take_copy(p, kv, T))
    p.stage_end()
    k = p.mem_k[:, 2 * layer:2 * layer + 2]

    @p.block.scalar
    def _(act):
        p.act_steps.link(act, act.activation(k, kv[:, 0:2], ACT.Copy))

    head_norm(p, k, 2, T, "pair_ones", 1.0 / 64, EPS, [p.par("xa_k_norm", layer)])
    to_tokens(p, kv[:, 2:4], 2, TILES1, p.mem_v[:, 2 * layer:2 * layer + 2], T)


def cross_attention(p, layer):
    T = SEQ
    q, at = p.area(p.a0, 2, T)
    o, at = p.area(at, 2, T)
    norm(p, p.h, p.u, "norm_xattn", KD * layer, T)
    gemm(p, f"xa_q{layer}", [p.u], T, act_unit=take_copy(p, q, T))
    p.stage_end()
    head_norm(p, q, 2, T, "pair_ones", 1.0 / 64, EPS, [p.par("xa_q_norm", layer)])
    items = heads_256(q, p.mem_k[:, 2 * layer:2 * layer + 2], p.mem_v[:, 2 * layer:2 * layer + 2], X_HEADS,
                      p.con("zero_mask"), o, 0)
    attention(p, items, 64 ** -0.5, at)
    gemm(p, f"xa_o{layer}", [o], T, dve_unit=take_add(p, p.h, T, 2))
    p.stage_end()


def dense_ffn(p):
    T = SEQ
    hidden, at = p.area(p.a0, D_FF // P, T)
    silu, at = p.area(at, 2, T)
    gated = p.counted("gate_ready")
    norm(p, p.h, p.u, "norm_ffn", 0, T)

    def act_unit(act, u, j, bank):
        act.activation(silu[:, j % 2], bank[:, 0], ACT.Silu).then_inc(gated.sem, 1)

    def dve_unit(dve, u, j, bank):
        dve.wait_ge(gated.sem, u + gated.at(1))
        dve.tensor_tensor(at_dyn(hidden, u, 1)[:, 0], silu[:, j % 2], bank[:, 1], ALU.mult).then_inc(p.unit_free, 1)

    gemm(p, "ff_gu", [p.u], T, act_unit, dve_unit, [("gate_ready", D_FF // P)])
    p.stage_end()
    gemm(p, "ff_down", [hidden], T, dve_unit=take_add(p, p.h, T, 1))
    p.stage_end()


def conv_silu(p, name, dst, T, weights, w0, n_chunks, bias, b0, units, at):
    padded, at = p.area(at, 4, T + 3)
    acc, at = p.area(at, 4, T)
    step = p.counted("conv_step")
    unit_base = p.plan[name][0].unit_base

    @p.block.vector
    def _(dve):
        p.dve_steps.link(dve, dve.memset(padded[:, :, 0:3], 0.0))

    def act_unit(act, u, j, bank):
        b = 2 * (j % 2)
        act.activation(padded[:, b:b + 2, 3:3 + T], bank, ACT.Copy).then_inc(p.unit_free, 1)
        act.wait_ge(step.sem, 8 * u + step.at(8))
        act.activation(at_dyn(dst, 2 * u, 2)[:, :, 0:T], acc[:, b:b + 2], ACT.Silu)

    def dve_unit(dve, u, j, bank):
        b = 2 * (j % 2)
        dve.wait_ge(p.unit_free, u + (unit_base + 1))
        for t in range(4):
            for c in range(2):
                if t:
                    dve.wait_ge(step.sem, 8 * u + step.at(2 * t + c - 1))
                w = p.par_dyn(weights, 2 * u + (w0 + t * n_chunks + c))
                if t == 0 and bias is not None:
                    ins = dve.tensor_scalar(acc[:, b + c], padded[:, b + c, 0:T], w, p.par_dyn(bias, 2 * u + (b0 + c)), ALU.mult, ALU.add)
                elif t == 0:
                    ins = dve.tensor_scalar(acc[:, b + c], padded[:, b + c, 0:T], w, None, ALU.mult)
                else:
                    ins = dve.scalar_tensor_tensor(acc[:, b + c], padded[:, b + c, t:t + T], w, acc[:, b + c], ALU.mult, ALU.add)
                ins.then_inc(step.sem, 1)

    return act_unit, dve_unit, [("conv_step", 8 * units)]


def layer_odd(p):
    T, H = SEQ, C_HEADS
    qkv, at = p.area(p.a0, 24, T)
    gate, at = p.area(at, 8, T)
    top = at
    norm(p, p.h, p.u, "norm_mix", KD, T)
    rows, at = p.area(at, 8, T)
    top = at
    small_ok = p.counted("small_ready")
    beta, gcum, *t = (rows[0:H, i] for i in range(7))
    na = rows[0:H, 7, 0:1]

    @p.block.tensor
    def _(pe):
        for s in range(2):
            for k in range(KD):
                mm = pe.matmul(p.ps[0:H, 6 + s, 0:T], p.par("od_small", 16 * k + 8 * s, 8), p.u[:, k, 0:T], start=(k == 0), stop=(k == KD - 1))
        mm.then_inc(small_ok.sem, 1)

    softplus_rows(p, p.ps[0:H, 7, 0:T], p.par("od_dt_bias")[0:H], p.par("od_a_log")[0:H], t, na,
                  also=(beta, p.ps[0:H, 6, 0:T]))

    @p.block.vector
    def _(dve):
        p.dve_steps.link(dve, dve.tensor_scalar(t[0], t[1], na, -1.0, ALU.mult, ALU.mult))
        for c in range(2):
            s = slice(c * DELTA_CHUNK, (c + 1) * DELTA_CHUNK)
            dve.tensor_tensor_scan(gcum[:, s], t[0][:, s], t[0][:, s], 0.0, ALU.add, ALU.bypass)

    p.stage_end()
    a, d, sig = conv_silu(p, "od_in", qkv, T, "od_conv", 0, 24, None, 0, 12, top)
    segs = p.plan["od_in"]
    split = split_segment(segs[0], 3)
    p.plan["od_qkv"], p.plan["od_gate"] = [split[0]], [split[1]]
    gemm(p, "od_qkv", [p.u], T, a, d, sig)
    p.stage_end()
    gemm(p, "od_gate", [p.u], T, act_unit=take_copy(p, gate, T, func=ACT.Silu))
    p.stage_end()
    q, k, v = qkv[:, 0:8], qkv[:, 8:16], qkv[:, 16:24]
    head_norm(p, q, 8, T, "ones", 1.0, EPS, factor=C_DIM ** -0.5)
    head_norm(p, k, 8, T, "ones", 1.0, EPS)
    out, at = p.area(top, 8, T)
    cols, at = p.area(at, 2, 5, H)
    keep = at
    for c in range(2):
        delta_chunk(p, c, q, k, v, beta, gcum, out, cols[:, c], p.u, keep)
    head_norm(p, out, 8, T, "ones", 1.0 / C_DIM, EPS, [p.par("od_o_norm")])

    @p.block.vector
    def _(dve):
        dve.tensor_tensor(out, out, gate, ALU.mult)

    p.stage_end()
    gemm(p, "od_out", [out], T, dve_unit=take_add(p, p.h, T, 2))
    p.stage_end()


def split_segment(seg, n):
    a = Segment(seg.name, n, seg.slots, seg.units, seg.unit0)
    b = Segment(seg.name, seg.iters - n, seg.slots, seg.units, 0)
    nu = len(seg.units)
    for s, done in ((a, 0), (b, n)):
        s.ring, s.full_step = seg.ring, seg.full_step
        s.full0 = [f + done * st for f, st in zip(seg.full0, seg.full_step)]
        s.unit_base = seg.unit_base + done * nu
    return a, b


def softplus_rows(p, bank, bias, a_log, t, na, also=None):
    ready, args, tables = p.counted("small_ready"), p.counted("softplus_arg_ready"), p.counted("softplus_table_ready")

    @p.block.vector
    def _(dve):
        link = p.dve_steps.link
        dve.wait_ge(ready.sem, ready.at(1))
        link(dve, dve.tensor_scalar(t[0], bank, bias, None, ALU.add))
        link(dve, dve.tensor_scalar(t[1], t[0], -1.0, None, ALU.mult))
        dve.tensor_tensor(t[1], t[0], t[1], ALU.min).then_inc(args.sem, 1)
        dve.wait_ge(tables.sem, tables.at(1))
        dve.tensor_scalar(t[2], t[1], 1.0, None, ALU.add).then_inc(args.sem, 1)
        dve.wait_ge(tables.sem, tables.at(2))
        link(dve, dve.scalar_tensor_tensor(t[4], t[2], -1.0, t[1], ALU.add, ALU.subtract))
        link(dve, dve.reciprocal(t[2], t[2]))
        link(dve, dve.tensor_tensor(t[4], t[4], t[2], ALU.mult))
        link(dve, dve.tensor_tensor(t[3], t[3], t[4], ALU.subtract))
        link(dve, dve.scalar_tensor_tensor(t[1], t[0], 0.0, t[3], ALU.max, ALU.add))

    @p.block.scalar
    def _(act):
        act.wait_ge(ready.sem, ready.at(1))
        if also is not None:
            act.activation(also[0], also[1], ACT.Sigmoid)
        act.activation(na, a_log, ACT.Exp)
        act.wait_ge(args.sem, args.at(1))
        act.activation(t[1], t[1], ACT.Exp).then_inc(tables.sem, 1)
        act.wait_ge(args.sem, args.at(2))
        act.activation(t[3], t[2], ACT.Ln).then_inc(tables.sem, 1)

    ready.close(1)
    args.close(2)
    tables.close(2)


def delta_chunk(p, c, q, k, v, beta, gcum, out, cols, state, at):
    H, n = C_HEADS, DELTA_CHUNK
    tok = slice(c * n, (c + 1) * n)
    big = lambda a: p.area(a, H, n)
    R, at = big(at)
    DT, at = big(at)
    X, at = big(at)
    Tm, at = big(at)
    Um, at = big(at)
    NT, at = big(at)
    CT, at = big(at)
    S = state[:, :, 0:C_DIM]
    banks = lambda b, m=2: p.ps[:, b:b + m, :].rearrange("p b (h t) -> p (b h) t", t=n)
    pe_ok, act_ok, dve_ok = p.counted("products_ready"), p.counted("scalar_ready"), p.counted("vector_ready")
    beta_t, gc_t, eg, edec, bg = (cols[:, i] for i in range(5))
    qT, kT, vT = q[:, :, tok], k[:, :, tok], v[:, :, tok]
    b3 = lambda x: x[:, :, None].to_broadcast([P, H, n])
    L = DELTA_LEVELS

    @p.block.tensor
    def _(pe):
        pe.transpose(p.ps[0:n, 6, 0:H], beta[:, tok], p.con("ident", n=H, rows=H))
        pe.transpose(p.ps[0:n, 6, H:2 * H], gcum[:, tok], p.con("ident", n=H, rows=H))
        for h in range(H):
            pick = p.con("ident", first=h, n=1, rows=H).to_broadcast([H, P])
            pe.matmul(banks(0)[:, h], pick, gcum[:, tok], start=True, stop=True)
        for h in range(H):
            pick = p.con("ident", first=h, n=1, rows=H).to_broadcast([H, P])
            mm = pe.matmul(banks(2)[:, h], pick, beta[:, tok], start=True, stop=True)
        mm.then_inc(pe_ok.sem, 1)
        pe.wait_ge(dve_ok.sem, dve_ok.at(2))
        for h in range(H):
            mm = pe.matmul(banks(4)[:, h], kT[:, h], X[:, h], start=True, stop=True)
        mm.then_inc(pe_ok.sem, 1)
        for l in range(L):
            pe.wait_ge(dve_ok.sem, dve_ok.at(4 + 2 * l))
            for h in range(H):
                mm = pe.matmul(banks(0)[:, h], CT[:, h], Tm[:, h], start=True, stop=True)
            mm.then_inc(pe_ok.sem, 1)
            pe.wait_ge(act_ok.sem, act_ok.at(2 + l))
            for h in range(H):
                pe.matmul(banks(2)[:, h], Um[:, h], X[:, h], start=True, stop=True)
            for h in range(H):
                mm = pe.matmul(banks(4)[:, h], X[:, h], Um[:, h], start=True, stop=True)
            mm.then_inc(pe_ok.sem, 1)
        pe.wait_ge(dve_ok.sem, dve_ok.at(3 + 2 * L))
        for h in range(H):
            pe.transpose(banks(0)[:, h], vT[:, h], p.con("ident"))
        for h in range(H):
            pe.transpose(banks(2)[:, h], kT[:, h], p.con("ident"))
        for h in range(H):
            mm = pe.matmul(banks(4)[:, h], kT[:, h], qT[:, h], start=True, stop=True)
        mm.then_inc(pe_ok.sem, 1)
        if c:
            pe.wait_ge(dve_ok.sem, dve_ok.at(3 + 2 * L + 1))
            for h in range(H):
                mm = pe.matmul(banks(0)[:, h], CT[:, h], Um[:, h], start=True, stop=True)
            mm.then_inc(pe_ok.sem, 1)
            pe.wait_ge(act_ok.sem, act_ok.at(2 + L))
        else:
            pe.wait_ge(dve_ok.sem, dve_ok.at(3 + 2 * L + 1))
        for h in range(H):
            mm = pe.matmul(banks(2)[:, h], Um[:, h], X[:, h], start=True, stop=(c == 0))
            if c:
                mm = pe.matmul(banks(2)[:, h], NT[:, h], S[:, h], start=False, stop=True)
        mm.then_inc(pe_ok.sem, 1)
        pe.wait_ge(act_ok.sem, act_ok.at(2 + L + c))
        for h in range(H):
            mm = pe.matmul(banks(4)[:, h], Tm[:, h], DT[:, h], start=True, stop=(c == 0))
            if c:
                mm = pe.matmul(banks(4)[:, h], S[:, h], CT[:, h], start=False, stop=True)
        if c == 0:
            for h in range(H):
                mm = pe.matmul(banks(0)[:, h], CT[:, h], Tm[:, h], start=True, stop=True)
        mm.then_inc(pe_ok.sem, 1)

    @p.block.vector
    def _(dve):
        link = p.dve_steps.link
        dve.wait_ge(pe_ok.sem, pe_ok.at(1))
        dve.tensor_copy(beta_t, p.ps[:, 6, 0:H])
        link(dve, dve.tensor_copy(gc_t, p.ps[:, 6, H:2 * H]))
        link(dve, dve.tensor_copy(R, banks(0)))
        link(dve, dve.tensor_tensor(edec, R[:, :, n - 1:n].rearrange("p h t -> p (h t)"), gc_t, ALU.subtract))
        link(dve, dve.tensor_tensor(DT, R, b3(gc_t), ALU.subtract))
        dve.tensor_tensor(DT, DT, p.con("below")[:, None, :].to_broadcast([P, H, n]), ALU.add).then_inc(dve_ok.sem, 1)
        dve.tensor_tensor(X, kT, banks(2), ALU.mult).then_inc(dve_ok.sem, 1)
        for m in (Tm, Um):
            link(dve, dve.tensor_copy(m, p.con("ident")[:, None, :].to_broadcast([P, H, n])))
        dve.wait_ge(act_ok.sem, act_ok.at(1))
        dve.tensor_tensor(bg, beta_t, eg, ALU.mult)
        dve.wait_ge(pe_ok.sem, pe_ok.at(2))
        dve.tensor_tensor(NT, banks(4), DT, ALU.mult).then_inc(dve_ok.sem, 1)
        for l in range(L):
            if l == 0:
                dve.wait_ge(dve_ok.sem, dve_ok.at(3))
            level = p.con("levels", l * P, P)[:, None, :].to_broadcast([P, H, n])
            dve.tensor_tensor(CT, NT, level, ALU.mult).then_inc(dve_ok.sem, 1)
            dve.wait_ge(pe_ok.sem, pe_ok.at(2 + 2 * l + 2))
            dve.tensor_tensor(Tm, Tm, banks(2), ALU.subtract)
            dve.tensor_tensor(Um, Um, banks(4), ALU.subtract).then_inc(dve_ok.sem, 1)
            dve.wait_ge(dve_ok.sem, dve_ok.at(3 + 2 * l + 2))
        dve.wait_ge(pe_ok.sem, pe_ok.at(2 + 2 * L + 1))
        dve.tensor_tensor(X, banks(0), b3(beta_t), ALU.mult)
        if c == 0:
            dve.tensor_tensor(CT, banks(2), b3(edec), ALU.mult)
        else:
            dve.tensor_tensor(CT, banks(2), b3(bg), ALU.mult)
        dve.tensor_tensor(DT, banks(4), DT, ALU.mult).then_inc(dve_ok.sem, 1)
        if c:
            dve.wait_ge(pe_ok.sem, pe_ok.at(2 + 2 * L + 2))
            dve.tensor_tensor(CT, qT, R, ALU.mult).then_inc(dve_ok.sem, 1)
        dve.wait_ge(pe_ok.sem, pe_ok.at(2 + 2 * L + 3 + c))
        dve.tensor_copy(out[:, :, tok], banks(4))
        if c == 0:
            dve.tensor_copy(S, banks(0))

    @p.block.scalar
    def _(act):
        act.wait_ge(dve_ok.sem, dve_ok.at(1))
        act.activation(DT, DT, ACT.Exp)
        act.activation(edec, edec, ACT.Exp)
        act.activation(R, R, ACT.Exp)
        act.activation(eg, gc_t, ACT.Exp).then_inc(act_ok.sem, 1)
        for l in range(L):
            act.wait_ge(pe_ok.sem, pe_ok.at(2 + 2 * l + 1))
            act.activation(X, banks(0), ACT.Copy).then_inc(act_ok.sem, 1)
        if c:
            act.wait_ge(pe_ok.sem, pe_ok.at(2 + 2 * L + 2))
            act.activation(NT, banks(0), ACT.Copy, scale=-1.0).then_inc(act_ok.sem, 1)
            act.wait_ge(dve_ok.sem, dve_ok.at(3 + 2 * L + 2))
        act.wait_ge(pe_ok.sem, pe_ok.at(2 + 2 * L + 2 + c))
        act.activation(Tm, banks(2), ACT.Copy).then_inc(act_ok.sem, 1)

    pe_ok.close(2 + 2 * L + 3 + c)
    act_ok.close(1 + L + c + 1)
    dve_ok.close(3 + 2 * L + 1 + c)
    p.stage_end()


def moe(p):
    T, E = SEQ, N_EXPERTS
    combine, at = p.area(p.a0, E, T)
    hidden, at = p.area(at, D_FFE // P, T)
    silu, at = p.area(at, 2, T)
    gu, at = p.area(at, 2, T)
    lg, at = p.area(at, 2, 8 * 8)
    comb_rows, at = p.area(at, 1, T)
    norm(p, p.h, p.u, "norm_ffn", KD, T)
    logits, exps, weighed, rows_ok = (p.counted(s) for s in ("logits_ready", "router_exp_ready", "weights_ready", "weight_rows_ready"))

    @p.block.tensor
    def _(pe):
        for i in range(2):
            for k in range(KD):
                mm = pe.matmul(p.ps[:, 4 + i, 0:E], p.u[:, k, i * P:(i + 1) * P], p.par("router", 8 * k, 8), start=(k == 0), stop=(k == KD - 1))
            mm.then_inc(logits.sem, 1)
        pe.wait_ge(weighed.sem, weighed.at(2))
        for i in range(2):
            mm = pe.transpose(p.ps[0:E, 6, i * P:(i + 1) * P], lg[:, i, 56:64], p.con("ident"))
        mm.then_inc(logits.sem, 1)
        pe.wait_ge(rows_ok.sem, rows_ok.at(1))
        for e in range(E):
            mm = pe.matmul(p.ps[:, e, 0:T], p.con("ident", first=e, n=1, rows=E).to_broadcast([E, P]), comb_rows[0:E, 0], start=True, stop=True)
        mm.then_inc(logits.sem, 1)

    @p.block.vector
    def _(dve):
        link = p.dve_steps.link
        for i in range(2):
            x, top, idx = lg[:, i, 0:8], lg[:, i, 8:16], lg[:, i, 16:24]
            diff, w1, w2 = lg[:, i, 24:25], lg[:, i, 25:26], lg[:, i, 26:27]
            dve.wait_ge(logits.sem, logits.at(i + 1))
            link(dve, dve.tensor_copy(x, p.ps[:, 4 + i, 0:E]))
            link(dve, dve.max(top, x))
            link(dve, dve.max_index(p.indices[:, i], top, x))
            link(dve, dve.tensor_copy(idx, p.indices[:, i]))
            dve.tensor_tensor(diff, top[:, 1:2], top[:, 0:1], ALU.subtract).then_inc(exps.sem, 1)
            dve.wait_ge(exps.sem, exps.at(2 * i + 2))
            link(dve, dve.tensor_scalar(w1, w2, 1.0, None, ALU.add))
            link(dve, dve.reciprocal(w1, w1))
            link(dve, dve.tensor_tensor(w2, w2, w1, ALU.mult))
            a, b = lg[:, i, 32:40], lg[:, i, 40:48]
            dve.tensor_scalar(a, p.con("iota"), idx[:, 0:1], w1, ALU.is_equal, ALU.mult)
            link(dve, dve.tensor_scalar(b, p.con("iota"), idx[:, 1:2], w2, ALU.is_equal, ALU.mult))
            dve.tensor_tensor(lg[:, i, 56:64], a, b, ALU.add).then_inc(weighed.sem, 1)

    @p.block.scalar
    def _(act):
        for i in range(2):
            act.wait_ge(exps.sem, exps.at(2 * i + 1))
            act.activation(lg[:, i, 26:27], lg[:, i, 24:25], ACT.Exp).then_inc(exps.sem, 1)
        act.wait_ge(logits.sem, logits.at(3))
        act.activation(comb_rows[0:E, 0], p.ps[0:E, 6, 0:T], ACT.Copy).then_inc(rows_ok.sem, 1)
        act.wait_ge(logits.sem, logits.at(4))
        act.activation(combine, p.ps[:, :, 0:T], ACT.Copy)

    logits.close(4)
    exps.close(4)
    weighed.close(2)
    rows_ok.close(1)
    p.stage_end()

    seg = p.plan["moe"][0]
    kt, nu = D_FFE // P, len(seg.units)
    gated, up_ok = p.counted("gate_ready"), p.counted("up_ready")

    @p.block.tensor
    def _(pe):
        def body(e):
            for j, unit in enumerate(seg.units):
                s = j
                pe.wait_ge(p.full[seg.ring[s]], e * seg.full_step[s] + seg.full0[s])
                pe.wait_ge(p.unit_free, e * nu + (seg.unit_base + j - 1))
                if j == kt:
                    pe.wait_ge(p.unit_free, e * nu + (seg.unit_base + kt))
                pair = moe_pair(j, kt, nu)
                for c, chunk in enumerate(unit):
                    for n, (s, k, col, xk, which) in enumerate(chunk):
                        x = p.u if which == 0 else hidden
                        mm = pe.matmul(p.ps[:, 2 * pair + c, 0:T], p.ring[:, seg.ring[s], col:col + P], x[:, xk, 0:T],
                                       start=(n == 0), stop=(n == len(chunk) - 1))
                mm.then_inc(p.unit_done, 1)
        repeat(pe, N_EXPERTS, body)

    @p.block.scalar
    def _(act):
        def body(e):
            for j in range(kt):
                act.wait_ge(p.unit_done, e * nu + (seg.unit_base + j + 1))
                act.activation(silu[:, j % 2], p.ps[:, 2 * moe_pair(j, kt, nu), 0:T], ACT.Silu).then_inc(gated.sem, 1)
        repeat(act, N_EXPERTS, body)

    @p.block.vector
    def _(dve):
        def body(e):
            for j in range(nu):
                pair = moe_pair(j, kt, nu)
                dve.wait_ge(p.unit_done, e * nu + (seg.unit_base + j + 1))
                if j < kt:
                    dve.tensor_tensor(gu[:, j % 2], p.ps[:, 2 * pair + 1, 0:T], at_dyn(combine, e, 1)[:, 0], ALU.mult).then_inc(up_ok.sem, 1)
                    dve.wait_ge(up_ok.sem, e * kt + up_ok.at(j + 1))
                    dve.wait_ge(gated.sem, e * kt + gated.at(j + 1))
                    dve.tensor_tensor(hidden[:, j], silu[:, j % 2], gu[:, j % 2], ALU.mult).then_inc(p.unit_free, 1)
                else:
                    m = j - kt
                    dve.tensor_tensor(p.h[:, m, 0:T], p.ps[:, 2 * pair, 0:T], p.h[:, m, 0:T], ALU.add).then_inc(p.unit_free, 1)
        repeat(dve, N_EXPERTS, body)

    gated.close(kt * N_EXPERTS)
    up_ok.close(kt * N_EXPERTS)
    p.stage_end()


def moe_pair(j, kt, nu):
    return 2 if j == nu - 1 else j % 2


def layer_two(p, l):
    T = L2
    z, at = p.area(p.a0, 16, T)
    xs, at = p.area(at, 32, T)
    at_q = at
    q, at = p.area(at, 8, T)
    kv, at = p.area(at, 4, T)
    gates, at = p.area(at, 16, T)
    rows, at = p.area(at, 3, T)
    top = at
    norm(p, p.h, p.u, "norm1", KD * l, T)
    small_ok = p.counted("small_ready")
    H = SSD_HEADS
    dt, acum = rows[0:H, 0], rows[0:H, 1]
    tmp, _ = p.area(at_q, 5, T)
    t = [tmp[0:H, 0], dt, tmp[0:H, 1], tmp[0:H, 2], tmp[0:H, 3]]
    na = tmp[0:H, 4, 0:1]

    @p.block.tensor
    def _(pe):
        for k in range(KD):
            mm = pe.matmul(p.ps[0:H, 7, 0:T], p.par("w_dt", (l * KD + k) * H, H), p.u[:, k, 0:T], start=(k == 0), stop=(k == KD - 1))
        mm.then_inc(small_ok.sem, 1)

    softplus_rows(p, p.ps[0:H, 7, 0:T], p.par("dt_bias", l)[0:H], p.par("a_log", l)[0:H], t, na)

    @p.block.vector
    def _(dve):
        p.dve_steps.link(dve, dve.tensor_scalar(t[0], dt, na, -1.0, ALU.mult, ALU.mult))
        for o, n in CHUNKS2:
            dve.tensor_tensor_scan(acum[:, o:o + n], t[0][:, o:o + n], t[0][:, o:o + n], 0.0, ALU.add, ALU.bypass)

    p.stage_end()
    gemm(p, f"z{l}", [p.u], T, act_unit=take_copy(p, z, T, func=ACT.Silu))
    p.stage_end()
    a, d, sig = conv_silu(p, f"xbc{l}", xs, T, "conv_w", l * CONV2 * 32, 32, "conv_b", l * 32, 16, at_q)
    gemm(p, f"xbc{l}", [p.u], T, a, d, sig)
    p.stage_end()
    gemm(p, f"q{l}", [p.u], T, act_unit=take_copy(p, q, T))
    gemm(p, f"kv{l}", [p.u], T, act_unit=take_copy(p, kv, T))

    def gate_unit(act, u, j, bank):
        for c in range(2):
            ins = act.activation(at_dyn(gates, 2 * u + c, 1)[:, 0], bank[:, c], ACT.Sigmoid, bias=p.par_dyn("b_gate", 2 * u + (l * 16 + c)))
        ins.then_inc(p.unit_free, 1)

    gemm(p, f"gate{l}", [p.u], T, act_unit=gate_unit)
    p.stage_end()

    ssd(p, l, xs, dt, acum, top)
    y = xs[:, 0:16]

    @p.block.vector
    def _(dve):
        dve.tensor_tensor(y, y, z, ALU.mult)

    p.stage_end()
    for half in range(2):
        head_norm(p, y[:, 8 * half:8 * half + 8], 8, T, "ones", 1.0 / 256, EPS,
                  [p.par("ssd_norm", l * 16 + 8 * half + c) for c in range(8)], group=2)
    merged, _ = p.area(p.a0, 8, T)

    def gated_unit(dve, u, j, bank):
        dve.tensor_tensor(at_dyn(merged, u, 1), bank, at_dyn(gates, u, 1), ALU.mult).then_inc(p.unit_free, 1)

    gemm(p, f"ssd_down{l}", [y], T, dve_unit=gated_unit)
    p.stage_end()

    at = p.a0 + 16 * T
    o, at = p.area(at, 8, T)
    kd, at = p.area(at, 4, T)
    v_tok, at = p.area(at, 3, 256)
    rot, at = p.area(at, 2, T)
    k = kv[:, 0:2]
    head_norm(p, q, 8, T, "pair_ones", 1.0 / 64, EPS, [p.par("q_norm", l)])
    head_norm(p, k, 2, T, "pair_ones", 1.0 / 64, EPS, [p.par("k_norm", l)])
    for x, n in ((q, 8), (k, 2)):
        rotary(p, x, n, T)

    @p.block.scalar
    def _(act):
        for h in range(KV_HEADS):
            lo = 64 * (h % 2)
            for half in range(2):
                act.activation(kd[64 * half:64 * half + 64, h], k[lo:lo + 64, h // 2], ACT.Copy)

    to_tokens(p, kv[:, 2:4], 2, CHUNKS2, v_tok, T)
    items = []
    for h in range(ATTN_HEADS):
        lo, g = 64 * (h % 2), h // 4
        for i, (first, nq) in enumerate(CHUNKS2):
            nk = first + nq
            items.append(dict(
                nq=nq, nk=nk, tiles=CHUNKS2[:i + 1], part=lo, sink=p.par("sinks", l * 16 + h)[0:nq],
                mask=p.con("window", i * L2, nk, rows=nq), q=q[lo:lo + 64, h // 2, first:first + nq], k=kd[lo:lo + 64, g, 0:nk],
                v=[v_tok[0:m, n, 64 * g:64 * g + 64] for n, (_, m) in enumerate(CHUNKS2[:i + 1])],
                out=o[lo:lo + 64, h // 2, first:first + nq]))
    attention(p, items, ATTN_DIM ** -0.5, at)
    product = p.counted("gated_product_ready")

    def merge_unit(dve, u, j, bank):
        dve.tensor_tensor(rot, bank, gates[:, 2 * u + 8:2 * u + 10], ALU.mult).then_inc(product.sem, 1)
        dve.wait_ge(product.sem, product.at(u + 1))
        m = merged[:, 2 * u:2 * u + 2]
        dve.tensor_tensor(m, m, rot, ALU.add).then_inc(p.unit_free, 1)
        dve.wait_ge(p.unit_free, p.plan[f"attn_down{l}"][0].unit_base + u + 1)

    gemm(p, f"attn_down{l}", [o], T, dve_unit=merge_unit, signals=[("gated_product_ready", 4)])
    p.stage_end()
    gemm(p, f"w_o{l}", [merged], T, dve_unit=take_add(p, p.h, T, 2))
    p.stage_end()


def rotary(p, x, n, T):
    swapped = p.counted("swapped")
    tmp = p.work[:, 0:n * T].rearrange("p (k t) -> p k t", t=T)

    @p.block.tensor
    def _(pe):
        for c in range(n):
            mm = pe.matmul(p.ps[:, c, 0:T], p.con("swap"), x[:, c], start=True, stop=True)
        mm.then_inc(swapped.sem, 1)

    @p.block.vector
    def _(dve):
        wide = lambda name: p.con(name)[:, None, :].to_broadcast([P, n, T])
        dve.wait_ge(swapped.sem, swapped.at(1))
        p.dve_steps.link(dve, dve.tensor_tensor(tmp, p.ps[:, 0:n, 0:T], wide("sin"), ALU.mult))
        p.dve_steps.link(dve, dve.tensor_tensor(x, x, wide("cos"), ALU.mult))
        dve.tensor_tensor(x, x, tmp, ALU.add)

    swapped.close(1)
    p.stage_end()


def ssd(p, l, xs, dt, acum, at):
    H, R, G = SSD_HEADS, SSD_R, SSD_GROUPS
    state, at = p.area(at, H * SSD_P)
    xdt = p.u_flat[:, 0:H * SSD_P]
    xdec = p.work[:, 0:H * SSD_P]
    b_tok, at = p.area(at, G * P)
    cols, at = p.area(at, 5, H)
    arg, at = p.area(at, 2, R, P)
    eR, at = p.area(at, 2, R, P)
    mt, at = p.area(at, 2, R, P)
    dt_t, ac_t, dec, gl, dd = (cols[:, i] for i in range(5))
    B, C = xs[:, 16:24], xs[:, 24:32]
    pe_ok, act_ok, dve_ok = p.counted("products_ready"), p.counted("scalar_ready"), p.counted("vector_ready")

    for ci, (o, n) in enumerate(CHUNKS2):
        last = ci == 2
        @p.block.tensor
        def _(pe):
            pe.transpose(p.ps[0:n, 0, 0:H], dt[:, o:o + n], p.con("ident", n=H, rows=H))
            pe.transpose(p.ps[0:n, 0, H:2 * H], acum[:, o:o + n], p.con("ident", n=H, rows=H))
            pe.matmul(p.ps[:, 1, 0:H], acum[:, o + n - 1:o + n].to_broadcast([H, P]), p.con("ident", n=H, rows=H), start=True, stop=True).then_inc(pe_ok.sem, 1)
            for b in range(4):
                for c in range(4):
                    mm = pe.transpose(p.ps[0:n, 2 + b, c * P:(c + 1) * P], xs[:, 4 * b + c, o:o + n], p.con("ident"))
            mm.then_inc(pe_ok.sem, 1)
            for b in range(2):
                for c in range(4):
                    mm = pe.transpose(p.ps[0:n, 6 + b, c * P:(c + 1) * P], B[:, 4 * b + c, o:o + n], p.con("ident"))
            mm.then_inc(pe_ok.sem, 1)

        @p.block.vector
        def _(dve):
            link = p.dve_steps.link
            dve.wait_ge(pe_ok.sem, pe_ok.at(1))
            dve.tensor_copy(dt_t[0:n], p.ps[0:n, 0, 0:H])
            dve.tensor_copy(ac_t[0:n], p.ps[0:n, 0, H:2 * H])
            link(dve, dve.tensor_copy(gl, p.ps[:, 1, 0:H]))
            dve.tensor_tensor(dec[0:n], gl[0:n], ac_t[0:n], ALU.subtract).then_inc(dve_ok.sem, 1)
            dve.wait_ge(pe_ok.sem, pe_ok.at(2))
            wide = lambda x: x[:, :, None].to_broadcast([n, H, SSD_P])
            rows = lambda x: x[0:n].rearrange("p (h d) -> p h d", d=SSD_P)
            link(dve, dve.tensor_tensor(rows(xdt), p.ps[0:n, 2:6, :].rearrange("p b (h d) -> p (b h) d", d=SSD_P), wide(dt_t[0:n]), ALU.mult))
            if not last:
                dve.wait_ge(act_ok.sem, act_ok.at(1))
                dve.tensor_tensor(rows(xdec), rows(xdt), wide(dec[0:n]), ALU.mult)

        @p.block.scalar
        def _(act):
            act.wait_ge(dve_ok.sem, dve_ok.at(1))
            act.activation(dec[0:n], dec[0:n], ACT.Exp).then_inc(act_ok.sem, 1)
            act.activation(gl, gl, ACT.Exp)
            act.wait_ge(pe_ok.sem, pe_ok.at(3))
            act.activation(b_tok[0:n].rearrange("p (b t) -> p b t", t=512), p.ps[0:n, 6:8, :], ACT.Copy)

        pe_ok.close(3)
        dve_ok.close(1)
        act_ok.close(1)
        p.stage_end()
        decays, cbs, ys, sts = (p.counted(s) for s in ("decay_rows_ready", "cb_ready", "y_ready", "state_ready"))
        args, exps, mts, ctaken, ytaken = (p.counted(s) for s in ("decay_args_ready", "decay_exp_ready", "mt_ready", "c_scaled_ready", "y_taken"))

        @p.block.tensor
        def _(pe):
            def first(g):
                if g >= 2:
                    pe.wait_ge(exps.sem, exps.at(g - 1))
                    pe.wait_ge(mts.sem, mts.at(g - 1))
                for r in range(R):
                    mm = pe.matmul(p.ps[:, g % 2, r * P:r * P + n], p.con("ident", first=4 * g + r, n=1, rows=H).to_broadcast([H, P]),
                                   acum[:, o:o + n], start=True, stop=True)
                mm.then_inc(decays.sem, 1)
                pe.matmul(p.ps[0:n, 2 + g % 2, 0:n], B[:, g, o:o + n], C[:, g, o:o + n], start=True, stop=True).then_inc(cbs.sem, 1)

            def second(g):
                pe.wait_ge(mts.sem, mts.at(g + 1))
                if ci:
                    pe.wait_ge(ctaken.sem, ctaken.at(g + 1))
                if g >= 2:
                    pe.wait_ge(ytaken.sem, ytaken.at(g - 1))
                for r in range(R):
                    h = 4 * g + r
                    lo = 64 * (r % 2)
                    out = p.ps[lo:lo + 64, 4 + g % 2, (r // 2) * P:(r // 2) * P + n]
                    mm = pe.matmul(out, xdt[0:n, h * 64:(h + 1) * 64], mt[0:n, g % 2, r, 0:n], start=True, stop=(ci == 0))
                    if ci:
                        mm = pe.matmul(out, state[:, h * 64:(h + 1) * 64], eR[:, g % 2, r, 0:n], start=False, stop=True)
                if not last:
                    mm = pe.matmul(p.ps[:, 6 + g % 2, 0:256], b_tok[0:n, g * P:(g + 1) * P], xdec[0:n, g * 256:(g + 1) * 256], start=True, stop=True)
                mm.then_inc(ys.sem, 1)

            for g in range(G + 1):
                if g < G:
                    first(g)
                if g:
                    second(g - 1)

        @p.block.scalar
        def _(act):
            def early(g):
                act.wait_ge(decays.sem, decays.at(g + 1))
                if g >= 2:
                    act.wait_ge(ys.sem, ys.at(g - 1))
                bank = p.ps[:, g % 2, :].rearrange("p (r t) -> p r t", t=P)[:, :, 0:n]
                act.wait_ge(args.sem, args.at(g + 1))
                if ci:
                    act.activation(eR[:, g % 2, :, 0:n], bank, ACT.Exp)
                act.activation(arg[0:n, g % 2, :, 0:n], arg[0:n, g % 2, :, 0:n], ACT.Exp).then_inc(exps.sem, 1)

            for g in range(G):
                early(g)

        @p.block.vector
        def _(dve):
            def early(g):
                dve.wait_ge(decays.sem, decays.at(g + 1))
                bank = p.ps[0:n, g % 2, :].rearrange("p (r t) -> p r t", t=P)
                for r in range(R):
                    ins = dve.scalar_tensor_tensor(arg[0:n, g % 2, r, 0:n], bank[:, r, 0:n], ac_t[0:n, 4 * g + r:4 * g + r + 1],
                                                   p.con("below")[0:n, 0:n], ALU.subtract, ALU.add)
                ins.then_inc(args.sem, 1)

            def middle(g):
                dve.wait_ge(exps.sem, exps.at(g + 1))
                dve.wait_ge(cbs.sem, cbs.at(g + 1))
                cb = p.ps[0:n, 2 + g % 2, 0:n][:, None, :].to_broadcast([n, R, n])
                dve.tensor_tensor(mt[0:n, g % 2, :, 0:n], arg[0:n, g % 2, :, 0:n], cb, ALU.mult).then_inc(mts.sem, 1)
                if ci:
                    dve.tensor_tensor(eR[:, g % 2, :, 0:n], eR[:, g % 2, :, 0:n], C[:, g, o:o + n][:, None, :].to_broadcast([P, R, n]),
                                      ALU.mult).then_inc(ctaken.sem, 1)

            def late(g):
                dve.wait_ge(ys.sem, ys.at(g + 1))
                for c in range(2):
                    x = xs[:, 2 * g + c, o:o + n]
                    ins = dve.scalar_tensor_tensor(x, x, p.par("d_skip", l * 16 + 2 * g + c), p.ps[:, 4 + g % 2, c * P:c * P + n], ALU.mult, ALU.add)
                if not last:
                    st = state[:, g * 256:(g + 1) * 256]
                    new = p.ps[:, 6 + g % 2, 0:256]
                    if ci:
                        s4 = st.rearrange("p (r d) -> p r d", d=SSD_P)
                        p.dve_steps.link(dve, dve.tensor_tensor(s4, s4, gl[:, 4 * g:4 * g + 4][:, :, None].to_broadcast([P, R, SSD_P]), ALU.mult))
                        ins = dve.tensor_tensor(st, st, new, ALU.add)
                    else:
                        ins = dve.tensor_copy(st, new)
                ins.then_inc(ytaken.sem, 1)

            for g in range(G + 1):
                if g < G:
                    early(g)
                    middle(g)
                if g:
                    late(g - 1)

        for s in (decays, cbs, ys, args, exps, mts, ytaken):
            s.close(G)
        if ci:
            ctaken.close(G)
        p.stage_end()


def mlp_two(p, l):
    T = L2
    hidden, at = p.area(p.a0, FF2 // P, T)
    relu, at = p.area(at, 4, T)
    norm(p, p.h, p.u, "norm2", KD * l, T)

    seg = p.plan[f"up{l}"][0]

    def act_square(act, u, j, bank):
        b = 2 * (j % 2)
        act.activation(relu[:, b:b + 2], bank, ACT.Relu).then_inc(p.unit_free, 1)
        act.wait_ge(p.unit_free, u + (seg.unit_base + 1))
        act.activation(at_dyn(hidden, 2 * u, 2), relu[:, b:b + 2], ACT.Square)

    gemm(p, f"up{l}", [p.u], T, act_unit=act_square)
    p.stage_end()
    gemm(p, f"down{l}", [hidden], T, dve_unit=take_add(p, p.h, T, 1))
    p.stage_end()


def build(nc, weights, params, consts, x, mem, meta, out, upto=10):
    with ExitStack() as ctx:
        block = None
        p = Program(nc, ctx, block, upto)
        p.u_flat = p.u[:].rearrange("p k t -> p (k t)")
        p.mem_k, at = p.area(0, 4, SEQ)
        p.mem_v, at = p.area(at, 4, SEQ)
        first_a0 = at
        tok_in, at = p.area(at, 4, D)
        meta_tok, at = p.area(at, 1, D)
        p.mem, at = p.area(at, KD, SEQ)
        mem_end = at
        p.block = ctx.enter_context(nc.Block())
        p.n_loads = 16 * 5

        @p.block.sync
        def _(sp):
            sp.dma_start(p.consts[:], consts).then_inc(p.loaded, 16)
            sp.dma_start(tok_in[:, 0:2], x[0].rearrange("(i p) d -> p i d", p=P)).then_inc(p.loaded, 16)
            sp.dma_start(tok_in[:, 2:4], mem[0].rearrange("(i p) d -> p i d", p=P)).then_inc(p.loaded, 16)
            sp.dma_start(p.params[:], params).then_inc(p.loaded, 16)
            sp.dma_start(meta_tok[0:N_META, 0], meta).then_inc(p.loaded, 16)
            used = {name for name, *_ in STREAM[:(2, 4, 6, 8, 10, 12, 13, 21, 23, 31, 33)[upto]]}
            for seg in p.order:
                if seg.name not in used:
                    continue
                def body(i):
                    n, nu = len(seg.slots), len(seg.units)
                    for j, cols in enumerate(seg.slots):
                        s = seg.ring[j]
                        if seg.free0[j] > 0 or (is_register(i) and seg.free0[j] + nu > 0):
                            sp.wait_ge(p.unit_done, i * nu + seg.free0[j])
                        index = i * n + (seg.slot_base + j)
                        src = weights[index] if isinstance(index, int) else weights[bass.ds(index, 1)].rearrange("a p c -> (a p) c")
                        sp.dma_start(p.ring[:, s, 0:cols], src[:, 0:cols]).then_inc(p.full[s], 16)
                repeat(sp, seg.iters, body)

        x_tiles = ((0, P), (P, P))
        from_tokens(p, tok_in[:, 0:2], p.h, x_tiles)
        from_tokens(p, tok_in[:, 2:4], p.mem, x_tiles)
        p.a0 = first_a0
        meta_h = ctx.enter_context(nc.sbuf_tensor("meta_h", [P, KD, N_META], F32))
        from_tokens(p, meta_tok, meta_h, ((0, N_META),))
        for layer in range(2):
            memory_heads(p, layer)
        stages = [
            lambda: layer_even(p), lambda: cross_attention(p, 0), lambda: dense_ffn(p),
            lambda: layer_odd(p), lambda: cross_attention(p, 1), lambda: moe(p),
        ]
        for s in stages[:min(upto, 6)]:
            s()
        T = SEQ
        first = 0
        if upto > 6:
            @p.block.vector
            def _(dve):
                p.dve_steps.link(dve, dve.tensor_copy(p.u[:, :, 0:SEQ], p.h[:, :, 0:SEQ]))
                dve.tensor_copy(p.h[:, :, N_META:L2], p.u[:, :, 0:SEQ])
                dve.tensor_copy(p.h[:, :, 0:N_META], meta_h[:])

            p.stage_end()
            p.a0 = 0
            first = N_META
            stages = [lambda: layer_two(p, 0), lambda: mlp_two(p, 0), lambda: layer_two(p, 1), lambda: mlp_two(p, 1)]
            for s in stages[:upto - 6]:
                s()
        res, _ = p.area(0, 2, D)
        to_tokens(p, p.h, KD, ((first, P), (first + P, P)), res, T)

        @p.block.sync
        def _(sp):
            sp.wait_ge(p.stage_done, 3 * p.stages)
            sp.dma_start(out[0].rearrange("(i p) d -> p i d", p=P), res).then_inc(p.stored, 16)
            sp.wait_ge(p.stored, 16)


def pack_weights(a):
    _, order, n_slots = plan_stream()
    w = np.zeros((n_slots, P, SLOT), np.float32)
    at = 0

    def wide(m):
        nonlocal at
        m = np.asarray(m)
        n = m.shape[1] // 256
        w[at:at + n] = m.reshape(KD, P, n, 256).transpose(2, 1, 0, 3).reshape(n, P, SLOT)
        at += n

    def deep(m):
        nonlocal at
        m = np.asarray(m)
        kt = m.shape[0] // P
        parts = 1 if kt <= 16 else 2
        c = m.reshape(parts, kt // parts, P, 8, P).transpose(3, 0, 2, 1, 4).reshape(8 * parts, P, kt // parts * P)
        w[at:at + 8 * parts, :, 0:c.shape[2]] = c
        at += 8 * parts

    def flat(m):
        nonlocal at
        w[at] = np.asarray(m).reshape(2, P, D).transpose(1, 0, 2).reshape(P, SLOT)
        at += 1

    def pairs(m):
        m = np.asarray(m)
        f = m.shape[1] // 2 // P
        wide(m.reshape(D, 2, f, P).transpose(0, 2, 1, 3).reshape(D, 2 * f * P))

    wide(a["xa_w_kv"][0])
    wide(a["xa_w_kv"][1])
    wide(a["ev_w_in"][0])
    wide(a["ev_w_out"][0])
    wide(a["xa_w_q"][0])
    flat(a["xa_w_o"][0])
    pairs(a["ff_w_gu"][0])
    deep(a["ff_w_down"][0])
    wide(a["od_w_in"][0][:, 0:4 * D])
    wide(a["od_w_out"][0])
    wide(a["xa_w_q"][1])
    flat(a["xa_w_o"][1])
    for e in range(N_EXPERTS):
        pairs(a["moe_w_gu"][0, e])
        deep(a["moe_w_down"][0, e])
    for l in range(2):
        m = np.asarray(a["w_in_2"][l])
        wide(m[:, 0:2048])
        wide(m[:, 2048:6144])
        wide(m[:, 6176:7200])
        wide(m[:, 7200:7712])
        wide(m[:, 7712:9760])
        deep(a["w_ssd_down_2"][l])
        wide(a["w_attn_down_2"][l])
        wide(a["w_o_2"][l])
        wide(a["w_mlp_up_2"][l])
        deep(a["w_mlp_down_2"][l])
    assert at == n_slots
    return w


def pack_params(a):
    ch = lambda v: np.asarray(v).reshape(-1, P).T
    twice = lambda v: np.concatenate([np.asarray(v), np.asarray(v)], axis=-1).reshape(-1, P).T
    tiles = lambda m: np.asarray(m).reshape(KD, P, -1).transpose(1, 0, 2).reshape(P, -1)

    def rows(v):
        v = np.asarray(v)
        v = v.reshape(-1, v.shape[-1])
        out = np.zeros((P, v.shape[0]), np.float32)
        out[0:v.shape[1]] = v.T
        return out

    skip = np.asarray(a["d_skip_2"])
    parts = {
        "norm_mix": ch(a["norm_mix"]), "norm_xattn": ch(a["norm_xattn"]), "norm_mem": ch(a["norm_mem"]),
        "norm_ffn": ch(a["norm_ffn"]), "ev_conv": ch(a["ev_conv"]), "ev_q_norm": twice(a["ev_q_norm"]),
        "ev_k_norm": twice(a["ev_k_norm"]), "od_conv": ch(a["od_conv"]), "od_o_norm": ch(a["od_o_norm"]),
        "od_a_log": rows(a["od_a_log"]), "od_dt_bias": rows(a["od_dt_bias"]),
        "xa_q_norm": twice(a["xa_q_norm"]), "xa_k_norm": twice(a["xa_k_norm"]),
        "od_small": tiles(np.asarray(a["od_w_in"])[0][:, 4 * D:]), "router": tiles(a["moe_router"][0]),
        "norm1": ch(a["norm1_g_2"]), "norm2": ch(a["norm2_g_2"]), "conv_w": ch(a["conv_w_2"]), "conv_b": ch(a["conv_b_2"]),
        "b_gate": ch(a["b_gate_2"]), "d_skip": ch(np.repeat(skip, 64, axis=-1)), "ssd_norm": ch(a["ssd_norm_g_2"]),
        "q_norm": twice(a["q_norm_g_2"]), "k_norm": twice(a["k_norm_g_2"]),
        "dt_bias": rows(a["dt_bias_2"]), "a_log": rows(a["a_log_2"]),
        "w_dt": np.concatenate([tiles(np.asarray(a["w_in_2"])[l][:, 6144:6176]) for l in range(2)], axis=1),
        "sinks": np.broadcast_to(np.asarray(a["sinks_2"]).reshape(1, 32), (P, 32)),
    }
    for name, n in PARAMS:
        assert parts[name].shape == (P, n), (name, parts[name].shape, n)
    return np.concatenate([parts[name] for name, _ in PARAMS], axis=1).astype(np.float32)


def make_consts():
    f = np.float32
    i = np.arange(P)
    out = {"ident": np.eye(P), "ones": np.ones((P, P)), "pair_ones": (i[:, None] // 64 == i[None] // 64)}
    s = np.zeros((P, P))
    for r in range(P):
        if r % 64 < 32:
            s[r + 32, r] = -1
        else:
            s[r - 32, r] = 1
    out["swap"] = s
    t, j = np.arange(SEQ)[:, None], np.arange(SEQ)[None]
    count = np.zeros((SEQ, SEQ))
    for window, d in ((128, 1), (512, 4), (2048, 16)):
        count += (j <= t) & ((t - j) % d == 0) & ((t - j) // d <= window // d)
    m = np.where(count > 0, np.log(np.maximum(count, 1)), NEG)
    out["dilated"] = np.concatenate([m[0:P], m[P:]], axis=1)
    out["zero_mask"] = np.zeros((P, 2 * SEQ))
    w = np.zeros((P, 3 * L2))
    for n, (first, rows) in enumerate(CHUNKS2):
        q, k = np.arange(first, first + rows)[:, None], np.arange(L2)[None]
        w[0:rows, n * L2:(n + 1) * L2] = np.where((k <= q) & ((k < N_META) | (q - k < WINDOW)), 0.0, NEG)
    out["window"] = w
    inv = f(10000.0) ** (-np.arange(32, dtype=f) / f(32))
    ang = np.arange(L2, dtype=f)[:, None] * inv[None, :].astype(f)
    out["cos"] = np.cos(ang).astype(f)[:, i % 32].T
    out["sin"] = np.sin(ang).astype(f)[:, i % 32].T
    lv = []
    for l in range(DELTA_LEVELS):
        b = 2 << l
        jj, ii = i[:, None], i[None]
        lv.append((jj // b == ii // b) & (ii % b >= b // 2) & (jj % b < b // 2))
    out["levels"] = np.concatenate(lv, axis=1)
    out["below"] = np.where(i[None] >= i[:, None], 0.0, NEG)
    out["iota"] = np.broadcast_to(np.arange(8), (P, 8))
    return np.concatenate([out[name].astype(f) for name, _ in CONSTS], axis=1)


def kernel(**inputs):
    import concourse.bacc as bacc
    from concourse.bass_utils import run_bass_kernel_spmd

    a = {k: np.asarray(v) for k, v in inputs.items()}
    arrays = {
        "in_weights": pack_weights(a), "in_params": pack_params(a), "in_consts": make_consts(),
        "in_x": np.ascontiguousarray(a["x"]), "in_mem": np.ascontiguousarray(a["mem"]),
        "in_meta": np.ascontiguousarray(a["meta_tokens_2"]),
    }
    nc = bacc.Bacc("TRN2", target_bir_lowering=False, num_devices=1)
    aps = [nc.dram_tensor(n, v.shape, F32, kind="ExternalInput").ap() for n, v in arrays.items()]
    out = nc.dram_tensor("out_h", (1, SEQ, D), F32, kind="ExternalOutput").ap()
    build(nc, *aps, out)
    r = run_bass_kernel_spmd(nc, [arrays], core_ids=[0])
    return r.results[0]["out_h"]
```

```python
from contextlib import ExitStack

import numpy as np
import concourse.bass as bass
from concourse import mybir

F32 = mybir.dt.float32
F32R = mybir.dt.float32r
U32 = mybir.dt.uint32
ALU = mybir.AluOpType
ACT = mybir.ActivationFunctionType
AX_X = mybir.AxisListType.X

P = 128
D = 1024
KD = D // P
SEQ = 256
EPS = 1e-6
NEG = -1e30

B_HEADS, B_DIM = 8, 64
C_HEADS, C_DIM, C_CONV = 8, 128, 4
X_HEADS = 4
A_CONV = 3
D_FF = 2816
N_EXPERTS = 8
D_FFE = D_FF // 2
DELTA_CHUNK = 128
DELTA_LEVELS = 7

N_META = 16
L2 = SEQ + N_META
CHUNKS2 = ((0, 16), (16, 128), (144, 128))
SSD_HEADS, SSD_GROUPS, SSD_R, SSD_P = 32, 8, 4, 64
ATTN_HEADS, KV_HEADS, ATTN_DIM = 16, 4, 64
WINDOW = 128
FF2 = 4 * D
CONV2 = 4
CONV_CHUNKS2 = 32

RING = 4
SPLITS = 2
SLOT = 2048

STREAM = (
    [("xa_kv0", "wide", 2), ("xa_kv1", "wide", 2)]
    + [("ev_in", "wide", 12), ("ev_out", "wide", 4), ("xa_q0", "wide", 1), ("xa_o0", "flat", 4)]
    + [("ff_gu", "wide", 22), ("ff_down", "deep", 22)]
    + [("od_in", "wide", 16), ("od_out", "wide", 4), ("xa_q1", "wide", 1), ("xa_o1", "flat", 4)]
    + [("moe", "moe", 8)]
    + [
        (f"{n}{l}", kind, size)
        for l in range(2)
        for n, kind, size in (
            ("xbc", "wide", 16), ("z", "wide", 8), ("q", "wide", 4), ("kv", "wide", 2), ("gate", "wide", 8),
            ("ssd_down", "deep", 16), ("attn_down", "wide", 4), ("w_o", "wide", 4),
            ("up", "wide", 16), ("down", "deep", 32),
        )
    ]
)


class Segment:

    def __init__(self, name, iters, slots, units, unit0):
        self.name, self.iters, self.slots, self.units, self.unit0 = name, iters, slots, units, unit0
        self.parts, self.part_end, self.last_part, self.first_used = 0, [], [0] * len(slots), []
        seen = set()
        for unit in units:
            used = sorted({c[0] for chunk in unit for c in chunk})
            self.first_used.append([s for s in used if s not in seen])
            seen |= set(used)
            for s in used:
                self.parts += 1
                self.last_part[s] = self.parts
            self.part_end.append(self.parts)


def wide_unit(s):
    return [[(s, k, k * 256 + c * P, k, 0) for k in range(KD)] for c in range(2)]


def plan_stream():
    plan, order = {}, []
    for name, kind, size in STREAM:
        segs = []
        if kind == "wide":
            n = size // 4 if size >= 8 else 0
            if n:
                segs.append(Segment(name, n, [SLOT] * 4, [wide_unit(s) for s in range(4)], 0))
            if size - 4 * n:
                rest = size - 4 * n
                segs.append(Segment(name, 1, [SLOT] * rest, [wide_unit(s) for s in range(rest)], 4 * n))
        elif kind == "deep":
            parts = 1 if size <= 16 else 2
            kt = size // parts
            per = 4 // parts
            units = [[[(u * parts + k // kt, k % kt, (k % kt) * P, k, 0) for k in range(size)]] for u in range(per)]
            segs.append(Segment(name, 8 // per, [kt * P] * 4, units, 0))
        elif kind == "flat":
            units = [[[(0, k, k * D + (2 * u + c) * P, k, 0) for k in range(2)] for c in range(2)] for u in range(4)]
            segs.append(Segment(name, 1, [SLOT], units, 0))
        else:
            kt = D_FFE // P
            units = [wide_unit(s) for s in range(kt)]
            units += [[[(kt + c, k, k * P, k, 1) for k in range(kt)]] for c in range(8)]
            segs.append(Segment(name, N_EXPERTS, [SLOT] * kt + [kt * P] * 8, units, 0))
        plan[name] = segs
        order += segs
    position, units_before, parts_before, slots_before = 0, 0, 0, 0
    fills = [0] * RING
    ring_holds, split_ends = [0] * RING, [0] * SPLITS
    for seg in order:
        looped = seg.iters > 1
        if looped:
            position = -(-position // RING) * RING
        seg.unit_base, seg.part_base, seg.slot_base = units_before, parts_before, slots_before
        n, nu, npart = len(seg.slots), len(seg.units), seg.parts
        seg.ring = [(position + j) % RING for j in range(n)]
        per = [seg.ring.count(s) for s in range(RING)]
        seen = list(fills)
        seg.full0, seg.full_step, seg.ring_free0, seg.split_free0 = [], [], [], []
        for j, s in enumerate(seg.ring):
            seen[s] += 1
            seg.full0.append(16 * seen[s])
            seg.full_step.append(16 * per[s])
            same = [i for i in range(n) if seg.ring[i] == s]
            half = [i for i in range(n) if seg.ring[i] % SPLITS == s % SPLITS]
            if same[0] < j:
                seg.ring_free0.append(slots_before + [i for i in same if i < j][-1] + 1)
            else:
                again = slots_before + same[-1] + 1 - n if looped else 0
                seg.ring_free0.append(max(again, ring_holds[s]))
            if half[0] < j:
                seg.split_free0.append(parts_before + seg.last_part[[i for i in half if i < j][-1]])
            else:
                again = parts_before + seg.last_part[half[-1]] - npart if looped else 0
                seg.split_free0.append(max(again, split_ends[s % SPLITS]))
        for j, s in enumerate(seg.ring):
            ring_holds[s] = slots_before + (seg.iters - 1) * n + j + 1
            split_ends[s % SPLITS] = parts_before + (seg.iters - 1) * npart + seg.last_part[j]
        for s in range(RING):
            fills[s] += seg.iters * per[s]
        position = -(-(position + n) // RING) * RING if looped else position + n
        units_before += seg.iters * nu
        parts_before += seg.iters * npart
        slots_before += seg.iters * n
    for seg, after in zip(order, order[1:] + [None]):
        seg.after = after
        seg.split_cols = list(seg.slots)
        if seg.iters > 1 and after is not None:
            seg.split_cols[0] = max(seg.slots[0], after.slots[0])
    return plan, order, slots_before


def split_segment(seg, n):
    a = Segment(seg.name, n, seg.slots, seg.units, seg.unit0)
    b = Segment(seg.name, seg.iters - n, seg.slots, seg.units, 0)
    for s, done in ((a, 0), (b, n)):
        s.ring, s.full_step, s.split_cols = seg.ring, seg.full_step, seg.split_cols
        s.full0 = [f + done * st for f, st in zip(seg.full0, seg.full_step)]
        s.ring_free0 = [f + done * len(seg.slots) for f in seg.ring_free0]
        s.split_free0 = [f + done * seg.parts for f in seg.split_free0]
        s.unit_base = seg.unit_base + done * len(seg.units)
        s.part_base = seg.part_base + done * seg.parts
        s.slot_base = seg.slot_base + done * len(seg.slots)
    a.after, b.after = b, seg.after
    return a, b


PARAMS = [
    ("norm_mix", 2 * KD), ("norm_xattn", 2 * KD), ("norm_mem", 2 * KD), ("norm_ffn", 2 * KD),
    ("ev_conv", A_CONV * 4), ("ev_q_norm", 1), ("ev_k_norm", 1),
    ("od_conv", C_CONV * 24), ("od_o_norm", 1), ("od_a_log", 1), ("od_dt_bias", 1),
    ("xa_q_norm", 2), ("xa_k_norm", 2),
    ("od_small", KD * 16), ("router", KD * 8),
    ("norm1", 2 * KD), ("norm2", 2 * KD), ("conv_w", 2 * CONV2 * 32), ("conv_b", 2 * 32), ("b_gate", 2 * 16),
    ("d_skip", 2 * 16), ("ssd_norm", 2 * 16), ("q_norm", 2), ("k_norm", 2), ("dt_bias", 2), ("a_log", 2),
    ("w_dt", 2 * KD * 32), ("sinks", 2 * 16),
]
CONSTS = [
    ("ident", P), ("ones", P), ("whole_col", 2 * 16 - 1), ("half_cols", 2 * 20 - 2), ("swap", P), ("dilated", 2 * SEQ), 
    ("window", 3 * L2), ("cos", L2), ("sin", L2), ("levels", DELTA_LEVELS * P), ("below", P), ("iota", 8),
]


def offsets(spec):
    at, out = 0, {}
    for name, n in spec:
        out[name] = (at, n)
        at += n
    return out, at


class Counted:

    def __init__(self, sem):
        self.sem, self.base = sem, 0

    def at(self, n):
        return self.base + n

    def close(self, n):
        self.base += n


class Steps:

    def __init__(self, sem):
        self.sem, self.count = sem, 0

    def link(self, eng, ins):
        self.count += 1
        ins.then_inc(self.sem, 1)
        eng.wait_ge(self.sem, self.count)


class Program:
    def __init__(self, nc, ctx, block, upto):
        self.nc, self.ctx, self.block, self.upto = nc, ctx, block, upto
        self.counts = {}
        self.plan, self.order, self.n_slots = plan_stream()
        end = self.order[-1]
        if end.iters > 1:
            self.plan[end.name] = self.order[-1:] = list(split_segment(end, end.iters - 1))
            self.plan[end.name][1].unit0 = (end.iters - 1) * len(end.units)
        self.stage_done = self.sem("stage_done")
        self.stages = 0
        self.part_done = self.sem("part_done")
        self.rounded = self.sem("slot_rounded")
        self.split = self.sem("slot_split")
        self.unit_free = self.sem("unit_free")
        self.full = [self.sem(f"slot_full{s}") for s in range(RING)]
        self.loaded = self.sem("inputs_loaded")
        self.stored = self.sem("output_stored")
        self.act_steps = Steps(self.sem("act_step"))
        self.dve_steps = Steps(self.sem("dve_step"))
        sb = lambda name, shape, dt=F32: ctx.enter_context(nc.sbuf_tensor(name, shape, dt))
        self.ring = sb("ring", [P, RING, SLOT])
        self.par_at, n_par = offsets(PARAMS)
        self.con_at, n_con = offsets(CONSTS)
        self.params = sb("params", [P, n_par])
        self.consts = sb("consts", [P, n_con])
        self.h = sb("h", [P, KD, L2])
        self.high = sb("act_high", [P, KD, L2], F32R)
        self.low = sb("act_low", [P, KD, L2], F32R)
        self.w_high = sb("w_high", [P, SPLITS, SLOT], F32R)
        self.w_low = sb("w_low", [P, SPLITS, SLOT], F32R)
        self.u = sb("u", [P, KD, L2])
        self.work = self.u[:].rearrange("p k t -> p (k t)")
        self.rstd = sb("rstd", [P, L2])
        self.arena_cols = 21600
        self.arena = sb("arena", [P, self.arena_cols])
        self.arena_r = nc.alloc_sbuf_tensor_at("arena_r", [P, self.arena_cols], F32R, offset=nc.lookup_mloc(self.arena).addr)
        self.indices = sb("indices", [P, 2, 8], U32)
        self.ps = ctx.enter_context(nc.psum_tensor("ps", [P, 8, 512], F32))

    def sem(self, name):
        return self.ctx.enter_context(self.nc.semaphore(name))

    def counted(self, name):
        if name not in self.counts:
            self.counts[name] = Counted(self.sem(name))
        return self.counts[name]

    def par(self, name, first=0, n=1):
        at = self.par_at[name][0] + first
        return self.params[:, at:at + n]

    def par_dyn(self, name, first):
        return self.params[:, bass.ds(self.par_at[name][0] + first, 1)]

    def con(self, name, first=0, n=None, rows=P):
        at, size = self.con_at[name]
        return self.consts[0:rows, at + first:at + first + (size if n is None else n)]

    def head_cols(self, heads, chunk, rows):
        if heads == 1:
            return self.con("whole_col", 15 - chunk, rows)
        return self.con("half_cols", 18 - 2 * chunk, rows)

    def area(self, at, *dims):
        n = int(np.prod(dims))
        assert at + n <= self.arena_cols, (at, n)
        v = self.arena[:, at:at + n]
        if len(dims) == 2:
            v = v.rearrange("p (a b) -> p a b", b=dims[1])
        elif len(dims) == 3:
            v = v.rearrange("p (a b c) -> p a b c", b=dims[1], c=dims[2])
        return v, at + n

    def split_area(self, at, n, T):
        assert at + 2 * n * T <= self.arena_cols
        v = [self.arena_r[:, at + i * n * T:at + (i + 1) * n * T].rearrange("p (k t) -> p k t", t=T) for i in range(2)]
        return v, at + 2 * n * T

    def stage_end(self):
        self.stages += 1
        goal = 3 * self.stages
        for start in (self.block.tensor, self.block.scalar, self.block.vector):
            @start
            def _(eng):
                eng.drain().then_inc(self.stage_done, 1)
                eng.wait_ge(self.stage_done, goal)


def repeat(eng, n, body):
    if n == 1:
        body(0)
    else:
        with eng.Fori(0, n) as i:
            body(i)


def at_dyn(view, first, n, size=None):
    return view[:, first:first + n] if isinstance(first, int) else view[:, bass.ds(first, n)]


def is_register(i):
    return not isinstance(i, int)


def round_slot(p, act, seg, j, i):
    s = seg.ring[j]
    cols = seg.split_cols[j]
    act.wait_ge(p.full[s], i * seg.full_step[j] + seg.full0[j])
    if seg.split_free0[j] > 0:
        act.wait_ge(p.part_done, i * seg.parts + seg.split_free0[j])
    act.activation(p.w_high[:, s % SPLITS, 0:cols], p.ring[:, s, 0:cols], ACT.Copy).then_inc(p.rounded, 1)


def rest_slot(p, dve, seg, j, i):
    s = seg.ring[j]
    cols = seg.split_cols[j]
    dve.wait_ge(p.rounded, i * len(seg.slots) + (seg.slot_base + j + 1))
    dve.tensor_tensor(p.w_low[:, s % SPLITS, 0:cols], p.ring[:, s, 0:cols], p.w_high[:, s % SPLITS, 0:cols].bitcast(F32),
                      ALU.subtract).then_inc(p.split, 1)


def next_slot(seg, j, i):
    if j + 1 < len(seg.slots):
        return seg, j + 1, i
    if seg.iters > 1:
        return seg, 0, i + 1
    return None if seg.after is None else (seg.after, 0, 0)


def same_buffers(seg, j, after):
    several = len(seg.slots) == 1 and seg.parts > 1
    return several or seg.ring[j] % SPLITS == after[0].ring[after[1]] % SPLITS


def gemm(p, name, xs, T, act_unit=None, dve_unit=None, signals=(), pair=lambda j: j % 2, before=None,
         act_late=None):
    for seg in p.plan[name]:
        nu = len(seg.units)

        @p.block.tensor
        def _(pe):
            def body(i):
                for j, unit in enumerate(seg.units):
                    number = seg.unit_base + j + 1
                    if number > 2:
                        pe.wait_ge(p.unit_free, i * nu + (number - 2))
                    if before is not None:
                        before(pe, i, j)
                    used = sorted({c[0] for chunk in unit for c in chunk})
                    for s in used:
                        b = seg.ring[s] % SPLITS
                        number = i * len(seg.slots) + (seg.slot_base + s + 1)
                        if s in seg.first_used[j]:
                            pe.wait_ge(p.rounded, number)
                        for w, parts in ((p.w_high, (0, 1)), (p.w_low, (0,))):
                            if w is p.w_low and s in seg.first_used[j]:
                                pe.wait_ge(p.split, number)
                            for c, chunk in enumerate(unit):
                                for n, (slot, k, col, xk, which) in enumerate(chunk):
                                    if slot != s:
                                        continue
                                    for x in parts:
                                        mm = pe.matmul(p.ps[:, 2 * pair(j) + c, 0:T], w[:, b, col:col + P], xs[which][x][:, xk, 0:T],
                                                       start=(n == 0 and w is p.w_high and x == 0),
                                                       stop=(n == len(chunk) - 1 and w is p.w_low))
                        mm.then_inc(p.part_done, 1)
            repeat(pe, seg.iters, body)

        for unit_fn, split_fn, start in ((act_unit, round_slot, p.block.scalar), (dve_unit, rest_slot, p.block.vector)):
            @start
            def _(eng):
                def body(i):
                    for j, unit in enumerate(seg.units):
                        for s in seg.first_used[j]:
                            after = next_slot(seg, s, i)
                            if after is not None and not same_buffers(seg, s, after):
                                split_fn(p, eng, *after)
                        late = act_late if split_fn is round_slot else None
                        if late is not None and j > 0:
                            late(eng, i * nu + (seg.unit0 + j - 1), j - 1)
                        if unit_fn is not None:
                            eng.wait_ge(p.part_done, i * seg.parts + (seg.part_base + seg.part_end[j]))
                            unit_fn(eng, i, i * nu + (seg.unit0 + j), j, p.ps[:, 2 * pair(j):2 * pair(j) + len(unit), 0:T])
                        for s in range(len(seg.slots)):
                            after = next_slot(seg, s, i)
                            if seg.last_part[s] == seg.part_end[j] and after is not None and same_buffers(seg, s, after):
                                split_fn(p, eng, *after)
                    if late is not None:
                        late(eng, i * nu + (seg.unit0 + nu - 1), nu - 1)
                repeat(eng, seg.iters, body)
    for name, n in signals:
        p.counted(name).close(n)


def take_copy(p, dst, T, per=2, func=ACT.Copy):
    def unit(act, i, u, j, bank):
        act.activation(at_dyn(dst, per * u, per)[:, :, 0:T], bank, func).then_inc(p.unit_free, 1)
    return unit


def take_add(p, dst, T, per):
    def unit(dve, i, u, j, bank):
        out = at_dyn(dst, per * u, per)[:, :, 0:T]
        dve.tensor_tensor(out, bank, out, ALU.add).then_inc(p.unit_free, 1)
    return unit


def split_activations(p, src, n, T, dst=None):
    high, low = dst or (p.high[:, 0:n, 0:T], p.low[:, 0:n, 0:T])
    done = p.counted("high_ready")

    @p.block.scalar
    def _(act):
        for k in range(0, n, 4):
            m = min(4, n - k)
            act.activation(high[:, k:k + m], src[:, k:k + m], ACT.Copy).then_inc(done.sem, 1)

    @p.block.vector
    def _(dve):
        for c, k in enumerate(range(0, n, 4)):
            m = min(4, n - k)
            dve.wait_ge(done.sem, done.at(c + 1))
            dve.tensor_tensor(low[:, k:k + m], src[:, k:k + m], high[:, k:k + m].bitcast(F32), ALU.subtract)

    done.close(-(-n // 4))
    p.stage_end()
    return [(high, low)]


def norm(p, src, gain, gain0, T):
    sq = p.u[:, :, 0:T]
    half = KD // 2
    squares, sums, means, roots = (p.counted(n) for n in ("squares_ready", "sums_ready", "means_ready", "roots_ready"))
    normed, high = p.counted("normed"), p.counted("high_ready")

    @p.block.scalar
    def _(act):
        act.activation(sq[:, 0:half], src[:, 0:half, 0:T], ACT.Square).then_inc(squares.sem, 1)
        act.wait_ge(means.sem, means.at(1))
        act.activation(p.rstd[:, 0:T], p.rstd[:, 0:T], ACT.Sqrt).then_inc(roots.sem, 1)
        for c in range(2):
            act.wait_ge(normed.sem, normed.at(c + 1))
            act.activation(p.high[:, c * half:(c + 1) * half, 0:T], p.u[:, c * half:(c + 1) * half, 0:T], ACT.Copy).then_inc(high.sem, 1)

    @p.block.tensor
    def _(pe):
        pe.wait_ge(squares.sem, squares.at(2))
        for k in range(KD):
            mm = pe.matmul(p.ps[:, 7, 0:T], p.con("ones"), sq[:, k], start=(k == 0), stop=(k == KD - 1))
        mm.then_inc(sums.sem, 1)

    @p.block.vector
    def _(dve):
        dve.tensor_tensor(sq[:, half:], src[:, half:KD, 0:T], src[:, half:KD, 0:T], ALU.mult).then_inc(squares.sem, 1)
        dve.wait_ge(sums.sem, sums.at(1))
        dve.tensor_scalar(p.rstd[:, 0:T], p.ps[:, 7, 0:T], 1.0 / D, EPS, ALU.mult, ALU.add).then_inc(means.sem, 1)
        dve.wait_ge(roots.sem, roots.at(1))
        p.dve_steps.link(dve, dve.reciprocal(p.rstd[:, 0:T], p.rstd[:, 0:T]))
        for k in range(KD):
            ins = dve.scalar_tensor_tensor(p.u[:, k, 0:T], src[:, k, 0:T], p.par(gain, gain0 + k), p.rstd[:, 0:T], ALU.mult, ALU.mult)
            if k % half == half - 1:
                ins.then_inc(normed.sem, 1)
        for c in range(2):
            dve.wait_ge(high.sem, high.at(c + 1))
            ks = slice(c * half, (c + 1) * half)
            dve.tensor_tensor(p.low[:, ks, 0:T], p.u[:, ks, 0:T], p.high[:, ks, 0:T].bitcast(F32), ALU.subtract)

    for s, n in ((squares, 2), (sums, 1), (means, 1), (roots, 1), (normed, 2), (high, 2)):
        s.close(n)
    p.stage_end()
    return [(p.high, p.low)]


def head_norm(p, x, gains, T, heads, scale, eps, group=1):
    n = len(gains)
    ng = n // group
    rows = ng * heads
    sq = p.work[:, 0:8 * T].rearrange("p (k t) -> p k t", t=T)
    pieces = [(c, min(4, n - c)) for c in range(0, n, 4)]
    squares, sums, means, roots, inverse, spread, scaled = (p.counted(s) for s in (
        "squares_ready", "sums_ready", "means_ready", "roots_ready", "inverse_ready", "spread_ready", "heads_scaled"))
    rstd = p.rstd[0:rows, 0:T]
    picks = p.work[0:rows, 0:rows * P // 2]

    @p.block.scalar
    def _(act):
        for b, (c, m) in enumerate(pieces):
            if b >= 2:
                act.wait_ge(sums.sem, sums.at(b - 1))
            act.activation(sq[:, 4 * (b % 2):4 * (b % 2) + m], x[:, c:c + m], ACT.Square).then_inc(squares.sem, 1)
        act.wait_ge(means.sem, means.at(1))
        act.activation(rstd, rstd, ACT.Sqrt).then_inc(roots.sem, 1)

    @p.block.tensor
    def _(pe):
        for b, (c0, m) in enumerate(pieces):
            pe.wait_ge(squares.sem, squares.at(b + 1))
            for c in range(c0, c0 + m):
                first = p.head_cols(heads, c // group, rows)
                mm = pe.matmul(p.ps[0:rows, 7, 0:T], first, sq[:, 4 * (b % 2) + c - c0], start=(c == 0), stop=(c == n - 1))
            mm.then_inc(sums.sem, 1)
        pe.wait_ge(inverse.sem, inverse.at(1))
        for g in range(ng):
            if g >= 7:
                pe.wait_ge(scaled.sem, scaled.at(g - 6))
            if heads == 2:
                pick = picks[:, g * P:(g + 1) * P]
            else:
                pick = p.con("ident", first=g, n=1, rows=rows).to_broadcast([rows, P])
            pe.matmul(p.ps[:, g % 7, 0:T], pick, rstd, start=True, stop=True).then_inc(spread.sem, 1)

    @p.block.vector
    def _(dve):
        dve.wait_ge(sums.sem, sums.at(len(pieces)))
        dve.tensor_scalar(rstd, p.ps[0:rows, 7, 0:T], scale, eps, ALU.mult, ALU.add).then_inc(means.sem, 1)
        if heads == 2:
            dve.tensor_copy(picks.rearrange("r (c m) -> r c m", m=P // 2), p.con("ident", n=rows, rows=rows)[:, :, None].to_broadcast([rows, rows, P // 2]))
        dve.wait_ge(roots.sem, roots.at(1))
        dve.reciprocal(rstd, rstd).then_inc(inverse.sem, 1)
        for g in range(ng):
            dve.wait_ge(spread.sem, spread.at(g + 1))
            for c in range(g * group, (g + 1) * group):
                ins = dve.scalar_tensor_tensor(x[:, c], x[:, c], gains[c], p.ps[:, g % 7, 0:T], ALU.mult, ALU.mult)
            ins.then_inc(scaled.sem, 1)

    for s, k in ((squares, len(pieces)), (sums, len(pieces)), (means, 1), (roots, 1), (inverse, 1), (spread, ng), (scaled, ng)):
        s.close(k)
    p.stage_end()


def to_tokens(p, src, n_chunks, tiles, dst, T):
    groups = [(i, o, n, c, min(4, n_chunks - c)) for i, (o, n) in enumerate(tiles) for c in range(0, n_chunks, 4)]
    turned, moved = p.counted("turned"), p.counted("moved")

    @p.block.tensor
    def _(pe):
        for g, (i, o, n, c0, m) in enumerate(groups):
            if g >= 4:
                pe.wait_ge(moved.sem, moved.at(g - 3))
            for c in range(m):
                mm = pe.transpose(p.ps[0:n, 4 + g % 4, c * P:(c + 1) * P], src[:, c0 + c, o:o + n], p.con("ident"))
            mm.then_inc(turned.sem, 1)

    @p.block.scalar
    def _(act):
        for g, (i, o, n, c0, m) in enumerate(groups):
            act.wait_ge(turned.sem, turned.at(g + 1))
            act.activation(dst[0:n, i, c0 * P:(c0 + m) * P], p.ps[0:n, 4 + g % 4, 0:m * P], ACT.Copy).then_inc(moved.sem, 1)

    turned.close(len(groups))
    moved.close(len(groups))
    p.stage_end()


def from_tokens(p, src, dst, tiles):
    groups = [(i, o, n, c) for i, (o, n) in enumerate(tiles) for c in (0, 4)]
    turned, moved = p.counted("turned"), p.counted("moved")

    @p.block.tensor
    def _(pe):
        pe.wait_ge(p.loaded, p.n_loads)
        for g, (i, o, n, c0) in enumerate(groups):
            if g >= 4:
                pe.wait_ge(moved.sem, moved.at(g - 3))
            for c in range(4):
                mm = pe.transpose(p.ps[:, 4 + g % 4, c * P:c * P + n], src[0:n, i, (c0 + c) * P:(c0 + c + 1) * P],
                                  p.con("ident", n=n, rows=n))
            mm.then_inc(turned.sem, 1)

    @p.block.scalar
    def _(act):
        for g, (i, o, n, c0) in enumerate(groups):
            act.wait_ge(turned.sem, turned.at(g + 1))
            bank = p.ps[:, 4 + g % 4, :].rearrange("p (c t) -> p c t", t=P)
            act.activation(dst[:, c0:c0 + 4, o:o + n], bank[:, :, 0:n], ACT.Copy).then_inc(moved.sem, 1)

    turned.close(len(groups))
    moved.close(len(groups))
    p.stage_end()


def attention(p, items, scale, at):
    masked, at = p.area(at, 3, L2)
    probs, at = p.area(at, 4, L2)
    turned_p, at = p.area(at, 3, 3, P)
    small, at = p.area(at, 4, 8)
    names = ("scores_ready", "masked_ready", "exp_ready", "probs_ready", "probs_turned", "turned_ready", "heads_ready", "heads_moved")
    scores, mask_ok, exp_ok, prob_ok, turn_ok, tcopy_ok, head_ok, moved = (p.counted(n) for n in names)
    N = len(items)

    @p.block.tensor
    def _(pe):
        def do_scores(i):
            t = items[i]
            if i >= 3:
                pe.wait_ge(mask_ok.sem, mask_ok.at(i - 2))
            pe.matmul(p.ps[0:t["nq"], i % 3, 0:t["nk"]], t["q"], t["k"], start=True, stop=True).then_inc(scores.sem, 1)

        def do_turn(i):
            t = items[i]
            pe.wait_ge(prob_ok.sem, prob_ok.at(i + 1))
            if i >= 3:
                pe.wait_ge(tcopy_ok.sem, tcopy_ok.at(i - 2))
            for n, (o, rows) in enumerate(t["tiles"]):
                mm = pe.transpose(p.ps[0:rows, 3 + i % 3, n * P:n * P + t["nq"]], probs[0:t["nq"], i % 4, o:o + rows],
                                  p.con("ident", n=t["nq"], rows=t["nq"]))
            mm.then_inc(turn_ok.sem, 1)

        def do_heads(i):
            t = items[i]
            pe.wait_ge(tcopy_ok.sem, tcopy_ok.at(i + 1))
            if i >= 2:
                pe.wait_ge(moved.sem, moved.at(i - 1))
            for n, (o, rows) in enumerate(t["tiles"]):
                mm = pe.matmul(p.ps[t["part"]:t["part"] + 64, 6 + i % 2, 0:t["nq"]], t["v"][n], turned_p[0:rows, i % 3, n, 0:t["nq"]],
                               start=(n == 0), stop=(n == len(t["tiles"]) - 1))
            mm.then_inc(head_ok.sem, 1)

        for i in range(N + 4):
            if i < N:
                do_scores(i)
            if 3 <= i < N + 3:
                do_turn(i - 3)
            if i >= 4:
                do_heads(i - 4)

    @p.block.vector
    def _(dve):
        def do_mask(i):
            t = items[i]
            nq, nk = t["nq"], t["nk"]
            dve.wait_ge(scores.sem, scores.at(i + 1))
            if i >= 3:
                dve.wait_ge(exp_ok.sem, exp_ok.at(i - 2))
            m, sm = masked[0:nq, i % 3, 0:nk], small[0:nq, i % 4]
            if t["mask"] is None:
                p.dve_steps.link(dve, dve.tensor_scalar(m, p.ps[0:nq, i % 3, 0:nk], scale, None, ALU.mult))
            else:
                p.dve_steps.link(dve, dve.scalar_tensor_tensor(m, p.ps[0:nq, i % 3, 0:nk], scale, t["mask"], ALU.mult, ALU.add))
            p.dve_steps.link(dve, dve.tensor_reduce(sm[:, 0:1], m, AX_X, ALU.max))
            other = t["sink"] if t["sink"] is not None else sm[:, 0:1]
            dve.tensor_scalar(sm[:, 1:2], sm[:, 0:1], other, -1.0, ALU.max, ALU.mult).then_inc(mask_ok.sem, 1)

        def do_divide(i):
            t = items[i]
            nq, nk = t["nq"], t["nk"]
            sm = small[0:nq, i % 4]
            dve.wait_ge(exp_ok.sem, exp_ok.at(i + 1))
            if t["sink"] is not None:
                p.dve_steps.link(dve, dve.tensor_tensor(sm[:, 2:3], sm[:, 2:3], sm[:, 3:4], ALU.add))
            p.dve_steps.link(dve, dve.reciprocal(sm[:, 4:5], sm[:, 2:3]))
            dve.tensor_scalar(probs[0:nq, i % 4, 0:nk], probs[0:nq, i % 4, 0:nk], sm[:, 4:5], None, ALU.mult).then_inc(prob_ok.sem, 1)

        for i in range(N + 2):
            if i < N:
                do_mask(i)
            if i >= 2:
                do_divide(i - 2)

    @p.block.scalar
    def _(act):
        def do_exp(i):
            t = items[i]
            nq, nk = t["nq"], t["nk"]
            sm = small[0:nq, i % 4]
            act.wait_ge(mask_ok.sem, mask_ok.at(i + 1))
            if i >= 4:
                act.wait_ge(turn_ok.sem, turn_ok.at(i - 3))
            if t["sink"] is not None:
                p.act_steps.link(act, act.activation(sm[:, 3:4], t["sink"], ACT.Exp, bias=sm[:, 1:2]))
            act.activation(probs[0:nq, i % 4, 0:nk], masked[0:nq, i % 3, 0:nk], ACT.Exp, bias=sm[:, 1:2],
                           accum_out=sm[:, 2:3]).then_inc(exp_ok.sem, 1)

        def do_copy(i):
            t = items[i]
            act.wait_ge(turn_ok.sem, turn_ok.at(i + 1))
            if i >= 3:
                act.wait_ge(head_ok.sem, head_ok.at(i - 2))
            bank = p.ps[:, 3 + i % 3, 0:3 * P].rearrange("p (n t) -> p n t", t=P)
            runs, n = [], 0
            while n < len(t["tiles"]):
                m = n + 1
                while m < len(t["tiles"]) and t["tiles"][m][1] == t["tiles"][n][1]:
                    m += 1
                runs.append((n, m, t["tiles"][n][1]))
                n = m
            for r, (n, m, rows) in enumerate(runs):
                ins = act.activation(turned_p[0:rows, i % 3, n:m, 0:t["nq"]], bank[0:rows, n:m, 0:t["nq"]], ACT.Copy)
                if r == len(runs) - 1:
                    ins.then_inc(tcopy_ok.sem, 1)

        def do_out(i):
            t = items[i]
            act.wait_ge(head_ok.sem, head_ok.at(i + 1))
            act.activation(t["out"], p.ps[t["part"]:t["part"] + 64, 6 + i % 2, 0:t["nq"]], ACT.Copy).then_inc(moved.sem, 1)

        for i in range(N + 4):
            if i < N:
                do_exp(i)
            if 3 <= i < N + 3:
                do_copy(i - 3)
            if i >= 4:
                do_out(i - 4)

    for s in (scores, mask_ok, exp_ok, prob_ok, turn_ok, tcopy_ok, head_ok, moved):
        s.close(N)
    p.stage_end()


TILES1 = ((0, 128), (128, 128))


def heads_256(q, k, v_tok, heads, mask, out, out0):
    items = []
    for h in range(heads):
        lo = 64 * (h % 2)
        for qt in range(2):
            items.append(dict(
                nq=P, nk=SEQ, tiles=TILES1, part=lo, sink=None, mask=None if mask is None else mask[:, qt * SEQ:(qt + 1) * SEQ],
                q=q[lo:lo + 64, h // 2, qt * P:(qt + 1) * P], k=k[lo:lo + 64, h // 2, 0:SEQ],
                v=[v_tok[:, n, 64 * h:64 * h + 64] for n in range(2)],
                out=out[lo:lo + 64, out0 + h // 2, qt * P:(qt + 1) * P]))
    return items


def layer_even(p):
    T = SEQ
    proj, at = p.area(p.a0, 24, T)
    padded, at = p.area(at, 4, T + A_CONV - 1)
    cat, at = p.area(at, 8, T)
    v_tok, at = p.area(at, 2, 512)
    x = norm(p, p.h, "norm_mix", 0, T)
    gemm(p, "ev_in", x, T, act_unit=take_copy(p, proj, T))
    p.stage_end()
    gb, gc, xc, q, k, v = (proj[:, 4 * i:4 * i + 4] for i in range(6))

    @p.block.vector
    def _(dve):
        dve.memset(padded[:, :, 0:A_CONV - 1], 0.0)
        p.dve_steps.link(dve, dve.tensor_tensor(padded[:, :, A_CONV - 1:], gc, xc, ALU.mult))
        for c in range(4):
            w = lambda j: p.par("ev_conv", j * 4 + c)
            p.dve_steps.link(dve, dve.tensor_scalar(cat[:, c], padded[:, c, 0:T], w(0), None, ALU.mult))
            for j in range(1, A_CONV):
                p.dve_steps.link(dve, dve.scalar_tensor_tensor(cat[:, c], padded[:, c, j:j + T], w(j), cat[:, c], ALU.mult, ALU.add))
        dve.tensor_tensor(cat[:, 0:4], cat[:, 0:4], gb, ALU.mult)

    head_norm(p, proj[:, 12:20], [p.par("ev_q_norm")] * 4 + [p.par("ev_k_norm")] * 4, T, 2, 1.0 / B_DIM, EPS)
    to_tokens(p, v, 4, TILES1, v_tok, T)
    attention(p, heads_256(q, k, v_tok, B_HEADS, p.con("dilated"), cat, 4), B_DIM ** -0.5, at)
    x = split_activations(p, cat, 8, T)
    gemm(p, "ev_out", x, T, dve_unit=take_add(p, p.h, T, 2))
    p.stage_end()


def memory_heads(p, layer):
    T = SEQ
    kv, at = p.area(p.a0, 4, T)
    x = norm(p, p.mem, "norm_mem", KD * layer, T)
    gemm(p, f"xa_kv{layer}", x, T, act_unit=take_copy(p, kv, T))
    p.stage_end()
    k = p.mem_k[:, 2 * layer:2 * layer + 2]

    @p.block.scalar
    def _(act):
        p.act_steps.link(act, act.activation(k, kv[:, 0:2], ACT.Copy))

    head_norm(p, k, [p.par("xa_k_norm", layer)] * 2, T, 2, 1.0 / 64, EPS)
    to_tokens(p, kv[:, 2:4], 2, TILES1, p.mem_v[:, 2 * layer:2 * layer + 2], T)


def cross_attention(p, layer):
    T = SEQ
    q, at = p.area(p.a0, 2, T)
    o, at = p.area(at, 2, T)
    x = norm(p, p.h, "norm_xattn", KD * layer, T)
    gemm(p, f"xa_q{layer}", x, T, act_unit=take_copy(p, q, T))
    p.stage_end()
    head_norm(p, q, [p.par("xa_q_norm", layer)] * 2, T, 2, 1.0 / 64, EPS)
    items = heads_256(q, p.mem_k[:, 2 * layer:2 * layer + 2], p.mem_v[:, 2 * layer:2 * layer + 2], X_HEADS,
                      None, o, 0)
    attention(p, items, 64 ** -0.5, at)
    x = split_activations(p, o, 2, T)
    gemm(p, f"xa_o{layer}", x, T, dve_unit=take_add(p, p.h, T, 2))
    p.stage_end()


def gated_hidden(p, hidden, silu, prod, kt, weight=None):
    T = SEQ
    gated, product, high = p.counted("gate_ready"), p.counted("product_ready"), p.counted("high_ready")
    up = p.counted("up_ready")

    def act_unit(act, i, u, j, bank):
        if j >= kt:
            return
        act.activation(silu[:, j % 2], bank[:, 0], ACT.Silu).then_inc(gated.sem, 1)
        act.wait_ge(product.sem, u + product.at(1))
        act.activation(chunk(0, u, j), prod[:, j % 2], ACT.Copy).then_inc(high.sem, 1)

    def chunk(part, u, j):
        return (at_dyn(hidden[part], u, 1) if weight is None else hidden[part][:, j:j + 1])[:, 0]

    def dve_unit(dve, i, u, j, bank):
        top = bank[:, 1]
        if weight is not None:
            dve.tensor_tensor(prod[:, j % 2], top, at_dyn(weight, i, 1)[:, 0], ALU.mult).then_inc(up.sem, 1)
            dve.wait_ge(up.sem, u + up.at(1))
            top = prod[:, j % 2]
        dve.wait_ge(gated.sem, u + gated.at(1))
        dve.tensor_tensor(prod[:, j % 2], silu[:, j % 2], top, ALU.mult).then_inc(product.sem, 1)
        dve.wait_ge(high.sem, u + high.at(1))
        dve.tensor_tensor(chunk(1, u, j), prod[:, j % 2], chunk(0, u, j).bitcast(F32), ALU.subtract).then_inc(p.unit_free, 1)

    return act_unit, dve_unit


def dense_ffn(p):
    T, kt = SEQ, D_FF // P
    hidden, at = p.split_area(p.a0, kt, T)
    silu, at = p.area(at, 2, T)
    prod, at = p.area(at, 2, T)
    x = norm(p, p.h, "norm_ffn", 0, T)
    act_unit, dve_unit = gated_hidden(p, hidden, silu, prod, kt)
    gemm(p, "ff_gu", x, T, act_unit, dve_unit, [("gate_ready", kt), ("product_ready", kt), ("high_ready", kt)])
    p.stage_end()
    gemm(p, "ff_down", [hidden], T, dve_unit=take_add(p, p.h, T, 1))
    p.stage_end()


def conv_silu(p, name, dst, T, weights, w0, n_chunks, bias, b0, units, at):
    padded, at = p.area(at, 4, T + 3)
    acc, at = p.area(at, 4, T)
    step = p.counted("conv_step")
    unit_base = p.plan[name][0].unit_base

    @p.block.vector
    def _(dve):
        p.dve_steps.link(dve, dve.memset(padded[:, :, 0:3], 0.0))

    def act_unit(act, i, u, j, bank):
        b = 2 * (j % 2)
        act.activation(padded[:, b:b + 2, 3:3 + T], bank, ACT.Copy)
        for c in range(2):
            w = p.par_dyn(weights, 2 * u + (w0 + 3 * n_chunks + c))
            if bias is None:
                ins = act.activation(acc[:, b + c], bank[:, c], ACT.Copy, scale=w)
            else:
                ins = act.activation(acc[:, b + c], bank[:, c], ACT.Identity, scale=w, bias=p.par_dyn(bias, 2 * u + (b0 + c)))
        ins.then_inc(p.unit_free, 1)

    def act_late(act, u, j):
        b = 2 * (j % 2)
        act.wait_ge(step.sem, 6 * u + step.at(6))
        act.activation(at_dyn(dst, 2 * u, 2)[:, :, 0:T], acc[:, b:b + 2], ACT.Silu)

    def dve_unit(dve, i, u, j, bank):
        b = 2 * (j % 2)
        dve.wait_ge(p.unit_free, u + (unit_base + 1))
        for t in range(3):
            for c in range(2):
                if t:
                    dve.wait_ge(step.sem, 6 * u + step.at(2 * t + c - 1))
                w = p.par_dyn(weights, 2 * u + (w0 + t * n_chunks + c))
                dve.scalar_tensor_tensor(acc[:, b + c], padded[:, b + c, t:t + T], w, acc[:, b + c], ALU.mult, ALU.add).then_inc(step.sem, 1)

    return dict(act_unit=act_unit, dve_unit=dve_unit, signals=[("conv_step", 6 * units)], act_late=act_late)


def layer_odd(p):
    T, H = SEQ, C_HEADS
    qkv, at = p.area(p.a0, 24, T)
    x = norm(p, p.h, "norm_mix", KD, T)
    rows, at = p.area(at, 8, T)
    top = at
    small_ok = p.counted("small_ready")
    beta, gcum, *t = (rows[0:H, i] for i in range(7))
    na = rows[0:H, 7, 0:1]

    @p.block.tensor
    def _(pe):
        for s in range(2):
            for k in range(KD):
                mm = pe.matmul(p.ps[0:H, 6 + s, 0:T], p.par("od_small", 16 * k + 8 * s, 8), p.u[:, k, 0:T], start=(k == 0), stop=(k == KD - 1))
        mm.then_inc(small_ok.sem, 1)

    softplus_rows(p, p.ps[0:H, 7, 0:T], p.par("od_dt_bias")[0:H], p.par("od_a_log")[0:H], t, na,
                  also=(beta, p.ps[0:H, 6, 0:T]))

    @p.block.vector
    def _(dve):
        p.dve_steps.link(dve, dve.tensor_scalar(t[0], t[1], na, -1.0, ALU.mult, ALU.mult))
        for c in range(2):
            s = slice(c * DELTA_CHUNK, (c + 1) * DELTA_CHUNK)
            dve.tensor_tensor_scan(gcum[:, s], t[0][:, s], t[0][:, s], 0.0, ALU.add, ALU.bypass)

    p.stage_end()
    conv = conv_silu(p, "od_in", qkv, T, "od_conv", 0, 24, None, 0, 12, top)
    segs = p.plan["od_in"]
    p.plan["od_qkv"], p.plan["od_gate"] = ([s] for s in split_segment(segs[0], 3))
    gemm(p, "od_qkv", x, T, **conv)
    p.stage_end()
    q, k, v = qkv[:, 0:8], qkv[:, 8:16], qkv[:, 16:24]
    head_norm(p, qkv[:, 0:16], [C_DIM ** -0.5] * 8 + [1.0] * 8, T, 1, 1.0, EPS)
    out, at = p.area(top, 8, T)
    state, at = p.area(at, 8, C_DIM)
    cols, at = p.area(at, 2, 5, H)
    keep = at
    for c in range(2):
        delta_chunk(p, c, q, k, v, beta, gcum, out, cols[:, c], state, keep)
    head_norm(p, out, [p.par("od_o_norm")] * 8, T, 1, 1.0 / C_DIM, EPS)
    gate, _ = p.area(keep, 8, T)
    gemm(p, "od_gate", x, T, act_unit=take_copy(p, gate, T, func=ACT.Silu))
    p.stage_end()

    @p.block.vector
    def _(dve):
        dve.tensor_tensor(out, out, gate, ALU.mult)

    p.stage_end()
    x = split_activations(p, out, 8, T)
    gemm(p, "od_out", x, T, dve_unit=take_add(p, p.h, T, 2))
    p.stage_end()


def softplus_rows(p, bank, bias, a_log, t, na, also=None):
    ready, args, tables = p.counted("small_ready"), p.counted("softplus_arg_ready"), p.counted("softplus_table_ready")

    @p.block.vector
    def _(dve):
        link = p.dve_steps.link
        dve.wait_ge(ready.sem, ready.at(1))
        link(dve, dve.tensor_scalar(t[0], bank, bias, None, ALU.add))
        link(dve, dve.tensor_scalar(t[1], t[0], -1.0, None, ALU.mult))
        dve.tensor_tensor(t[1], t[0], t[1], ALU.min).then_inc(args.sem, 1)
        dve.wait_ge(tables.sem, tables.at(1))
        dve.tensor_scalar(t[2], t[1], 1.0, None, ALU.add).then_inc(args.sem, 1)
        dve.wait_ge(tables.sem, tables.at(2))
        link(dve, dve.scalar_tensor_tensor(t[4], t[2], -1.0, t[1], ALU.add, ALU.subtract))
        link(dve, dve.reciprocal(t[2], t[2]))
        link(dve, dve.tensor_tensor(t[4], t[4], t[2], ALU.mult))
        link(dve, dve.tensor_tensor(t[3], t[3], t[4], ALU.subtract))
        link(dve, dve.scalar_tensor_tensor(t[1], t[0], 0.0, t[3], ALU.max, ALU.add))

    @p.block.scalar
    def _(act):
        act.wait_ge(ready.sem, ready.at(1))
        if also is not None:
            act.activation(also[0], also[1], ACT.Sigmoid)
        act.activation(na, a_log, ACT.Exp)
        act.wait_ge(args.sem, args.at(1))
        act.activation(t[1], t[1], ACT.Exp).then_inc(tables.sem, 1)
        act.wait_ge(args.sem, args.at(2))
        act.activation(t[3], t[2], ACT.Ln).then_inc(tables.sem, 1)

    ready.close(1)
    args.close(2)
    tables.close(2)


def delta_chunk(p, c, q, k, v, beta, gcum, out, cols, state, at):
    H, n = C_HEADS, DELTA_CHUNK
    tok = slice(c * n, (c + 1) * n)
    big = lambda a: p.area(a, H, n)
    R, at = big(at)
    DT, at = big(at)
    X, at = big(at)
    Tm, at = big(at)
    Um, at = big(at)
    NT, at = big(at)
    CT, at = big(at)
    S = state[:, :, 0:C_DIM]
    banks = lambda b, m=2: p.ps[:, b:b + m, :].rearrange("p b (h t) -> p (b h) t", t=n)
    pe_ok, act_ok, dve_ok = p.counted("products_ready"), p.counted("scalar_ready"), p.counted("vector_ready")
    beta_t, gc_t, eg, edec, bg = (cols[:, i] for i in range(5))
    qT, kT, vT = q[:, :, tok], k[:, :, tok], v[:, :, tok]
    b3 = lambda x: x[:, :, None].to_broadcast([P, H, n])
    L, G = DELTA_LEVELS, H // 2
    groups = [slice(g * G, (g + 1) * G) for g in range(2)]
    pe_end, act_end, dve_end = 2 + 4 * L, 1 + 2 * L, 3 + 4 * L

    @p.block.tensor
    def _(pe):
        pe.transpose(p.ps[0:n, 6, 0:H], beta[:, tok], p.con("ident", n=H, rows=H))
        pe.transpose(p.ps[0:n, 6, H:2 * H], gcum[:, tok], p.con("ident", n=H, rows=H))
        for h in range(H):
            pick = p.con("ident", first=h, n=1, rows=H).to_broadcast([H, P])
            pe.matmul(banks(0)[:, h], pick, gcum[:, tok], start=True, stop=True)
        for h in range(H):
            pick = p.con("ident", first=h, n=1, rows=H).to_broadcast([H, P])
            mm = pe.matmul(banks(2)[:, h], pick, beta[:, tok], start=True, stop=True)
        mm.then_inc(pe_ok.sem, 1)
        pe.wait_ge(dve_ok.sem, dve_ok.at(2))
        for h in range(H):
            mm = pe.matmul(banks(4)[:, h], kT[:, h], X[:, h], start=True, stop=True)
        mm.then_inc(pe_ok.sem, 1)
        for l in range(L):
            for g in range(2):
                pe.wait_ge(dve_ok.sem, dve_ok.at(4 + 4 * l + g))
                for h in range(g * G, (g + 1) * G):
                    mm = pe.matmul(banks(0)[:, h], CT[:, h], Tm[:, h], start=True, stop=True)
                mm.then_inc(pe_ok.sem, 1)
            for g in range(2):
                pe.wait_ge(act_ok.sem, act_ok.at(2 + 2 * l + g))
                for h in range(g * G, (g + 1) * G):
                    pe.matmul(banks(2)[:, h], Um[:, h], X[:, h], start=True, stop=True)
                    mm = pe.matmul(banks(4)[:, h], X[:, h], Um[:, h], start=True, stop=True)
                mm.then_inc(pe_ok.sem, 1)
        pe.wait_ge(dve_ok.sem, dve_ok.at(dve_end))
        for h in range(H):
            pe.transpose(banks(0)[:, h], vT[:, h], p.con("ident"))
        for h in range(H):
            pe.transpose(banks(2)[:, h], kT[:, h], p.con("ident"))
        for h in range(H):
            mm = pe.matmul(banks(4)[:, h], kT[:, h], qT[:, h], start=True, stop=True)
        mm.then_inc(pe_ok.sem, 1)
        if c:
            pe.wait_ge(dve_ok.sem, dve_ok.at(dve_end + 1))
            for h in range(H):
                mm = pe.matmul(banks(0)[:, h], CT[:, h], Um[:, h], start=True, stop=True)
            mm.then_inc(pe_ok.sem, 1)
            pe.wait_ge(act_ok.sem, act_ok.at(act_end + 1))
        else:
            pe.wait_ge(dve_ok.sem, dve_ok.at(dve_end + 1))
        for h in range(H):
            mm = pe.matmul(banks(2)[:, h], Um[:, h], X[:, h], start=True, stop=(c == 0))
            if c:
                mm = pe.matmul(banks(2)[:, h], NT[:, h], S[:, h], start=False, stop=True)
        mm.then_inc(pe_ok.sem, 1)
        pe.wait_ge(act_ok.sem, act_ok.at(act_end + 1 + c))
        for h in range(H):
            mm = pe.matmul(banks(4)[:, h], Tm[:, h], DT[:, h], start=True, stop=(c == 0))
            if c:
                mm = pe.matmul(banks(4)[:, h], S[:, h], CT[:, h], start=False, stop=True)
        if c == 0:
            for h in range(H):
                mm = pe.matmul(banks(0)[:, h], CT[:, h], Tm[:, h], start=True, stop=True)
        mm.then_inc(pe_ok.sem, 1)

    @p.block.vector
    def _(dve):
        link = p.dve_steps.link
        dve.wait_ge(pe_ok.sem, pe_ok.at(1))
        dve.tensor_copy(beta_t, p.ps[:, 6, 0:H])
        link(dve, dve.tensor_copy(gc_t, p.ps[:, 6, H:2 * H]))
        link(dve, dve.tensor_copy(R, banks(0)))
        link(dve, dve.tensor_tensor(edec, R[:, :, n - 1:n].rearrange("p h t -> p (h t)"), gc_t, ALU.subtract))
        link(dve, dve.tensor_tensor(DT, R, b3(gc_t), ALU.subtract))
        dve.tensor_tensor(DT, DT, p.con("below")[:, None, :].to_broadcast([P, H, n]), ALU.add).then_inc(dve_ok.sem, 1)
        dve.tensor_tensor(X, kT, banks(2), ALU.mult).then_inc(dve_ok.sem, 1)
        for m in (Tm, Um):
            link(dve, dve.tensor_copy(m, p.con("ident")[:, None, :].to_broadcast([P, H, n])))
        dve.wait_ge(act_ok.sem, act_ok.at(1))
        dve.tensor_tensor(bg, beta_t, eg, ALU.mult)
        dve.wait_ge(pe_ok.sem, pe_ok.at(2))
        dve.tensor_tensor(NT, banks(4), DT, ALU.mult).then_inc(dve_ok.sem, 1)

        def level_ct(l, g):
            level = p.con("levels", l * P, P)[:, None, :].to_broadcast([P, G, n])
            dve.tensor_tensor(CT[:, groups[g]], NT[:, groups[g]], level, ALU.mult).then_inc(dve_ok.sem, 1)

        dve.wait_ge(dve_ok.sem, dve_ok.at(3))
        for g in range(2):
            level_ct(0, g)
        for l in range(L):
            for g in range(2):
                if l + 1 < L:
                    dve.wait_ge(pe_ok.sem, pe_ok.at(2 + 4 * l + 1 + g))
                    level_ct(l + 1, g)
            for g, hs in enumerate(groups):
                dve.wait_ge(pe_ok.sem, pe_ok.at(2 + 4 * l + 3 + g))
                dve.tensor_tensor(Tm[:, hs], Tm[:, hs], banks(2)[:, hs], ALU.subtract)
                dve.tensor_tensor(Um[:, hs], Um[:, hs], banks(4)[:, hs], ALU.subtract).then_inc(dve_ok.sem, 1)
        dve.wait_ge(pe_ok.sem, pe_ok.at(pe_end + 1))
        dve.tensor_tensor(X, banks(0), b3(beta_t), ALU.mult)
        if c == 0:
            dve.tensor_tensor(CT, banks(2), b3(edec), ALU.mult)
        else:
            dve.tensor_tensor(CT, banks(2), b3(bg), ALU.mult)
        dve.tensor_tensor(DT, banks(4), DT, ALU.mult).then_inc(dve_ok.sem, 1)
        if c:
            dve.wait_ge(pe_ok.sem, pe_ok.at(pe_end + 2))
            dve.tensor_tensor(CT, qT, R, ALU.mult).then_inc(dve_ok.sem, 1)
        dve.wait_ge(pe_ok.sem, pe_ok.at(pe_end + 3 + c))
        dve.tensor_copy(out[:, :, tok], banks(4))
        if c == 0:
            dve.tensor_copy(S, banks(0))

    @p.block.scalar
    def _(act):
        act.wait_ge(dve_ok.sem, dve_ok.at(1))
        act.activation(DT, DT, ACT.Exp)
        act.activation(edec, edec, ACT.Exp)
        act.activation(R, R, ACT.Exp)
        act.activation(eg, gc_t, ACT.Exp).then_inc(act_ok.sem, 1)
        for l in range(L):
            for g, hs in enumerate(groups):
                act.wait_ge(pe_ok.sem, pe_ok.at(2 + 4 * l + 1 + g))
                act.activation(X[:, hs], banks(0)[:, hs], ACT.Copy).then_inc(act_ok.sem, 1)
        if c:
            act.wait_ge(pe_ok.sem, pe_ok.at(pe_end + 2))
            act.activation(NT, banks(0), ACT.Copy, scale=-1.0).then_inc(act_ok.sem, 1)
            act.wait_ge(dve_ok.sem, dve_ok.at(dve_end + 2))
        act.wait_ge(pe_ok.sem, pe_ok.at(pe_end + 2 + c))
        act.activation(Tm, banks(2), ACT.Copy).then_inc(act_ok.sem, 1)

    pe_ok.close(pe_end + 3 + c)
    act_ok.close(act_end + 1 + c)
    dve_ok.close(dve_end + 1 + c)
    p.stage_end()


def moe(p):
    T, E = SEQ, N_EXPERTS
    combine, at = p.area(p.a0, E, T)
    hidden, at = p.split_area(at, D_FFE // P, T)
    silu, at = p.area(at, 2, T)
    prod, at = p.area(at, 2, T)
    lg, at = p.area(at, 2, 8 * 8)
    comb_rows, at = p.area(at, 1, T)
    x = norm(p, p.h, "norm_ffn", KD, T)
    logits, exps, weighed, rows_ok = (p.counted(s) for s in ("logits_ready", "router_exp_ready", "weights_ready", "weight_rows_ready"))

    @p.block.tensor
    def _(pe):
        for i in range(2):
            for k in range(KD):
                mm = pe.matmul(p.ps[:, 4 + i, 0:E], p.u[:, k, i * P:(i + 1) * P], p.par("router", 8 * k, 8), start=(k == 0), stop=(k == KD - 1))
            mm.then_inc(logits.sem, 1)
        pe.wait_ge(weighed.sem, weighed.at(2))
        for i in range(2):
            mm = pe.transpose(p.ps[0:E, 6, i * P:(i + 1) * P], lg[:, i, 56:64], p.con("ident"))
        mm.then_inc(logits.sem, 1)
        pe.wait_ge(rows_ok.sem, rows_ok.at(1))
        for e in range(E):
            mm = pe.matmul(p.ps[:, e, 0:T], p.con("ident", first=e, n=1, rows=E).to_broadcast([E, P]), comb_rows[0:E, 0], start=True, stop=True)
        mm.then_inc(logits.sem, 1)

    @p.block.vector
    def _(dve):
        link = p.dve_steps.link
        for i in range(2):
            x, top, idx = lg[:, i, 0:8], lg[:, i, 8:16], lg[:, i, 16:24]
            diff, w1, w2 = lg[:, i, 24:25], lg[:, i, 25:26], lg[:, i, 26:27]
            dve.wait_ge(logits.sem, logits.at(i + 1))
            link(dve, dve.tensor_copy(x, p.ps[:, 4 + i, 0:E]))
            link(dve, dve.max(top, x))
            link(dve, dve.max_index(p.indices[:, i], top, x))
            link(dve, dve.tensor_copy(idx, p.indices[:, i]))
            dve.tensor_tensor(diff, top[:, 1:2], top[:, 0:1], ALU.subtract).then_inc(exps.sem, 1)
            dve.wait_ge(exps.sem, exps.at(2 * i + 2))
            link(dve, dve.tensor_scalar(w1, w2, 1.0, None, ALU.add))
            link(dve, dve.reciprocal(w1, w1))
            link(dve, dve.tensor_tensor(w2, w2, w1, ALU.mult))
            a, b = lg[:, i, 32:40], lg[:, i, 40:48]
            dve.tensor_scalar(a, p.con("iota"), idx[:, 0:1], w1, ALU.is_equal, ALU.mult)
            link(dve, dve.tensor_scalar(b, p.con("iota"), idx[:, 1:2], w2, ALU.is_equal, ALU.mult))
            dve.tensor_tensor(lg[:, i, 56:64], a, b, ALU.add).then_inc(weighed.sem, 1)

    @p.block.scalar
    def _(act):
        for i in range(2):
            act.wait_ge(exps.sem, exps.at(2 * i + 1))
            act.activation(lg[:, i, 26:27], lg[:, i, 24:25], ACT.Exp).then_inc(exps.sem, 1)
        act.wait_ge(logits.sem, logits.at(3))
        act.activation(comb_rows[0:E, 0], p.ps[0:E, 6, 0:T], ACT.Copy).then_inc(rows_ok.sem, 1)
        act.wait_ge(logits.sem, logits.at(4))
        act.activation(combine, p.ps[:, :, 0:T], ACT.Copy)

    logits.close(4)
    exps.close(4)
    weighed.close(2)
    rows_ok.close(1)
    p.stage_end()

    seg = p.plan["moe"][0]
    kt, nu = D_FFE // P, len(seg.units)
    act_unit, gate_dve = gated_hidden(p, hidden, silu, prod, kt, combine)
    def act_fn(act, i, u, j, bank):
        if j < kt:
            act_unit(act, i, i * kt + j, j, bank)

    def dve_fn(dve, i, u, j, bank):
        if j < kt:
            gate_dve(dve, i, i * kt + j, j, bank)
        else:
            m = j - kt
            dve.tensor_tensor(p.h[:, m, 0:T], bank[:, 0], p.h[:, m, 0:T], ALU.add).then_inc(p.unit_free, 1)

    def before(pe, i, j):
        if j == kt:
            pe.wait_ge(p.unit_free, i * nu + (seg.unit_base + kt))

    n = kt * N_EXPERTS
    gemm(p, "moe", [x[0], hidden], T, act_fn, dve_fn, [("gate_ready", n), ("product_ready", n), ("high_ready", n), ("up_ready", n)],
         pair=lambda j: moe_pair(j, kt, nu), before=before)
    p.stage_end()


def moe_pair(j, kt, nu):
    return 2 if j == nu - 1 else j % 2


def layer_two(p, l):
    T = L2
    xs, at = p.area(p.a0, 32, T)
    rows, at = p.area(at, 2, T)
    at_q = at
    x = norm(p, p.h, "norm1", KD * l, T)
    small_ok = p.counted("small_ready")
    H = SSD_HEADS
    dt, acum = rows[0:H, 0], rows[0:H, 1]
    tmp, _ = p.area(at_q, 5, T)
    t = [tmp[0:H, 0], dt, tmp[0:H, 1], tmp[0:H, 2], tmp[0:H, 3]]
    na = tmp[0:H, 4, 0:1]

    @p.block.tensor
    def _(pe):
        for k in range(KD):
            mm = pe.matmul(p.ps[0:H, 7, 0:T], p.par("w_dt", (l * KD + k) * H, H), p.u[:, k, 0:T], start=(k == 0), stop=(k == KD - 1))
        mm.then_inc(small_ok.sem, 1)

    softplus_rows(p, p.ps[0:H, 7, 0:T], p.par("dt_bias", l)[0:H], p.par("a_log", l)[0:H], t, na)

    @p.block.vector
    def _(dve):
        p.dve_steps.link(dve, dve.tensor_scalar(t[0], dt, na, -1.0, ALU.mult, ALU.mult))
        for o, n in CHUNKS2:
            dve.tensor_tensor_scan(acum[:, o:o + n], t[0][:, o:o + n], t[0][:, o:o + n], 0.0, ALU.add, ALU.bypass)

    p.stage_end()
    conv = conv_silu(p, f"xbc{l}", xs, T, "conv_w", l * CONV2 * 32, 32, "conv_b", l * 32, 16, at_q)
    gemm(p, f"xbc{l}", x, T, **conv)
    p.stage_end()
    ssd(p, l, xs, dt, acum, at_q)
    y = xs[:, 0:16]
    z, at = p.area(p.a0 + 16 * T, 16, T)
    q, at = p.area(p.a0 + 48 * T, 8, T)
    kv, at = p.area(at, 4, T)
    gates, at = p.area(at, 16, T)
    gemm(p, f"z{l}", x, T, act_unit=take_copy(p, z, T, func=ACT.Silu))
    gemm(p, f"q{l}", x, T, act_unit=take_copy(p, q, T))
    gemm(p, f"kv{l}", x, T, act_unit=take_copy(p, kv, T))

    def gate_unit(act, i, u, j, bank):
        for c in range(2):
            ins = act.activation(at_dyn(gates, 2 * u + c, 1)[:, 0], bank[:, c], ACT.Sigmoid, bias=p.par_dyn("b_gate", 2 * u + (l * 16 + c)))
        ins.then_inc(p.unit_free, 1)

    gemm(p, f"gate{l}", x, T, act_unit=gate_unit)
    p.stage_end()

    @p.block.vector
    def _(dve):
        dve.tensor_tensor(y, y, z, ALU.mult)

    p.stage_end()
    head_norm(p, y, [p.par("ssd_norm", l * 16 + c) for c in range(16)], T, 1, 1.0 / 256, EPS, group=2)
    y_split, _ = p.split_area(p.a0 + 16 * T, 16, T)
    x = split_activations(p, y, 16, T, y_split)
    merged, _ = p.area(p.a0, 8, T)

    def gated_unit(dve, i, u, j, bank):
        dve.tensor_tensor(at_dyn(merged, u, 1), bank, at_dyn(gates, u, 1), ALU.mult).then_inc(p.unit_free, 1)

    gemm(p, f"ssd_down{l}", x, T, dve_unit=gated_unit)
    p.stage_end()

    at = p.a0 + 8 * T
    o, at = p.area(at, 8, T)
    kd, at = p.area(at, 4, T)
    v_tok, at = p.area(at, 3, 256)
    rot, at = p.area(at, 2, T)
    k = kv[:, 0:2]
    qk, _ = p.area(p.a0 + 48 * T, 10, T)
    head_norm(p, qk, [p.par("q_norm", l)] * 8 + [p.par("k_norm", l)] * 2, T, 2, 1.0 / 64, EPS)
    for x, n in ((q, 8), (k, 2)):
        rotary(p, x, n, T)

    @p.block.scalar
    def _(act):
        for h in range(KV_HEADS):
            lo = 64 * (h % 2)
            for half in range(2):
                act.activation(kd[64 * half:64 * half + 64, h], k[lo:lo + 64, h // 2], ACT.Copy)

    to_tokens(p, kv[:, 2:4], 2, CHUNKS2, v_tok, T)
    items = []
    for h in range(ATTN_HEADS):
        lo, g = 64 * (h % 2), h // 4
        for i, (first, nq) in enumerate(CHUNKS2):
            nk = first + nq
            items.append(dict(
                nq=nq, nk=nk, tiles=CHUNKS2[:i + 1], part=lo, sink=p.par("sinks", l * 16 + h)[0:nq],
                mask=p.con("window", i * L2, nk, rows=nq), q=q[lo:lo + 64, h // 2, first:first + nq], k=kd[lo:lo + 64, g, 0:nk],
                v=[v_tok[0:m, n, 64 * g:64 * g + 64] for n, (_, m) in enumerate(CHUNKS2[:i + 1])],
                out=o[lo:lo + 64, h // 2, first:first + nq]))
    attention(p, items, ATTN_DIM ** -0.5, at)
    product = p.counted("gated_product_ready")

    def merge_unit(dve, i, u, j, bank):
        dve.tensor_tensor(rot, bank, gates[:, 2 * u + 8:2 * u + 10], ALU.mult).then_inc(product.sem, 1)
        dve.wait_ge(product.sem, product.at(u + 1))
        m = merged[:, 2 * u:2 * u + 2]
        dve.tensor_tensor(m, m, rot, ALU.add).then_inc(p.unit_free, 1)
        dve.wait_ge(p.unit_free, p.plan[f"attn_down{l}"][0].unit_base + u + 1)

    x = split_activations(p, o, 8, T)
    gemm(p, f"attn_down{l}", x, T, dve_unit=merge_unit, signals=[("gated_product_ready", 4)])
    p.stage_end()
    x = split_activations(p, merged, 8, T)
    gemm(p, f"w_o{l}", x, T, dve_unit=take_add(p, p.h, T, 2))
    p.stage_end()


def rotary(p, x, n, T):
    swapped = p.counted("swapped")
    tmp = p.work[:, 0:n * T].rearrange("p (k t) -> p k t", t=T)

    @p.block.tensor
    def _(pe):
        for c in range(n):
            mm = pe.matmul(p.ps[:, c, 0:T], p.con("swap"), x[:, c], start=True, stop=True)
        mm.then_inc(swapped.sem, 1)

    @p.block.vector
    def _(dve):
        wide = lambda name: p.con(name)[:, None, :].to_broadcast([P, n, T])
        dve.wait_ge(swapped.sem, swapped.at(1))
        p.dve_steps.link(dve, dve.tensor_tensor(tmp, p.ps[:, 0:n, 0:T], wide("sin"), ALU.mult))
        p.dve_steps.link(dve, dve.tensor_tensor(x, x, wide("cos"), ALU.mult))
        dve.tensor_tensor(x, x, tmp, ALU.add)

    swapped.close(1)
    p.stage_end()


def ssd(p, l, xs, dt, acum, at):
    H, R, G = SSD_HEADS, SSD_R, SSD_GROUPS
    state, at = p.area(at, H * SSD_P)
    xdt, at = p.area(at, H * SSD_P)
    xdec = p.work[:, 0:H * SSD_P]
    b_tok, at = p.area(at, G * P)
    cols, at = p.area(at, 5, H)
    arg, at = p.area(at, 2, R, P)
    eR, at = p.area(at, 2, R, P)
    mt, at = p.area(at, 2, R, P)
    dt_t, ac_t, dec, gl, dd = (cols[:, i] for i in range(5))
    B, C = xs[:, 16:24], xs[:, 24:32]
    pe_ok, act_ok, dve_ok = p.counted("products_ready"), p.counted("scalar_ready"), p.counted("vector_ready")

    for ci, (o, n) in enumerate(CHUNKS2):
        last = ci == 2
        @p.block.tensor
        def _(pe):
            pe.transpose(p.ps[0:n, 0, 0:H], dt[:, o:o + n], p.con("ident", n=H, rows=H))
            pe.transpose(p.ps[0:n, 0, H:2 * H], acum[:, o:o + n], p.con("ident", n=H, rows=H))
            pe.matmul(p.ps[:, 1, 0:H], acum[:, o + n - 1:o + n].to_broadcast([H, P]), p.con("ident", n=H, rows=H), start=True, stop=True).then_inc(pe_ok.sem, 1)
            for b in range(4):
                for c in range(4):
                    mm = pe.transpose(p.ps[0:n, 2 + b, c * P:(c + 1) * P], xs[:, 4 * b + c, o:o + n], p.con("ident"))
            mm.then_inc(pe_ok.sem, 1)
            for b in range(2):
                for c in range(4):
                    mm = pe.transpose(p.ps[0:n, 6 + b, c * P:(c + 1) * P], B[:, 4 * b + c, o:o + n], p.con("ident"))
            mm.then_inc(pe_ok.sem, 1)

        @p.block.vector
        def _(dve):
            link = p.dve_steps.link
            dve.wait_ge(pe_ok.sem, pe_ok.at(1))
            dve.tensor_copy(dt_t[0:n], p.ps[0:n, 0, 0:H])
            dve.tensor_copy(ac_t[0:n], p.ps[0:n, 0, H:2 * H])
            link(dve, dve.tensor_copy(gl, p.ps[:, 1, 0:H]))
            dve.tensor_tensor(dec[0:n], gl[0:n], ac_t[0:n], ALU.subtract).then_inc(dve_ok.sem, 1)
            dve.wait_ge(pe_ok.sem, pe_ok.at(2))
            wide = lambda x: x[:, :, None].to_broadcast([n, H, SSD_P])
            rows = lambda x: x[0:n].rearrange("p (h d) -> p h d", d=SSD_P)
            link(dve, dve.tensor_tensor(rows(xdt), p.ps[0:n, 2:6, :].rearrange("p b (h d) -> p (b h) d", d=SSD_P), wide(dt_t[0:n]), ALU.mult))
            if not last:
                dve.wait_ge(act_ok.sem, act_ok.at(1))
                dve.tensor_tensor(rows(xdec), rows(xdt), wide(dec[0:n]), ALU.mult)

        @p.block.scalar
        def _(act):
            act.wait_ge(dve_ok.sem, dve_ok.at(1))
            act.activation(dec[0:n], dec[0:n], ACT.Exp).then_inc(act_ok.sem, 1)
            act.activation(gl, gl, ACT.Exp)
            act.wait_ge(pe_ok.sem, pe_ok.at(3))
            act.activation(b_tok[0:n].rearrange("p (b t) -> p b t", t=512), p.ps[0:n, 6:8, :], ACT.Copy)

        pe_ok.close(3)
        dve_ok.close(1)
        act_ok.close(1)
        p.stage_end()
        decays, cbs, ys, sts = (p.counted(s) for s in ("decay_rows_ready", "cb_ready", "y_ready", "state_ready"))
        args, exps, mts, ctaken, ytaken = (p.counted(s) for s in ("decay_args_ready", "decay_exp_ready", "mt_ready", "c_scaled_ready", "y_taken"))

        @p.block.tensor
        def _(pe):
            def first(g):
                if g >= 2:
                    pe.wait_ge(exps.sem, exps.at(g - 1))
                    pe.wait_ge(mts.sem, mts.at(g - 1))
                for r in range(R):
                    mm = pe.matmul(p.ps[:, g % 2, r * P:r * P + n], p.con("ident", first=4 * g + r, n=1, rows=H).to_broadcast([H, P]),
                                   acum[:, o:o + n], start=True, stop=True)
                mm.then_inc(decays.sem, 1)
                pe.matmul(p.ps[0:n, 2 + g % 2, 0:n], B[:, g, o:o + n], C[:, g, o:o + n], start=True, stop=True).then_inc(cbs.sem, 1)

            def second(g):
                pe.wait_ge(mts.sem, mts.at(g + 1))
                if ci:
                    pe.wait_ge(ctaken.sem, ctaken.at(g + 1))
                if g >= 2:
                    pe.wait_ge(ytaken.sem, ytaken.at(g - 1))
                for r in range(R):
                    h = 4 * g + r
                    lo = 64 * (r % 2)
                    out = p.ps[lo:lo + 64, 4 + g % 2, (r // 2) * P:(r // 2) * P + n]
                    mm = pe.matmul(out, xdt[0:n, h * 64:(h + 1) * 64], mt[0:n, g % 2, r, 0:n], start=True, stop=(ci == 0))
                    if ci:
                        mm = pe.matmul(out, state[:, h * 64:(h + 1) * 64], eR[:, g % 2, r, 0:n], start=False, stop=True)
                if not last:
                    mm = pe.matmul(p.ps[:, 6 + g % 2, 0:256], b_tok[0:n, g * P:(g + 1) * P], xdec[0:n, g * 256:(g + 1) * 256], start=True, stop=True)
                mm.then_inc(ys.sem, 1)

            for g in range(G + 1):
                if g < G:
                    first(g)
                if g:
                    second(g - 1)

        @p.block.scalar
        def _(act):
            def early(g):
                act.wait_ge(decays.sem, decays.at(g + 1))
                if g >= 2:
                    act.wait_ge(ys.sem, ys.at(g - 1))
                bank = p.ps[:, g % 2, :].rearrange("p (r t) -> p r t", t=P)[:, :, 0:n]
                act.wait_ge(args.sem, args.at(g + 1))
                if ci:
                    act.activation(eR[:, g % 2, :, 0:n], bank, ACT.Exp)
                act.activation(arg[0:n, g % 2, :, 0:n], arg[0:n, g % 2, :, 0:n], ACT.Exp).then_inc(exps.sem, 1)

            for g in range(G):
                early(g)

        @p.block.vector
        def _(dve):
            def early(g):
                dve.wait_ge(decays.sem, decays.at(g + 1))
                bank = p.ps[0:n, g % 2, :].rearrange("p (r t) -> p r t", t=P)
                for r in range(R):
                    ins = dve.scalar_tensor_tensor(arg[0:n, g % 2, r, 0:n], bank[:, r, 0:n], ac_t[0:n, 4 * g + r:4 * g + r + 1],
                                                   p.con("below")[0:n, 0:n], ALU.subtract, ALU.add)
                ins.then_inc(args.sem, 1)

            def middle(g):
                dve.wait_ge(exps.sem, exps.at(g + 1))
                dve.wait_ge(cbs.sem, cbs.at(g + 1))
                cb = p.ps[0:n, 2 + g % 2, 0:n][:, None, :].to_broadcast([n, R, n])
                dve.tensor_tensor(mt[0:n, g % 2, :, 0:n], arg[0:n, g % 2, :, 0:n], cb, ALU.mult).then_inc(mts.sem, 1)
                if ci:
                    dve.tensor_tensor(eR[:, g % 2, :, 0:n], eR[:, g % 2, :, 0:n], C[:, g, o:o + n][:, None, :].to_broadcast([P, R, n]),
                                      ALU.mult).then_inc(ctaken.sem, 1)

            def late(g):
                dve.wait_ge(ys.sem, ys.at(g + 1))
                for c in range(2):
                    x = xs[:, 2 * g + c, o:o + n]
                    ins = dve.scalar_tensor_tensor(x, x, p.par("d_skip", l * 16 + 2 * g + c), p.ps[:, 4 + g % 2, c * P:c * P + n], ALU.mult, ALU.add)
                if not last:
                    st = state[:, g * 256:(g + 1) * 256]
                    new = p.ps[:, 6 + g % 2, 0:256]
                    if ci:
                        s4 = st.rearrange("p (r d) -> p r d", d=SSD_P)
                        p.dve_steps.link(dve, dve.tensor_tensor(s4, s4, gl[:, 4 * g:4 * g + 4][:, :, None].to_broadcast([P, R, SSD_P]), ALU.mult))
                        ins = dve.tensor_tensor(st, st, new, ALU.add)
                    else:
                        ins = dve.tensor_copy(st, new)
                ins.then_inc(ytaken.sem, 1)

            for g in range(G + 1):
                if g < G:
                    early(g)
                    middle(g)
                if g:
                    late(g - 1)

        for s in (decays, cbs, ys, args, exps, mts, ytaken):
            s.close(G)
        if ci:
            ctaken.close(G)
        p.stage_end()


def mlp_two(p, l):
    T = L2
    hidden, at = p.split_area(p.a0, FF2 // P, T)
    relu, at = p.area(at, 2, T)
    square, at = p.area(at, 4, T)
    x = norm(p, p.h, "norm2", KD * l, T)
    seg = p.plan[f"up{l}"][0]
    squared, high = p.counted("squares_ready"), p.counted("high_ready")

    def act_unit(act, i, u, j, bank):
        b = 2 * (j % 2)
        act.activation(relu, bank, ACT.Relu).then_inc(p.unit_free, 1)
        act.wait_ge(squared.sem, u + squared.at(1))
        act.activation(at_dyn(hidden[0], 2 * u, 2), square[:, b:b + 2], ACT.Copy).then_inc(high.sem, 1)

    def dve_unit(dve, i, u, j, bank):
        b = 2 * (j % 2)
        dve.wait_ge(p.unit_free, u + (seg.unit_base + 1))
        dve.tensor_tensor(square[:, b:b + 2], relu, relu, ALU.mult).then_inc(squared.sem, 1)
        dve.wait_ge(high.sem, u + high.at(1))
        dve.tensor_tensor(at_dyn(hidden[1], 2 * u, 2), square[:, b:b + 2], at_dyn(hidden[0], 2 * u, 2).bitcast(F32), ALU.subtract)

    gemm(p, f"up{l}", x, T, act_unit, dve_unit, [("squares_ready", 16), ("high_ready", 16)])
    p.stage_end()
    gemm(p, f"down{l}", [hidden], T, dve_unit=take_add(p, p.h, T, 1))
    p.stage_end()


def build(nc, weights, params, consts, x, mem, meta, out, upto=10):
    with ExitStack() as ctx:
        block = None
        p = Program(nc, ctx, block, upto)
        p.mem_k, at = p.area(0, 4, SEQ)
        p.mem_v, at = p.area(at, 4, SEQ)
        first_a0 = at
        tok_in, at = p.area(at, 4, D)
        meta_tok, at = p.area(at, 1, D)
        p.mem, at = p.area(at, KD, SEQ)
        mem_end = at
        p.block = ctx.enter_context(nc.Block())
        p.n_loads = 16 * 5

        @p.block.sync
        def _(sp):
            sp.dma_start(p.consts[:], consts).then_inc(p.loaded, 16)
            sp.dma_start(tok_in[:, 0:2], x[0].rearrange("(i p) d -> p i d", p=P)).then_inc(p.loaded, 16)
            sp.dma_start(tok_in[:, 2:4], mem[0].rearrange("(i p) d -> p i d", p=P)).then_inc(p.loaded, 16)
            sp.dma_start(p.params[:], params).then_inc(p.loaded, 16)
            sp.dma_start(meta_tok[0:N_META, 0], meta).then_inc(p.loaded, 16)
            for seg in p.order:
                def body(i):
                    n = len(seg.slots)
                    for j, cols in enumerate(seg.slots):
                        s = seg.ring[j]
                        if seg.ring_free0[j] > 0:
                            sp.wait_ge(p.split, i * n + seg.ring_free0[j])
                        index = i * n + (seg.slot_base + j)
                        src = weights[index] if isinstance(index, int) else weights[bass.ds(index, 1)].rearrange("a p c -> (a p) c")
                        sp.dma_start(p.ring[:, s, 0:cols], src[:, 0:cols]).then_inc(p.full[s], 16)
                repeat(sp, seg.iters, body)

        first = p.order[0]

        @p.block.scalar
        def _(act):
            round_slot(p, act, first, 0, 0)

        @p.block.vector
        def _(dve):
            rest_slot(p, dve, first, 0, 0)

        x_tiles = ((0, P), (P, P))
        from_tokens(p, tok_in[:, 0:2], p.h, x_tiles)
        from_tokens(p, tok_in[:, 2:4], p.mem, x_tiles)
        p.a0 = first_a0
        meta_h = ctx.enter_context(nc.sbuf_tensor("meta_h", [P, KD, N_META], F32))
        from_tokens(p, meta_tok, meta_h, ((0, N_META),))
        for layer in range(2):
            memory_heads(p, layer)
        stages = [
            lambda: layer_even(p), lambda: cross_attention(p, 0), lambda: dense_ffn(p),
            lambda: layer_odd(p), lambda: cross_attention(p, 1), lambda: moe(p),
        ]
        for s in stages[:min(upto, 6)]:
            s()
        T = SEQ
        first = 0
        if upto > 6:
            @p.block.vector
            def _(dve):
                p.dve_steps.link(dve, dve.tensor_copy(p.u[:, :, 0:SEQ], p.h[:, :, 0:SEQ]))
                dve.tensor_copy(p.h[:, :, N_META:L2], p.u[:, :, 0:SEQ])
                dve.tensor_copy(p.h[:, :, 0:N_META], meta_h[:])

            p.stage_end()
            p.a0 = 0
            first = N_META
            stages = [lambda: layer_two(p, 0), lambda: mlp_two(p, 0), lambda: layer_two(p, 1), lambda: mlp_two(p, 1)]
            for s in stages[:upto - 6]:
                s()
        res, _ = p.area(0, 2, D)
        to_tokens(p, p.h, KD, ((first, P), (first + P, P)), res, T)

        @p.block.sync
        def _(sp):
            sp.wait_ge(p.stage_done, 3 * p.stages)
            sp.dma_start(out[0].rearrange("(i p) d -> p i d", p=P), res).then_inc(p.stored, 16)
            sp.wait_ge(p.stored, 16)


def pack_weights(a):
    _, order, n_slots = plan_stream()
    w = np.zeros((n_slots, P, SLOT), np.asarray(a["x"]).dtype)
    at = 0

    def wide(m):
        nonlocal at
        m = np.asarray(m)
        n = m.shape[1] // 256
        w[at:at + n] = m.reshape(KD, P, n, 256).transpose(2, 1, 0, 3).reshape(n, P, SLOT)
        at += n

    def deep(m):
        nonlocal at
        m = np.asarray(m)
        kt = m.shape[0] // P
        parts = 1 if kt <= 16 else 2
        c = m.reshape(parts, kt // parts, P, 8, P).transpose(3, 0, 2, 1, 4).reshape(8 * parts, P, kt // parts * P)
        w[at:at + 8 * parts, :, 0:c.shape[2]] = c
        at += 8 * parts

    def flat(m):
        nonlocal at
        w[at] = np.asarray(m).reshape(2, P, D).transpose(1, 0, 2).reshape(P, SLOT)
        at += 1

    def pairs(m):
        m = np.asarray(m)
        f = m.shape[1] // 2 // P
        wide(m.reshape(D, 2, f, P).transpose(0, 2, 1, 3).reshape(D, 2 * f * P))

    wide(a["xa_w_kv"][0])
    wide(a["xa_w_kv"][1])
    wide(a["ev_w_in"][0])
    wide(a["ev_w_out"][0])
    wide(a["xa_w_q"][0])
    flat(a["xa_w_o"][0])
    pairs(a["ff_w_gu"][0])
    deep(a["ff_w_down"][0])
    wide(a["od_w_in"][0][:, 0:4 * D])
    wide(a["od_w_out"][0])
    wide(a["xa_w_q"][1])
    flat(a["xa_w_o"][1])
    for e in range(N_EXPERTS):
        pairs(a["moe_w_gu"][0, e])
        deep(a["moe_w_down"][0, e])
    for l in range(2):
        m = np.asarray(a["w_in_2"][l])
        wide(m[:, 2048:6144])
        wide(m[:, 0:2048])
        wide(m[:, 6176:7200])
        wide(m[:, 7200:7712])
        wide(m[:, 7712:9760])
        deep(a["w_ssd_down_2"][l])
        wide(a["w_attn_down_2"][l])
        wide(a["w_o_2"][l])
        wide(a["w_mlp_up_2"][l])
        deep(a["w_mlp_down_2"][l])
    assert at == n_slots
    return w


def pack_params(a):
    ch = lambda v: np.asarray(v).reshape(-1, P).T
    twice = lambda v: np.concatenate([np.asarray(v), np.asarray(v)], axis=-1).reshape(-1, P).T
    tiles = lambda m: np.asarray(m).reshape(KD, P, -1).transpose(1, 0, 2).reshape(P, -1)

    def rows(v):
        v = np.asarray(v)
        v = v.reshape(-1, v.shape[-1])
        out = np.zeros((P, v.shape[0]), np.float32)
        out[0:v.shape[1]] = v.T
        return out

    skip = np.asarray(a["d_skip_2"])
    parts = {
        "norm_mix": ch(a["norm_mix"]), "norm_xattn": ch(a["norm_xattn"]), "norm_mem": ch(a["norm_mem"]),
        "norm_ffn": ch(a["norm_ffn"]), "ev_conv": ch(a["ev_conv"]), "ev_q_norm": twice(a["ev_q_norm"]),
        "ev_k_norm": twice(a["ev_k_norm"]), "od_conv": ch(a["od_conv"]), "od_o_norm": ch(a["od_o_norm"]),
        "od_a_log": rows(a["od_a_log"]), "od_dt_bias": rows(a["od_dt_bias"]),
        "xa_q_norm": twice(a["xa_q_norm"]), "xa_k_norm": twice(a["xa_k_norm"]),
        "od_small": tiles(np.asarray(a["od_w_in"])[0][:, 4 * D:]), "router": tiles(a["moe_router"][0]),
        "norm1": ch(a["norm1_g_2"]), "norm2": ch(a["norm2_g_2"]), "conv_w": ch(a["conv_w_2"]), "conv_b": ch(a["conv_b_2"]),
        "b_gate": ch(a["b_gate_2"]), "d_skip": ch(np.repeat(skip, 64, axis=-1)), "ssd_norm": ch(a["ssd_norm_g_2"]),
        "q_norm": twice(a["q_norm_g_2"]), "k_norm": twice(a["k_norm_g_2"]),
        "dt_bias": rows(a["dt_bias_2"]), "a_log": rows(a["a_log_2"]),
        "w_dt": np.concatenate([tiles(np.asarray(a["w_in_2"])[l][:, 6144:6176]) for l in range(2)], axis=1),
        "sinks": np.broadcast_to(np.asarray(a["sinks_2"]).reshape(1, 32), (P, 32)),
    }
    for name, n in PARAMS:
        assert parts[name].shape == (P, n), (name, parts[name].shape, n)
    return np.concatenate([parts[name] for name, _ in PARAMS], axis=1).astype(np.float32)


def make_consts():
    f = np.float32
    i = np.arange(P)
    out = {"ident": np.eye(P), "ones": np.ones((P, P))}
    out["whole_col"] = np.zeros((P, 31))
    out["whole_col"][:, 15] = 1
    out["half_cols"] = np.zeros((P, 38))
    out["half_cols"][0:64, 18] = 1
    out["half_cols"][64:, 19] = 1
    s = np.zeros((P, P))
    for r in range(P):
        if r % 64 < 32:
            s[r + 32, r] = -1
        else:
            s[r - 32, r] = 1
    out["swap"] = s
    t, j = np.arange(SEQ)[:, None], np.arange(SEQ)[None]
    count = np.zeros((SEQ, SEQ))
    for window, d in ((128, 1), (512, 4), (2048, 16)):
        count += (j <= t) & ((t - j) % d == 0) & ((t - j) // d <= window // d)
    m = np.where(count > 0, np.log(np.maximum(count, 1)), NEG)
    out["dilated"] = np.concatenate([m[0:P], m[P:]], axis=1)
    w = np.zeros((P, 3 * L2))
    for n, (first, rows) in enumerate(CHUNKS2):
        q, k = np.arange(first, first + rows)[:, None], np.arange(L2)[None]
        w[0:rows, n * L2:(n + 1) * L2] = np.where((k <= q) & ((k < N_META) | (q - k < WINDOW)), 0.0, NEG)
    out["window"] = w
    inv = f(10000.0) ** (-np.arange(32, dtype=f) / f(32))
    ang = np.arange(L2, dtype=f)[:, None] * inv[None, :].astype(f)
    out["cos"] = np.cos(ang).astype(f)[:, i % 32].T
    out["sin"] = np.sin(ang).astype(f)[:, i % 32].T
    lv = []
    for l in range(DELTA_LEVELS):
        b = 2 << l
        jj, ii = i[:, None], i[None]
        lv.append((jj // b == ii // b) & (ii % b >= b // 2) & (jj % b < b // 2))
    out["levels"] = np.concatenate(lv, axis=1)
    out["below"] = np.where(i[None] >= i[:, None], 0.0, NEG)
    out["iota"] = np.broadcast_to(np.arange(8), (P, 8))
    return np.concatenate([out[name].astype(f) for name, _ in CONSTS], axis=1)


def kernel(**inputs):
    import concourse.bacc as bacc
    from concourse.bass_utils import run_bass_kernel_spmd

    a = {k: np.asarray(v) for k, v in inputs.items()}
    arrays = {
        "in_weights": pack_weights(a), "in_params": pack_params(a), "in_consts": make_consts(),
        "in_x": np.ascontiguousarray(a["x"]), "in_mem": np.ascontiguousarray(a["mem"]),
        "in_meta": np.ascontiguousarray(a["meta_tokens_2"]),
    }
    nc = bacc.Bacc("TRN2", target_bir_lowering=False, num_devices=1)
    aps = [nc.dram_tensor(n, v.shape, F32, kind="ExternalInput").ap() for n, v in arrays.items()]
    out = nc.dram_tensor("out_h", (1, SEQ, D), F32, kind="ExternalOutput").ap()
    build(nc, *aps, out)
    r = run_bass_kernel_spmd(nc, [arrays], core_ids=[0])
    return r.results[0]["out_h"]
```

```python
from contextlib import ExitStack

import numpy as np
import concourse.bass as bass
from concourse import mybir

F32 = mybir.dt.float32
F32R = mybir.dt.float32r
U32 = mybir.dt.uint32
ALU = mybir.AluOpType
ACT = mybir.ActivationFunctionType
AX_X = mybir.AxisListType.X

P = 128
D = 1024
KD = D // P
SEQ = 256
EPS = 1e-6
NEG = -1e30

B_HEADS, B_DIM = 8, 64
C_HEADS, C_DIM, C_CONV = 8, 128, 4
X_HEADS = 4
A_CONV = 3
D_FF = 2816
N_EXPERTS = 8
D_FFE = D_FF // 2
DELTA_CHUNK = 128
DELTA_LEVELS = 7

N_META = 16
L2 = SEQ + N_META
CHUNKS2 = ((0, 16), (16, 128), (144, 128))
SSD_HEADS, SSD_GROUPS, SSD_R, SSD_P = 32, 8, 4, 64
ATTN_HEADS, KV_HEADS, ATTN_DIM = 16, 4, 64
WINDOW = 128
FF2 = 4 * D
CONV2 = 4
CONV_CHUNKS2 = 32

RING = 4
SPLITS = 2
SLOT = 2048

STREAM = (
    [("xa_kv0", "wide", 2), ("xa_kv1", "wide", 2)]
    + [("ev_in", "wide", 12), ("ev_out", "wide", 4), ("xa_q0", "wide", 1), ("xa_o0", "flat", 4)]
    + [("ff_gu", "wide", 22), ("ff_down", "deep", 22)]
    + [("od_in", "wide", 16), ("od_out", "wide", 4), ("xa_q1", "wide", 1), ("xa_o1", "flat", 4)]
    + [("moe", "moe", 8)]
    + [
        (f"{n}{l}", kind, size)
        for l in range(2)
        for n, kind, size in (
            ("xbc", "wide", 16), ("z", "wide", 8), ("q", "wide", 4), ("kv", "wide", 2), ("gate", "wide", 8),
            ("ssd_down", "deep", 16), ("attn_down", "wide", 4), ("w_o", "wide", 4),
            ("up", "wide", 16), ("down", "deep", 32),
        )
    ]
)


class Segment:

    def __init__(self, name, iters, slots, units, unit0):
        self.name, self.iters, self.slots, self.units, self.unit0 = name, iters, slots, units, unit0
        self.parts, self.part_end, self.last_part, self.first_used = 0, [], [0] * len(slots), []
        seen = set()
        for unit in units:
            used = sorted({c[0] for chunk in unit for c in chunk})
            self.first_used.append([s for s in used if s not in seen])
            seen |= set(used)
            for s in used:
                self.parts += 1
                self.last_part[s] = self.parts
            self.part_end.append(self.parts)


def wide_unit(s):
    return [[(s, k, k * 256 + c * P, k, 0) for k in range(KD)] for c in range(2)]


def plan_stream():
    plan, order = {}, []
    for name, kind, size in STREAM:
        segs = []
        if kind == "wide":
            n = size // 4 if size >= 8 else 0
            if n:
                segs.append(Segment(name, n, [SLOT] * 4, [wide_unit(s) for s in range(4)], 0))
            if size - 4 * n:
                rest = size - 4 * n
                segs.append(Segment(name, 1, [SLOT] * rest, [wide_unit(s) for s in range(rest)], 4 * n))
        elif kind == "deep":
            parts = 1 if size <= 16 else 2
            kt = size // parts
            per = 4 // parts
            units = [[[(u * parts + k // kt, k % kt, (k % kt) * P, k, 0) for k in range(size)]] for u in range(per)]
            segs.append(Segment(name, 8 // per, [kt * P] * 4, units, 0))
        elif kind == "flat":
            units = [[[(0, k, k * D + (2 * u + c) * P, k, 0) for k in range(2)] for c in range(2)] for u in range(4)]
            segs.append(Segment(name, 1, [SLOT], units, 0))
        else:
            kt = D_FFE // P
            half = KD // 2
            units = [[[(k // half, k % half, k % half * 256 + c * P, k, 0) for k in range(KD)] for c in range(2)]]
            units += [wide_unit(s + 1) for s in range(1, kt)]
            units += [[[(kt + 1 + c, k, k * P, k, 1) for k in range(kt)]] for c in range(8)]
            segs.append(Segment(name, N_EXPERTS, [SLOT // 2] * 2 + [SLOT] * (kt - 1) + [kt * P] * 8, units, 0))
            assert len(segs[0].slots) % SPLITS == 0
        plan[name] = segs
        order += segs
    position, units_before, parts_before, slots_before = 0, 0, 0, 0
    fills = [0] * RING
    ring_holds, split_ends = [0] * RING, [0] * SPLITS
    for seg in order:
        looped = seg.iters > 1
        if looped:
            position = -(-position // RING) * RING
        seg.unit_base, seg.part_base, seg.slot_base = units_before, parts_before, slots_before
        n, nu, npart = len(seg.slots), len(seg.units), seg.parts
        seg.ring = [(position + j) % RING for j in range(n)]
        per = [seg.ring.count(s) for s in range(RING)]
        seen = list(fills)
        seg.full0, seg.full_step, seg.ring_free0, seg.split_free0 = [], [], [], []
        for j, s in enumerate(seg.ring):
            seen[s] += 1
            seg.full0.append(16 * seen[s])
            seg.full_step.append(16 * per[s])
            same = [i for i in range(n) if seg.ring[i] == s]
            half = [i for i in range(n) if seg.ring[i] % SPLITS == s % SPLITS]
            if same[0] < j:
                seg.ring_free0.append(slots_before + [i for i in same if i < j][-1] + 1)
            else:
                again = slots_before + same[-1] + 1 - n if looped else 0
                seg.ring_free0.append(max(again, ring_holds[s]))
            if half[0] < j:
                seg.split_free0.append(parts_before + seg.last_part[[i for i in half if i < j][-1]])
            else:
                again = parts_before + seg.last_part[half[-1]] - npart if looped else 0
                seg.split_free0.append(max(again, split_ends[s % SPLITS]))
        for j, s in enumerate(seg.ring):
            ring_holds[s] = slots_before + (seg.iters - 1) * n + j + 1
            split_ends[s % SPLITS] = parts_before + (seg.iters - 1) * npart + seg.last_part[j]
        for s in range(RING):
            fills[s] += seg.iters * per[s]
        position = -(-(position + n) // RING) * RING if looped else position + n
        units_before += seg.iters * nu
        parts_before += seg.iters * npart
        slots_before += seg.iters * n
    for seg, after in zip(order, order[1:] + [None]):
        seg.after = after
        seg.split_cols = list(seg.slots)
        if seg.iters > 1 and after is not None:
            seg.split_cols[0] = max(seg.slots[0], after.slots[0])
    return plan, order, slots_before


def split_segment(seg, n):
    a = Segment(seg.name, n, seg.slots, seg.units, seg.unit0)
    b = Segment(seg.name, seg.iters - n, seg.slots, seg.units, 0)
    for s, done in ((a, 0), (b, n)):
        s.ring, s.full_step, s.split_cols = seg.ring, seg.full_step, seg.split_cols
        s.full0 = [f + done * st for f, st in zip(seg.full0, seg.full_step)]
        s.ring_free0 = [f + done * len(seg.slots) for f in seg.ring_free0]
        s.split_free0 = [f + done * seg.parts for f in seg.split_free0]
        s.unit_base = seg.unit_base + done * len(seg.units)
        s.part_base = seg.part_base + done * seg.parts
        s.slot_base = seg.slot_base + done * len(seg.slots)
    a.after, b.after = b, seg.after
    return a, b


PARAMS = [
    ("norm_mix", 2 * KD), ("norm_xattn", 2 * KD), ("norm_mem", 2 * KD), ("norm_ffn", 2 * KD),
    ("ev_conv", A_CONV * 4), ("ev_q_norm", 1), ("ev_k_norm", 1),
    ("od_conv", C_CONV * 24), ("od_o_norm", 1), ("od_a_log", 1), ("od_dt_bias", 1),
    ("xa_q_norm", 2), ("xa_k_norm", 2),
    ("od_small", KD * 16), ("router", KD * 8),
    ("norm1", 2 * KD), ("norm2", 2 * KD), ("conv_w", 2 * CONV2 * 32), ("conv_b", 2 * 32), ("b_gate", 2 * 16),
    ("d_skip", 2 * 16), ("ssd_norm", 2 * 16), ("q_norm", 2), ("k_norm", 2), ("dt_bias", 2), ("a_log", 2),
    ("w_dt", 2 * KD * 32), ("sinks", 2 * 16),
]
CONSTS = [
    ("ident", P), ("ones", P), ("whole_col", 2 * 16 - 1), ("half_cols", 2 * 20 - 2), ("dilated", 2 * SEQ),
    ("swap", P),
    ("window", 3 * L2), ("cos", L2), ("sin", L2), ("levels", DELTA_LEVELS * P), ("below", P), ("iota", 8),
]


def offsets(spec):
    at, out = 0, {}
    for name, n in spec:
        out[name] = (at, n)
        at += n
    return out, at


class Counted:

    def __init__(self, sem):
        self.sem, self.base = sem, 0

    def at(self, n):
        return self.base + n

    def close(self, n):
        self.base += n


class Steps:

    def __init__(self, sem):
        self.sem, self.count = sem, 0

    def mark(self, ins):
        self.count += 1
        ins.then_inc(self.sem, 1)
        return self.count

    def link(self, eng, ins):
        eng.wait_ge(self.sem, self.mark(ins))


class Program:
    def __init__(self, nc, ctx):
        self.nc, self.ctx = nc, ctx
        self.counts = {}
        self.plan, self.order, self.n_slots = plan_stream()
        end = self.order[-1]
        if end.iters > 1:
            self.plan[end.name] = self.order[-1:] = list(split_segment(end, end.iters - 1))
            self.plan[end.name][1].unit0 = (end.iters - 1) * len(end.units)
        self.stage_done = self.sem("stage_done")
        self.stages = 0
        self.part_done = self.sem("part_done")
        self.rounded = self.sem("slot_rounded")
        self.split = self.sem("slot_split")
        self.unit_free = self.sem("unit_free")
        self.full = [self.sem(f"slot_full{s}") for s in range(RING)]
        self.mem_loaded = self.sem("memory_loaded")
        self.loaded = self.sem("inputs_loaded")
        self.stored = self.sem("output_stored")
        self.act_steps = Steps(self.sem("act_step"))
        self.dve_steps = Steps(self.sem("dve_step"))
        sb = lambda name, shape, dt=F32: ctx.enter_context(nc.sbuf_tensor(name, shape, dt))
        self.ring = sb("ring", [P, RING, SLOT])
        self.par_at, n_par = offsets(PARAMS)
        self.con_at, n_con = offsets(CONSTS)
        self.params = sb("params", [P, n_par])
        self.consts = sb("consts", [P, n_con])
        self.h = sb("h", [P, KD, L2])
        self.high = sb("act_high", [P, KD, L2], F32R)
        self.low = sb("act_low", [P, KD, L2], F32R)
        self.w_high = sb("w_high", [P, SPLITS, SLOT], F32R)
        self.w_low = sb("w_low", [P, SPLITS, SLOT], F32R)
        self.u = sb("u", [P, KD, L2])
        self.work = self.u[:].rearrange("p k t -> p (k t)")
        self.rstd = sb("rstd", [P, L2])
        self.arena_cols = 21600
        self.arena = sb("arena", [P, self.arena_cols])
        self.arena_r = nc.alloc_sbuf_tensor_at("arena_r", [P, self.arena_cols], F32R, offset=nc.lookup_mloc(self.arena).addr)
        self.indices = sb("indices", [P, 2, 8], U32)
        self.ps = ctx.enter_context(nc.psum_tensor("ps", [P, 8, 512], F32))

    def sem(self, name):
        return self.ctx.enter_context(self.nc.semaphore(name))

    def counted(self, name):
        if name not in self.counts:
            self.counts[name] = Counted(self.sem(name))
        return self.counts[name]

    def par(self, name, first=0, n=1):
        at = self.par_at[name][0] + first
        return self.params[:, at:at + n]

    def par_dyn(self, name, first):
        return self.params[:, bass.ds(self.par_at[name][0] + first, 1)]

    def con(self, name, first=0, n=None, rows=P):
        at, size = self.con_at[name]
        return self.consts[0:rows, at + first:at + first + (size if n is None else n)]

    def head_cols(self, heads, chunk, rows):
        if heads == 1:
            return self.con("whole_col", 15 - chunk, rows)
        return self.con("half_cols", 18 - 2 * chunk, rows)

    def area(self, at, *dims):
        n = int(np.prod(dims))
        assert at + n <= self.arena_cols, (at, n)
        v = self.arena[:, at:at + n]
        if len(dims) == 2:
            v = v.rearrange("p (a b) -> p a b", b=dims[1])
        elif len(dims) == 3:
            v = v.rearrange("p (a b c) -> p a b c", b=dims[1], c=dims[2])
        return v, at + n

    def split_area(self, at, n, T):
        assert at + 2 * n * T <= self.arena_cols
        v = [self.arena_r[:, at + i * n * T:at + (i + 1) * n * T].rearrange("p (k t) -> p k t", t=T) for i in range(2)]
        return v, at + 2 * n * T

    def stage_end(self):
        self.stages += 1
        goal = 3 * self.stages
        for start in (self.block.tensor, self.block.scalar, self.block.vector):
            @start
            def _(eng):
                eng.drain().then_inc(self.stage_done, 1)
                eng.wait_ge(self.stage_done, goal)


def repeat(eng, n, body):
    if n == 1:
        body(0)
    else:
        with eng.Fori(0, n) as i:
            body(i)


def at_dyn(view, first, n):
    return view[:, first:first + n] if isinstance(first, int) else view[:, bass.ds(first, n)]


def round_slot(p, act, seg, j, i):
    s = seg.ring[j]
    cols = seg.split_cols[j]
    act.wait_ge(p.full[s], i * seg.full_step[j] + seg.full0[j])
    if seg.split_free0[j] > 0:
        act.wait_ge(p.part_done, i * seg.parts + seg.split_free0[j])
    act.activation(p.w_high[:, s % SPLITS, 0:cols], p.ring[:, s, 0:cols], ACT.Copy).then_inc(p.rounded, 1)


def rest_slot(p, dve, seg, j, i):
    s = seg.ring[j]
    cols = seg.split_cols[j]
    dve.wait_ge(p.rounded, i * len(seg.slots) + (seg.slot_base + j + 1))
    dve.tensor_tensor(p.w_low[:, s % SPLITS, 0:cols], p.ring[:, s, 0:cols], p.w_high[:, s % SPLITS, 0:cols].bitcast(F32),
                      ALU.subtract).then_inc(p.split, 1)


def next_slot(seg, j, i):
    if j + 1 < len(seg.slots):
        return seg, j + 1, i
    if seg.iters > 1:
        return seg, 0, i + 1
    return None if seg.after is None else (seg.after, 0, 0)


def same_buffers(seg, j, after):
    several = len(seg.slots) == 1 and seg.parts > 1
    return several or seg.ring[j] % SPLITS == after[0].ring[after[1]] % SPLITS


def gemm(p, name, xs, T, act_unit=None, dve_unit=None, signals=(), pair=lambda j: j % 2, before=None,
         act_late=None, beside=None):
    for seg in p.plan[name]:
        nu = len(seg.units)

        @p.block.tensor
        def _(pe):
            def body(i):
                for j, unit in enumerate(seg.units):
                    number = seg.unit_base + j + 1
                    if number > 2:
                        pe.wait_ge(p.unit_free, i * nu + (number - 2))
                    used = sorted({c[0] for chunk in unit for c in chunk})
                    for s in used:
                        b = seg.ring[s] % SPLITS
                        number = i * len(seg.slots) + (seg.slot_base + s + 1)
                        if s in seg.first_used[j]:
                            pe.wait_ge(p.rounded, number)
                        for w, parts in ((p.w_high, (0, 1)), (p.w_low, (0,))):
                            if w is p.w_low and s in seg.first_used[j]:
                                pe.wait_ge(p.split, number)
                            for c, chunk in enumerate(unit):
                                for n, (slot, k, col, xk, which) in enumerate(chunk):
                                    if slot != s:
                                        continue
                                    for x in parts:
                                        if before is not None and w is p.w_high and x == 0:
                                            before(pe, i, j, n)
                                        mm = pe.matmul(p.ps[:, 2 * pair(j) + c, 0:T], w[:, b, col:col + P], xs[which][x][:, xk, 0:T],
                                                       start=(n == 0 and w is p.w_high and x == 0),
                                                       stop=(n == len(chunk) - 1 and w is p.w_low))
                        mm.then_inc(p.part_done, 1)
            repeat(pe, seg.iters, body)

        pre_split = beside is not None and seg is p.plan[name][0]
        if pre_split:
            assert seg.iters == 1
            after = next_slot(seg, 0, 0)
            for split_fn, start in ((round_slot, p.block.scalar), (rest_slot, p.block.vector)):
                @start
                def _(eng):
                    split_fn(p, eng, *after)
            beside()

        for unit_fn, split_fn, start in ((act_unit, round_slot, p.block.scalar), (dve_unit, rest_slot, p.block.vector)):
            @start
            def _(eng):
                def body(i):
                    for j, unit in enumerate(seg.units):
                        for s in seg.first_used[j]:
                            after = next_slot(seg, s, i)
                            if after is not None and not same_buffers(seg, s, after) and not (pre_split and s == 0):
                                split_fn(p, eng, *after)
                        late = act_late if split_fn is round_slot else None
                        if late is not None and j > 0:
                            late(eng, i * nu + (seg.unit0 + j - 1), j - 1)
                        if unit_fn is not None:
                            eng.wait_ge(p.part_done, i * seg.parts + (seg.part_base + seg.part_end[j]))
                            unit_fn(eng, i, i * nu + (seg.unit0 + j), j, p.ps[:, 2 * pair(j):2 * pair(j) + len(unit), 0:T])
                        for s in range(len(seg.slots)):
                            after = next_slot(seg, s, i)
                            if seg.last_part[s] == seg.part_end[j] and after is not None and same_buffers(seg, s, after):
                                split_fn(p, eng, *after)
                    if late is not None:
                        late(eng, i * nu + (seg.unit0 + nu - 1), nu - 1)
                repeat(eng, seg.iters, body)
    for name, n in signals:
        p.counted(name).close(n)


def take_copy(p, dst, T, per=2, func=ACT.Copy):
    def unit(act, i, u, j, bank):
        act.activation(at_dyn(dst, per * u, per)[:, :, 0:T], bank, func).then_inc(p.unit_free, 1)
    return unit


def gate_in(p, name, dst, gate, T):
    base = p.plan[name][0].unit_base

    def unit(dve, i, u, j, bank):
        dve.wait_ge(p.unit_free, u + (base + 1))
        pair = at_dyn(dst, 2 * u, 2)
        dve.tensor_tensor(pair, pair, at_dyn(gate, 2 * u, 2), ALU.mult)
    return unit


def take_add(p, dst, T, per):
    def unit(dve, i, u, j, bank):
        out = at_dyn(dst, per * u, per)[:, :, 0:T]
        dve.tensor_tensor(out, bank, out, ALU.add).then_inc(p.unit_free, 1)
    return unit


def split_activations(p, src, n, T, dst=None):
    high, low = dst or (p.high[:, 0:n, 0:T], p.low[:, 0:n, 0:T])
    done = p.counted("high_ready")

    @p.block.scalar
    def _(act):
        for k in range(0, n, 2):
            act.activation(high[:, k:k + 2], src[:, k:k + 2], ACT.Copy).then_inc(done.sem, 1)

    @p.block.vector
    def _(dve):
        for c, k in enumerate(range(0, n, 2)):
            dve.wait_ge(done.sem, done.at(c + 1))
            dve.tensor_tensor(low[:, k:k + 2], src[:, k:k + 2], high[:, k:k + 2].bitcast(F32), ALU.subtract)

    done.close(n // 2)
    p.stage_end()
    return [(high, low)]


def keep_clock(p, pe, n):
    for _ in range(n):
        pe.matmul(p.ps[:, 6, 0:P], p.con("ones"), p.con("ones"), start=True, stop=True)


def norm(p, src, gain, gain0, T):
    sq = p.u[:, :, 0:T]
    pairs = [slice(k, k + 2) for k in range(0, KD, 2)]
    n = len(pairs)
    sums, means, roots, normed, high = (p.counted(s) for s in ("sums_ready", "means_ready", "roots_ready", "normed", "high_ready"))
    squares = p.counted("squares_ready"), p.counted("odd_squares_ready")

    @p.block.scalar
    def _(act):
        for ks in pairs[0::2]:
            act.activation(sq[:, ks], src[:, ks, 0:T], ACT.Square).then_inc(squares[0].sem, 1)
        act.wait_ge(means.sem, means.at(1))
        act.activation(p.rstd[:, 0:T], p.rstd[:, 0:T], ACT.Sqrt).then_inc(roots.sem, 1)
        for c, ks in enumerate(pairs):
            act.wait_ge(normed.sem, normed.at(c + 1))
            act.activation(p.high[:, ks, 0:T], p.u[:, ks, 0:T], ACT.Copy).then_inc(high.sem, 1)

    @p.block.tensor
    def _(pe):
        for c, ks in enumerate(pairs):
            pe.wait_ge(squares[c % 2].sem, squares[c % 2].at(c // 2 + 1))
            for k in range(ks.start, ks.stop):
                mm = pe.matmul(p.ps[:, 7, 0:T], p.con("ones"), sq[:, k], start=(k == 0), stop=(k == KD - 1))
        mm.then_inc(sums.sem, 1)
        keep_clock(p, pe, 32)

    @p.block.vector
    def _(dve):
        def low_part(c):
            dve.wait_ge(high.sem, high.at(c + 1))
            ks = pairs[c]
            dve.tensor_tensor(p.low[:, ks, 0:T], p.u[:, ks, 0:T], p.high[:, ks, 0:T].bitcast(F32), ALU.subtract)

        for ks in pairs[1::2]:
            dve.tensor_tensor(sq[:, ks], src[:, ks, 0:T], src[:, ks, 0:T], ALU.mult).then_inc(squares[1].sem, 1)
        dve.wait_ge(sums.sem, sums.at(1))
        dve.tensor_scalar(p.rstd[:, 0:T], p.ps[:, 7, 0:T], 1.0 / D, EPS, ALU.mult, ALU.add).then_inc(means.sem, 1)
        dve.wait_ge(roots.sem, roots.at(1))
        p.dve_steps.link(dve, dve.reciprocal(p.rstd[:, 0:T], p.rstd[:, 0:T]))
        for k in range(KD):
            ins = dve.scalar_tensor_tensor(p.u[:, k, 0:T], src[:, k, 0:T], p.par(gain, gain0 + k), p.rstd[:, 0:T], ALU.mult, ALU.mult)
            if k % 2:
                ins.then_inc(normed.sem, 1)
        for c in range(n):
            low_part(c)

    for s, m in ((squares[0], n // 2), (squares[1], n // 2), (sums, 1), (means, 1), (roots, 1), (normed, n), (high, n)):
        s.close(m)
    p.stage_end()
    return [(p.high, p.low)]


def head_norm(p, x, gains, T, heads, scale, eps, group=1, split=None):
    n = len(gains)
    ng = n // group
    rows = ng * heads
    sq = p.work[:, 0:8 * T].rearrange("p (k t) -> p k t", t=T)
    pieces = [(c, min(4, n - c)) for c in range(0, n, 4)]
    squares, sums, means, roots, inverse, spread, scaled = (p.counted(s) for s in (
        "squares_ready", "sums_ready", "means_ready", "roots_ready", "inverse_ready", "spread_ready", "heads_scaled"))
    high = p.counted("high_ready")
    rstd = p.rstd[0:rows, 0:T]
    picks = p.work[0:rows, 0:rows * P // 2]

    @p.block.scalar
    def _(act):
        for b, (c, m) in enumerate(pieces):
            if b >= 2:
                act.wait_ge(sums.sem, sums.at(b - 1))
            act.activation(sq[:, 4 * (b % 2):4 * (b % 2) + m], x[:, c:c + m], ACT.Square).then_inc(squares.sem, 1)
        act.wait_ge(means.sem, means.at(1))
        act.activation(rstd, rstd, ACT.Sqrt).then_inc(roots.sem, 1)
        if split is not None:
            for g in range(ng):
                cs = slice(g * group, (g + 1) * group)
                act.wait_ge(scaled.sem, scaled.at(g + 1))
                act.activation(split[0][:, cs], x[:, cs], ACT.Copy).then_inc(high.sem, 1)

    @p.block.tensor
    def _(pe):
        for b, (c0, m) in enumerate(pieces):
            pe.wait_ge(squares.sem, squares.at(b + 1))
            for c in range(c0, c0 + m):
                first = p.head_cols(heads, c // group, rows)
                mm = pe.matmul(p.ps[0:rows, 7, 0:T], first, sq[:, 4 * (b % 2) + c - c0], start=(c == 0), stop=(c == n - 1))
            mm.then_inc(sums.sem, 1)
        keep_clock(p, pe, 16)
        pe.wait_ge(inverse.sem, inverse.at(1))
        for g in range(ng):
            if g >= 7:
                pe.wait_ge(scaled.sem, scaled.at(g - 6))
            if heads == 2:
                pick = picks[:, g * P:(g + 1) * P]
            else:
                pick = p.con("ident", first=g, n=1, rows=rows).to_broadcast([rows, P])
            pe.matmul(p.ps[:, g % 7, 0:T], pick, rstd, start=True, stop=True).then_inc(spread.sem, 1)

    @p.block.vector
    def _(dve):
        def low_part(g):
            cs = slice(g * group, (g + 1) * group)
            dve.wait_ge(high.sem, high.at(g + 1))
            dve.tensor_tensor(split[1][:, cs], x[:, cs], split[0][:, cs].bitcast(F32), ALU.subtract)

        dve.wait_ge(sums.sem, sums.at(len(pieces)))
        dve.tensor_scalar(rstd, p.ps[0:rows, 7, 0:T], scale, eps, ALU.mult, ALU.add).then_inc(means.sem, 1)
        if heads == 2:
            dve.tensor_copy(picks.rearrange("r (c m) -> r c m", m=P // 2), p.con("ident", n=rows, rows=rows)[:, :, None].to_broadcast([rows, rows, P // 2]))
        dve.wait_ge(roots.sem, roots.at(1))
        dve.reciprocal(rstd, rstd).then_inc(inverse.sem, 1)
        for g in range(ng):
            dve.wait_ge(spread.sem, spread.at(g + 1))
            for c in range(g * group, (g + 1) * group):
                ins = dve.scalar_tensor_tensor(x[:, c], x[:, c], gains[c], p.ps[:, g % 7, 0:T], ALU.mult, ALU.mult)
            ins.then_inc(scaled.sem, 1)
            if split is not None and g:
                low_part(g - 1)
        if split is not None:
            low_part(ng - 1)

    if split is not None:
        high.close(ng)
    for s, k in ((squares, len(pieces)), (sums, len(pieces)), (means, 1), (roots, 1), (inverse, 1), (spread, ng), (scaled, ng)):
        s.close(k)
    p.stage_end()


def to_tokens(p, src, n_chunks, tiles, dst):
    groups = [(i, o, n, c, min(4, n_chunks - c)) for i, (o, n) in enumerate(tiles) for c in range(0, n_chunks, 4)]
    turned, moved = p.counted("turned"), p.counted("moved")

    @p.block.tensor
    def _(pe):
        for g, (i, o, n, c0, m) in enumerate(groups):
            if g >= 4:
                pe.wait_ge(moved.sem, moved.at(g - 3))
            for c in range(m):
                mm = pe.transpose(p.ps[0:n, 4 + g % 4, c * P:(c + 1) * P], src[:, c0 + c, o:o + n], p.con("ident"))
            mm.then_inc(turned.sem, 1)

    @p.block.scalar
    def _(act):
        for g, (i, o, n, c0, m) in enumerate(groups):
            act.wait_ge(turned.sem, turned.at(g + 1))
            act.activation(dst[0:n, i, c0 * P:(c0 + m) * P], p.ps[0:n, 4 + g % 4, 0:m * P], ACT.Copy).then_inc(moved.sem, 1)

    turned.close(len(groups))
    moved.close(len(groups))
    p.stage_end()


def from_tokens(p, src, dst, tiles, loaded, n_loads):
    groups = [(i, o, n, c) for i, (o, n) in enumerate(tiles) for c in (0, 4)]
    turned, moved = p.counted("turned"), p.counted("moved")

    @p.block.tensor
    def _(pe):
        pe.wait_ge(loaded, 16 * n_loads)
        for g, (i, o, n, c0) in enumerate(groups):
            if g >= 4:
                pe.wait_ge(moved.sem, moved.at(g - 3))
            for c in range(4):
                mm = pe.transpose(p.ps[:, 4 + g % 4, c * P:c * P + n], src[0:n, i, (c0 + c) * P:(c0 + c + 1) * P],
                                  p.con("ident", n=n, rows=n))
            mm.then_inc(turned.sem, 1)

    @p.block.scalar
    def _(act):
        for g, (i, o, n, c0) in enumerate(groups):
            act.wait_ge(turned.sem, turned.at(g + 1))
            bank = p.ps[:, 4 + g % 4, :].rearrange("p (c t) -> p c t", t=P)
            act.activation(dst[:, c0:c0 + 4, o:o + n], bank[:, :, 0:n], ACT.Copy).then_inc(moved.sem, 1)

    turned.close(len(groups))
    moved.close(len(groups))
    p.stage_end()


def attention(p, items, scale, at):
    masked, at = p.area(at, 3, L2)
    probs, at = p.area(at, 4, L2)
    turned_p, at = p.area(at, 3, 3, P)
    small, at = p.area(at, 4, 8)
    names = ("scores_ready", "masked_ready", "exp_ready", "probs_ready", "probs_turned", "turned_ready", "heads_ready", "heads_moved")
    scores, mask_ok, exp_ok, prob_ok, turn_ok, tcopy_ok, head_ok, moved = (p.counted(n) for n in names)
    high = p.counted("high_ready")
    N = len(items)

    @p.block.tensor
    def _(pe):
        def do_scores(i):
            t = items[i]
            if i >= 3:
                pe.wait_ge(mask_ok.sem, mask_ok.at(i - 2))
            pe.matmul(p.ps[0:t["nq"], i % 3, 0:t["nk"]], t["q"], t["k"], start=True, stop=True).then_inc(scores.sem, 1)

        def do_turn(i):
            t = items[i]
            pe.wait_ge(prob_ok.sem, prob_ok.at(i + 1))
            if i >= 3:
                pe.wait_ge(tcopy_ok.sem, tcopy_ok.at(i - 2))
            for n, (o, rows) in enumerate(t["tiles"]):
                mm = pe.transpose(p.ps[0:rows, 3 + i % 3, n * P:n * P + t["nq"]], probs[0:t["nq"], i % 4, o:o + rows],
                                  p.con("ident", n=t["nq"], rows=t["nq"]))
            mm.then_inc(turn_ok.sem, 1)

        def do_heads(i):
            t = items[i]
            pe.wait_ge(tcopy_ok.sem, tcopy_ok.at(i + 1))
            if i >= 2:
                pe.wait_ge(moved.sem, moved.at(i - 1))
            for n, (o, rows) in enumerate(t["tiles"]):
                mm = pe.matmul(p.ps[t["part"]:t["part"] + 64, 6 + i % 2, 0:t["nq"]], t["v"][n], turned_p[0:rows, i % 3, n, 0:t["nq"]],
                               start=(n == 0), stop=(n == len(t["tiles"]) - 1))
            mm.then_inc(head_ok.sem, 1)

        do_scores(0)
        for i in range(N + 4):
            if i + 1 < N:
                do_scores(i + 1)
            if 3 <= i < N + 3:
                do_turn(i - 3)
            if i >= 4:
                do_heads(i - 4)

    @p.block.vector
    def _(dve):
        mark, sem = p.dve_steps.mark, p.dve_steps.sem

        def low_part(i):
            t = items[i]
            high_out, low_out = t["out"]
            dve.wait_ge(high.sem, high.at(i + 1))
            dve.tensor_tensor(low_out, p.ps[t["part"]:t["part"] + 64, 6 + i % 2, 0:t["nq"]], high_out.bitcast(F32), ALU.subtract).then_inc(moved.sem, 1)

        for i in range(N + 5):
            if i < N:
                t = items[i]
                nq, nk = t["nq"], t["nk"]
                dve.wait_ge(scores.sem, scores.at(i + 1))
                if i >= 3:
                    dve.wait_ge(exp_ok.sem, exp_ok.at(i - 2))
                m, sm = masked[0:nq, i % 3, 0:nk], small[0:nq, i % 4]
                if t["mask"] is None:
                    masked_at = mark(dve.tensor_scalar(m, p.ps[0:nq, i % 3, 0:nk], scale, None, ALU.mult))
                else:
                    masked_at = mark(dve.scalar_tensor_tensor(m, p.ps[0:nq, i % 3, 0:nk], scale, t["mask"], ALU.mult, ALU.add))
            if 2 <= i < N + 2:
                old = items[i - 2]
                oq, ok = old["nq"], old["nk"]
                osm = small[0:oq, (i - 2) % 4]
                dve.wait_ge(exp_ok.sem, exp_ok.at(i - 1))
                if old["sink"] is not None:
                    summed_at = mark(dve.tensor_tensor(osm[:, 2:3], osm[:, 2:3], osm[:, 3:4], ALU.add))
            if i < N:
                dve.wait_ge(sem, masked_at)
                max_at = mark(dve.tensor_reduce(sm[:, 0:1], m, AX_X, ALU.max))
            if 2 <= i < N + 2:
                if old["sink"] is not None:
                    dve.wait_ge(sem, summed_at)
                inverse_at = mark(dve.reciprocal(osm[:, 4:5], osm[:, 2:3]))
            if i < N:
                other = t["sink"] if t["sink"] is not None else sm[:, 0:1]
                dve.wait_ge(sem, max_at)
                dve.tensor_scalar(sm[:, 1:2], sm[:, 0:1], other, -1.0, ALU.max, ALU.mult).then_inc(mask_ok.sem, 1)
            if 2 <= i < N + 2:
                dve.wait_ge(sem, inverse_at)
                probs_old = probs[0:oq, (i - 2) % 4, 0:ok]
                dve.tensor_scalar(probs_old, probs_old, osm[:, 4:5], None, ALU.mult).then_inc(prob_ok.sem, 1)
            if i >= 5:
                low_part(i - 5)

    @p.block.scalar
    def _(act):
        def do_exp(i):
            t = items[i]
            nq, nk = t["nq"], t["nk"]
            sm = small[0:nq, i % 4]
            act.wait_ge(mask_ok.sem, mask_ok.at(i + 1))
            if i >= 4:
                act.wait_ge(turn_ok.sem, turn_ok.at(i - 3))
            if t["sink"] is not None:
                act.activation(sm[:, 3:4], t["sink"], ACT.Exp, bias=sm[:, 1:2])
            act.activation(probs[0:nq, i % 4, 0:nk], masked[0:nq, i % 3, 0:nk], ACT.Exp, bias=sm[:, 1:2],
                           accum_out=sm[:, 2:3]).then_inc(exp_ok.sem, 1)

        def do_copy(i):
            t = items[i]
            act.wait_ge(turn_ok.sem, turn_ok.at(i + 1))
            if i >= 3:
                act.wait_ge(head_ok.sem, head_ok.at(i - 2))
            bank = p.ps[:, 3 + i % 3, 0:3 * P].rearrange("p (n t) -> p n t", t=P)
            runs, n = [], 0
            while n < len(t["tiles"]):
                m = n + 1
                while m < len(t["tiles"]) and t["tiles"][m][1] == t["tiles"][n][1]:
                    m += 1
                runs.append((n, m, t["tiles"][n][1]))
                n = m
            for r, (n, m, rows) in enumerate(runs):
                ins = act.activation(turned_p[0:rows, i % 3, n:m, 0:t["nq"]], bank[0:rows, n:m, 0:t["nq"]], ACT.Copy)
                if r == len(runs) - 1:
                    ins.then_inc(tcopy_ok.sem, 1)

        def do_out(i):
            t = items[i]
            act.wait_ge(head_ok.sem, head_ok.at(i + 1))
            act.activation(t["out"][0], p.ps[t["part"]:t["part"] + 64, 6 + i % 2, 0:t["nq"]], ACT.Copy).then_inc(high.sem, 1)

        for i in range(N + 4):
            if 3 <= i < N + 3:
                do_copy(i - 3)
            if i < N:
                do_exp(i)
            if i >= 4:
                do_out(i - 4)

    for s in (scores, mask_ok, exp_ok, prob_ok, turn_ok, tcopy_ok, head_ok, high, moved):
        s.close(N)
    p.stage_end()


TILES1 = ((0, 128), (128, 128))


def heads_256(q, k, v_tok, heads, mask, out, out0):
    items = []
    for h in range(heads):
        lo = 64 * (h % 2)
        for qt in range(2):
            items.append(dict(
                nq=P, nk=SEQ, tiles=TILES1, part=lo, sink=None, mask=None if mask is None else mask[:, qt * SEQ:(qt + 1) * SEQ],
                q=q[lo:lo + 64, h // 2, qt * P:(qt + 1) * P], k=k[lo:lo + 64, h // 2, 0:SEQ],
                v=[v_tok[:, n, 64 * h:64 * h + 64] for n in range(2)],
                out=[o[lo:lo + 64, out0 + h // 2, qt * P:(qt + 1) * P] for o in out]))
    return items


def layer_even(p):
    T = SEQ
    proj, at = p.area(p.a0, 24, T)
    padded, at = p.area(at, 4, T + A_CONV - 1)
    cat, at = p.area(at, 8, T)
    v_tok, at = p.area(at, 2, 512)
    x = norm(p, p.h, "norm_mix", 0, T)
    gemm(p, "ev_in", x, T, act_unit=take_copy(p, proj, T))
    p.stage_end()
    gb, gc, xc, q, k, v = (proj[:, 4 * i:4 * i + 4] for i in range(6))

    @p.block.vector
    def _(dve):
        dve.memset(padded[:, :, 0:A_CONV - 1], 0.0)
        p.dve_steps.link(dve, dve.tensor_tensor(padded[:, :, A_CONV - 1:], gc, xc, ALU.mult))
        for c in range(4):
            w = lambda j: p.par("ev_conv", j * 4 + c)
            p.dve_steps.link(dve, dve.tensor_scalar(cat[:, c], padded[:, c, 0:T], w(0), None, ALU.mult))
            for j in range(1, A_CONV):
                p.dve_steps.link(dve, dve.scalar_tensor_tensor(cat[:, c], padded[:, c, j:j + T], w(j), cat[:, c], ALU.mult, ALU.add))
        dve.tensor_tensor(cat[:, 0:4], cat[:, 0:4], gb, ALU.mult)

    head_norm(p, proj[:, 12:20], [p.par("ev_q_norm")] * 4 + [p.par("ev_k_norm")] * 4, T, 2, 1.0 / B_DIM, EPS)
    to_tokens(p, v, 4, TILES1, v_tok)
    cat_split = (p.high, p.low)
    attention(p, heads_256(q, k, v_tok, B_HEADS, p.con("dilated"), cat_split, 4), B_DIM ** -0.5, at)
    split_activations(p, cat, 4, T)
    gemm(p, "ev_out", [cat_split], T, dve_unit=take_add(p, p.h, T, 2))
    p.stage_end()


def memory_heads(p, layer):
    T = SEQ
    kv, at = p.area(p.a0, 4, T)
    x = norm(p, p.mem, "norm_mem", KD * layer, T)
    gemm(p, f"xa_kv{layer}", x, T, act_unit=take_copy(p, kv, T))
    p.stage_end()
    k = p.mem_k[:, 2 * layer:2 * layer + 2]

    @p.block.scalar
    def _(act):
        p.act_steps.link(act, act.activation(k, kv[:, 0:2], ACT.Copy))

    head_norm(p, k, [p.par("xa_k_norm", layer)] * 2, T, 2, 1.0 / 64, EPS)
    to_tokens(p, kv[:, 2:4], 2, TILES1, p.mem_v[:, 2 * layer:2 * layer + 2])


def cross_attention(p, layer):
    T = SEQ
    q, at = p.area(p.a0, 2, T)
    x = norm(p, p.h, "norm_xattn", KD * layer, T)
    gemm(p, f"xa_q{layer}", x, T, act_unit=take_copy(p, q, T))
    p.stage_end()
    head_norm(p, q, [p.par("xa_q_norm", layer)] * 2, T, 2, 1.0 / 64, EPS)
    items = heads_256(q, p.mem_k[:, 2 * layer:2 * layer + 2], p.mem_v[:, 2 * layer:2 * layer + 2], X_HEADS,
                      None, x[0], 0)
    attention(p, items, 64 ** -0.5, at)
    gemm(p, f"xa_o{layer}", x, T, dve_unit=take_add(p, p.h, T, 2))
    p.stage_end()


def gated_hidden(p, hidden, silu, prod, kt, weight=None):
    T = SEQ
    gated, product, high = p.counted("gate_ready"), p.counted("product_ready"), p.counted("high_ready")
    up = p.counted("up_ready")

    def act_unit(act, i, u, j, bank):
        if j >= kt:
            return
        act.activation(silu[:, j % 2], bank[:, 0], ACT.Silu).then_inc(gated.sem, 1)
        act.wait_ge(product.sem, u + product.at(1))
        act.activation(chunk(0, u, j), prod[:, j % 2], ACT.Copy).then_inc(high.sem, 1)

    def chunk(part, u, j):
        return (at_dyn(hidden[part], u, 1) if weight is None else hidden[part][:, j:j + 1])[:, 0]

    def dve_unit(dve, i, u, j, bank):
        top = bank[:, 1]
        if weight is not None:
            dve.tensor_tensor(prod[:, j % 2], top, at_dyn(weight, i, 1)[:, 0], ALU.mult).then_inc(up.sem, 1)
            dve.wait_ge(up.sem, u + up.at(1))
            top = prod[:, j % 2]
        dve.wait_ge(gated.sem, u + gated.at(1))
        dve.tensor_tensor(prod[:, j % 2], silu[:, j % 2], top, ALU.mult).then_inc(product.sem, 1)
        dve.wait_ge(high.sem, u + high.at(1))
        dve.tensor_tensor(chunk(1, u, j), prod[:, j % 2], chunk(0, u, j).bitcast(F32), ALU.subtract).then_inc(p.unit_free, 1)

    return act_unit, dve_unit


def dense_ffn(p):
    T, kt = SEQ, D_FF // P
    hidden, at = p.split_area(p.a0, kt, T)
    silu, at = p.area(at, 2, T)
    prod, at = p.area(at, 2, T)
    x = norm(p, p.h, "norm_ffn", 0, T)
    act_unit, dve_unit = gated_hidden(p, hidden, silu, prod, kt)
    gemm(p, "ff_gu", x, T, act_unit, dve_unit, [("gate_ready", kt), ("product_ready", kt), ("high_ready", kt)])
    p.stage_end()
    gemm(p, "ff_down", [hidden], T, dve_unit=take_add(p, p.h, T, 1))
    p.stage_end()


def conv_silu(p, name, dst, T, weights, w0, n_chunks, bias, b0, units, at):
    padded, at = p.area(at, 4, T + 3)
    acc, at = p.area(at, 4, T)
    step = p.counted("conv_step")
    unit_base = p.plan[name][0].unit_base

    @p.block.vector
    def _(dve):
        p.dve_steps.link(dve, dve.memset(padded[:, :, 0:3], 0.0))

    def act_unit(act, i, u, j, bank):
        b = 2 * (j % 2)
        act.activation(padded[:, b:b + 2, 3:3 + T], bank, ACT.Copy)
        for c in range(2):
            w = p.par_dyn(weights, 2 * u + (w0 + 3 * n_chunks + c))
            if bias is None:
                ins = act.activation(acc[:, b + c], bank[:, c], ACT.Copy, scale=w)
            else:
                ins = act.activation(acc[:, b + c], bank[:, c], ACT.Identity, scale=w, bias=p.par_dyn(bias, 2 * u + (b0 + c)))
        ins.then_inc(p.unit_free, 1)

    def act_late(act, u, j):
        b = 2 * (j % 2)
        act.wait_ge(step.sem, 6 * u + step.at(6))
        act.activation(at_dyn(dst, 2 * u, 2)[:, :, 0:T], acc[:, b:b + 2], ACT.Silu)

    def dve_unit(dve, i, u, j, bank):
        b = 2 * (j % 2)
        dve.wait_ge(p.unit_free, u + (unit_base + 1))
        for t in range(3):
            for c in range(2):
                if t:
                    dve.wait_ge(step.sem, 6 * u + step.at(2 * t + c - 1))
                w = p.par_dyn(weights, 2 * u + (w0 + t * n_chunks + c))
                dve.scalar_tensor_tensor(acc[:, b + c], padded[:, b + c, t:t + T], w, acc[:, b + c], ALU.mult, ALU.add).then_inc(step.sem, 1)

    return dict(act_unit=act_unit, dve_unit=dve_unit, signals=[("conv_step", 6 * units)], act_late=act_late)


def layer_odd(p):
    T, H = SEQ, C_HEADS
    qkv, at = p.area(p.a0, 24, T)
    x = norm(p, p.h, "norm_mix", KD, T)
    rows, at = p.area(at, 8, T)
    top = at
    small_ok = p.counted("small_ready")
    beta, gcum, *t = (rows[0:H, i] for i in range(7))
    na = rows[0:H, 7, 0:1]

    @p.block.tensor
    def _(pe):
        for s in range(2):
            for k in range(KD):
                mm = pe.matmul(p.ps[0:H, 6 + s, 0:T], p.par("od_small", 16 * k + 8 * s, 8), p.u[:, k, 0:T], start=(k == 0), stop=(k == KD - 1))
        mm.then_inc(small_ok.sem, 1)

    def decays():
        softplus_rows(p, p.ps[0:H, 7, 0:T], p.par("od_dt_bias")[0:H], p.par("od_a_log")[0:H], t, na,
                      also=(beta, p.ps[0:H, 6, 0:T]))

        @p.block.vector
        def _(dve):
            p.dve_steps.link(dve, dve.tensor_scalar(t[0], t[1], na, -1.0, ALU.mult, ALU.mult))
            for c in range(2):
                s = slice(c * DELTA_CHUNK, (c + 1) * DELTA_CHUNK)
                dve.tensor_tensor_scan(gcum[:, s], t[0][:, s], t[0][:, s], 0.0, ALU.add, ALU.bypass)

    conv = conv_silu(p, "od_in", qkv, T, "od_conv", 0, 24, None, 0, 12, top)
    first_round, rest = split_segment(p.plan["od_in"][0], 1)
    qkv_rest, gate_round = split_segment(rest, 2)
    qkv_rest.unit0 = len(rest.units)
    p.plan["od_qkv"], p.plan["od_gate"] = [first_round, qkv_rest], [gate_round]
    gemm(p, "od_qkv", x, T, **conv, beside=decays)
    p.stage_end()
    q, k, v = qkv[:, 0:8], qkv[:, 8:16], qkv[:, 16:24]
    head_norm(p, qkv[:, 0:16], [C_DIM ** -0.5] * 8 + [1.0] * 8, T, 1, 1.0, EPS)
    out, at = p.area(top, 8, T)
    state, at = p.area(at, 8, C_DIM)
    cols, at = p.area(at, 2, 5, H)
    keep = at
    for c in range(2):
        delta_chunk(p, c, q, k, v, beta, gcum, out, cols[:, c], state, keep)
    head_norm(p, out, [p.par("od_o_norm")] * 8, T, 1, 1.0 / C_DIM, EPS)
    gate, _ = p.area(keep, 8, T)
    gemm(p, "od_gate", x, T, act_unit=take_copy(p, gate, T, func=ACT.Silu), dve_unit=gate_in(p, "od_gate", out, gate, T))
    p.stage_end()
    x = split_activations(p, out, 8, T)
    gemm(p, "od_out", x, T, dve_unit=take_add(p, p.h, T, 2))
    p.stage_end()


def softplus_rows(p, bank, bias, a_log, t, na, also=None):
    ready, args, tables = p.counted("small_ready"), p.counted("softplus_arg_ready"), p.counted("softplus_table_ready")

    @p.block.vector
    def _(dve):
        link = p.dve_steps.link
        dve.wait_ge(ready.sem, ready.at(1))
        link(dve, dve.tensor_scalar(t[0], bank, bias, None, ALU.add))
        link(dve, dve.tensor_scalar(t[1], t[0], -1.0, None, ALU.mult))
        dve.tensor_tensor(t[1], t[0], t[1], ALU.min).then_inc(args.sem, 1)
        dve.wait_ge(tables.sem, tables.at(1))
        dve.tensor_scalar(t[2], t[1], 1.0, None, ALU.add).then_inc(args.sem, 1)
        dve.wait_ge(tables.sem, tables.at(2))
        link(dve, dve.scalar_tensor_tensor(t[4], t[2], -1.0, t[1], ALU.add, ALU.subtract))
        link(dve, dve.reciprocal(t[2], t[2]))
        link(dve, dve.tensor_tensor(t[4], t[4], t[2], ALU.mult))
        link(dve, dve.tensor_tensor(t[3], t[3], t[4], ALU.subtract))
        link(dve, dve.scalar_tensor_tensor(t[1], t[0], 0.0, t[3], ALU.max, ALU.add))

    @p.block.scalar
    def _(act):
        act.wait_ge(ready.sem, ready.at(1))
        if also is not None:
            act.activation(also[0], also[1], ACT.Sigmoid)
        act.activation(na, a_log, ACT.Exp)
        act.wait_ge(args.sem, args.at(1))
        act.activation(t[1], t[1], ACT.Exp).then_inc(tables.sem, 1)
        act.wait_ge(args.sem, args.at(2))
        act.activation(t[3], t[2], ACT.Ln).then_inc(tables.sem, 1)

    ready.close(1)
    args.close(2)
    tables.close(2)


def delta_chunk(p, c, q, k, v, beta, gcum, out, cols, state, at):
    H, n = C_HEADS, DELTA_CHUNK
    tok = slice(c * n, (c + 1) * n)
    big = lambda a: p.area(a, H, n)
    R, at = big(at)
    DT, at = big(at)
    X, at = big(at)
    Tm, at = big(at)
    Um, at = big(at)
    NT, at = big(at)
    CT, at = big(at)
    S = state[:, :, 0:C_DIM]
    banks = lambda b, m=2: p.ps[:, b:b + m, :].rearrange("p b (h t) -> p (b h) t", t=n)
    pe_ok, act_ok, dve_ok = p.counted("products_ready"), p.counted("scalar_ready"), p.counted("vector_ready")
    beta_t, gc_t, eg, edec, bg = (cols[:, i] for i in range(5))
    qT, kT, vT = q[:, :, tok], k[:, :, tok], v[:, :, tok]
    b3 = lambda x: x[:, :, None].to_broadcast([P, H, n])
    L, G = DELTA_LEVELS, H // 2
    groups = [slice(g * G, (g + 1) * G) for g in range(2)]
    pe_end, act_end, dve_end = 2 + 4 * L, 1 + 2 * L, 3 + 4 * L

    @p.block.tensor
    def _(pe):
        pe.transpose(p.ps[0:n, 6, 0:H], beta[:, tok], p.con("ident", n=H, rows=H))
        pe.transpose(p.ps[0:n, 6, H:2 * H], gcum[:, tok], p.con("ident", n=H, rows=H))
        for h in range(H):
            pick = p.con("ident", first=h, n=1, rows=H).to_broadcast([H, P])
            pe.matmul(banks(0)[:, h], pick, gcum[:, tok], start=True, stop=True)
        for h in range(H):
            pick = p.con("ident", first=h, n=1, rows=H).to_broadcast([H, P])
            mm = pe.matmul(banks(2)[:, h], pick, beta[:, tok], start=True, stop=True)
        mm.then_inc(pe_ok.sem, 1)
        pe.wait_ge(dve_ok.sem, dve_ok.at(2))
        for h in range(H):
            mm = pe.matmul(banks(4)[:, h], kT[:, h], X[:, h], start=True, stop=True)
        mm.then_inc(pe_ok.sem, 1)
        for l in range(L):
            for g in range(2):
                pe.wait_ge(dve_ok.sem, dve_ok.at(4 + 4 * l + g))
                for h in range(g * G, (g + 1) * G):
                    mm = pe.matmul(banks(0)[:, h], CT[:, h], Tm[:, h], start=True, stop=True)
                mm.then_inc(pe_ok.sem, 1)
            for g in range(2):
                pe.wait_ge(act_ok.sem, act_ok.at(2 + 2 * l + g))
                for h in range(g * G, (g + 1) * G):
                    pe.matmul(banks(2)[:, h], Um[:, h], X[:, h], start=True, stop=True)
                    mm = pe.matmul(banks(4)[:, h], X[:, h], Um[:, h], start=True, stop=True)
                mm.then_inc(pe_ok.sem, 1)
        pe.wait_ge(dve_ok.sem, dve_ok.at(dve_end))
        for h in range(H):
            pe.transpose(banks(0)[:, h], vT[:, h], p.con("ident"))
        for h in range(H):
            pe.transpose(banks(2)[:, h], kT[:, h], p.con("ident"))
        for h in range(H):
            mm = pe.matmul(banks(4)[:, h], kT[:, h], qT[:, h], start=True, stop=True)
        mm.then_inc(pe_ok.sem, 1)
        if c:
            pe.wait_ge(dve_ok.sem, dve_ok.at(dve_end + 1))
            for h in range(H):
                mm = pe.matmul(banks(0)[:, h], CT[:, h], Um[:, h], start=True, stop=True)
            mm.then_inc(pe_ok.sem, 1)
            pe.wait_ge(act_ok.sem, act_ok.at(act_end + 1))
        else:
            pe.wait_ge(dve_ok.sem, dve_ok.at(dve_end + 1))
        for h in range(H):
            mm = pe.matmul(banks(2)[:, h], Um[:, h], X[:, h], start=True, stop=(c == 0))
            if c:
                mm = pe.matmul(banks(2)[:, h], NT[:, h], S[:, h], start=False, stop=True)
        mm.then_inc(pe_ok.sem, 1)
        pe.wait_ge(act_ok.sem, act_ok.at(act_end + 1 + c))
        for h in range(H):
            mm = pe.matmul(banks(4)[:, h], Tm[:, h], DT[:, h], start=True, stop=(c == 0))
            if c:
                mm = pe.matmul(banks(4)[:, h], S[:, h], CT[:, h], start=False, stop=True)
        if c == 0:
            for h in range(H):
                mm = pe.matmul(banks(0)[:, h], CT[:, h], Tm[:, h], start=True, stop=True)
        mm.then_inc(pe_ok.sem, 1)

    @p.block.vector
    def _(dve):
        link = p.dve_steps.link
        dve.wait_ge(pe_ok.sem, pe_ok.at(1))
        dve.tensor_copy(beta_t, p.ps[:, 6, 0:H])
        link(dve, dve.tensor_copy(gc_t, p.ps[:, 6, H:2 * H]))
        link(dve, dve.tensor_copy(R, banks(0)))
        link(dve, dve.tensor_tensor(edec, R[:, :, n - 1:n].rearrange("p h t -> p (h t)"), gc_t, ALU.subtract))
        link(dve, dve.tensor_tensor(DT, R, b3(gc_t), ALU.subtract))
        dve.tensor_tensor(DT, DT, p.con("below")[:, None, :].to_broadcast([P, H, n]), ALU.add).then_inc(dve_ok.sem, 1)
        dve.tensor_tensor(X, kT, banks(2), ALU.mult).then_inc(dve_ok.sem, 1)
        for m in (Tm, Um):
            link(dve, dve.tensor_copy(m, p.con("ident")[:, None, :].to_broadcast([P, H, n])))
        dve.wait_ge(act_ok.sem, act_ok.at(1))
        dve.tensor_tensor(bg, beta_t, eg, ALU.mult)
        dve.wait_ge(pe_ok.sem, pe_ok.at(2))
        dve.tensor_tensor(NT, banks(4), DT, ALU.mult).then_inc(dve_ok.sem, 1)

        def level_ct(l, g):
            level = p.con("levels", l * P, P)[:, None, :].to_broadcast([P, G, n])
            dve.tensor_tensor(CT[:, groups[g]], NT[:, groups[g]], level, ALU.mult).then_inc(dve_ok.sem, 1)

        dve.wait_ge(dve_ok.sem, dve_ok.at(3))
        for g in range(2):
            level_ct(0, g)
        for l in range(L):
            for g in range(2):
                if l + 1 < L:
                    dve.wait_ge(pe_ok.sem, pe_ok.at(2 + 4 * l + 1 + g))
                    level_ct(l + 1, g)
            for g, hs in enumerate(groups):
                dve.wait_ge(pe_ok.sem, pe_ok.at(2 + 4 * l + 3 + g))
                dve.tensor_tensor(Tm[:, hs], Tm[:, hs], banks(2)[:, hs], ALU.subtract)
                dve.tensor_tensor(Um[:, hs], Um[:, hs], banks(4)[:, hs], ALU.subtract).then_inc(dve_ok.sem, 1)
        dve.wait_ge(pe_ok.sem, pe_ok.at(pe_end + 1))
        dve.tensor_tensor(X, banks(0), b3(beta_t), ALU.mult)
        if c == 0:
            dve.tensor_tensor(CT, banks(2), b3(edec), ALU.mult)
        else:
            dve.tensor_tensor(CT, banks(2), b3(bg), ALU.mult)
        dve.tensor_tensor(DT, banks(4), DT, ALU.mult).then_inc(dve_ok.sem, 1)
        if c:
            dve.wait_ge(pe_ok.sem, pe_ok.at(pe_end + 2))
            dve.tensor_tensor(CT, qT, R, ALU.mult).then_inc(dve_ok.sem, 1)
        dve.wait_ge(pe_ok.sem, pe_ok.at(pe_end + 3 + c))
        dve.tensor_copy(out[:, :, tok], banks(4))
        if c == 0:
            dve.tensor_copy(S, banks(0))

    @p.block.scalar
    def _(act):
        act.wait_ge(dve_ok.sem, dve_ok.at(1))
        act.activation(DT, DT, ACT.Exp)
        act.activation(edec, edec, ACT.Exp)
        act.activation(R, R, ACT.Exp)
        act.activation(eg, gc_t, ACT.Exp).then_inc(act_ok.sem, 1)
        for l in range(L):
            for g, hs in enumerate(groups):
                act.wait_ge(pe_ok.sem, pe_ok.at(2 + 4 * l + 1 + g))
                act.activation(X[:, hs], banks(0)[:, hs], ACT.Copy).then_inc(act_ok.sem, 1)
        if c:
            act.wait_ge(pe_ok.sem, pe_ok.at(pe_end + 2))
            act.activation(NT, banks(0), ACT.Copy, scale=-1.0).then_inc(act_ok.sem, 1)
            act.wait_ge(dve_ok.sem, dve_ok.at(dve_end + 2))
        act.wait_ge(pe_ok.sem, pe_ok.at(pe_end + 2 + c))
        act.activation(Tm, banks(2), ACT.Copy).then_inc(act_ok.sem, 1)

    pe_ok.close(pe_end + 3 + c)
    act_ok.close(act_end + 1 + c)
    dve_ok.close(dve_end + 1 + c)
    p.stage_end()


def moe(p):
    T, E = SEQ, N_EXPERTS
    combine, at = p.area(p.a0, E, T)
    hidden, at = p.split_area(at, D_FFE // P, T)
    silu, at = p.area(at, 2, T)
    prod, at = p.area(at, 2, T)
    lg, at = p.area(at, 2, 8 * 8)
    comb_rows, at = p.area(at, 1, T)
    x = norm(p, p.h, "norm_ffn", KD, T)
    logits, diffs, exps, weighed, rows_ok = (p.counted(s) for s in ("logits_ready", "logit_gaps_ready", "router_exp_ready", "weights_ready", "weight_rows_ready"))

    @p.block.tensor
    def _(pe):
        for i in range(2):
            for k in range(KD):
                mm = pe.matmul(p.ps[:, 4 + i, 0:E], p.u[:, k, i * P:(i + 1) * P], p.par("router", 8 * k, 8), start=(k == 0), stop=(k == KD - 1))
            mm.then_inc(logits.sem, 1)
        keep_clock(p, pe, 40)
        pe.wait_ge(weighed.sem, weighed.at(2))
        for i in range(2):
            mm = pe.transpose(p.ps[0:E, 6, i * P:(i + 1) * P], lg[:, i, 56:64], p.con("ident"))
        mm.then_inc(logits.sem, 1)
        pe.wait_ge(rows_ok.sem, rows_ok.at(1))
        for e in range(E):
            mm = pe.matmul(p.ps[:, e, 0:T], p.con("ident", first=e, n=1, rows=E).to_broadcast([E, P]), comb_rows[0:E, 0], start=True, stop=True)
        mm.then_inc(logits.sem, 1)

    @p.block.vector
    def _(dve):
        link = p.dve_steps.link
        for i in range(2):
            x, top, idx = lg[:, i, 0:8], lg[:, i, 8:16], lg[:, i, 16:24]
            diff = lg[:, i, 24:25]
            dve.wait_ge(logits.sem, logits.at(i + 1))
            link(dve, dve.tensor_copy(x, p.ps[:, 4 + i, 0:E]))
            link(dve, dve.max(top, x))
            link(dve, dve.max_index(p.indices[:, i], top, x))
            link(dve, dve.tensor_copy(idx, p.indices[:, i]))
            dve.tensor_tensor(diff, top[:, 1:2], top[:, 0:1], ALU.subtract).then_inc(diffs.sem, 1)
        for i in range(2):
            idx, w1, w2 = lg[:, i, 16:24], lg[:, i, 25:26], lg[:, i, 26:27]
            dve.wait_ge(exps.sem, exps.at(i + 1))
            link(dve, dve.tensor_scalar(w1, w2, 1.0, None, ALU.add))
            link(dve, dve.reciprocal(w1, w1))
            link(dve, dve.tensor_tensor(w2, w2, w1, ALU.mult))
            a, b = lg[:, i, 32:40], lg[:, i, 40:48]
            dve.tensor_scalar(a, p.con("iota"), idx[:, 0:1], w1, ALU.is_equal, ALU.mult)
            link(dve, dve.tensor_scalar(b, p.con("iota"), idx[:, 1:2], w2, ALU.is_equal, ALU.mult))
            dve.tensor_tensor(lg[:, i, 56:64], a, b, ALU.add).then_inc(weighed.sem, 1)

    @p.block.scalar
    def _(act):
        for i in range(2):
            act.wait_ge(diffs.sem, diffs.at(i + 1))
            act.activation(lg[:, i, 26:27], lg[:, i, 24:25], ACT.Exp).then_inc(exps.sem, 1)
        act.wait_ge(logits.sem, logits.at(3))
        act.activation(comb_rows[0:E, 0], p.ps[0:E, 6, 0:T], ACT.Copy).then_inc(rows_ok.sem, 1)
        act.wait_ge(logits.sem, logits.at(4))
        act.activation(combine, p.ps[:, :, 0:T], ACT.Copy)

    logits.close(4)
    diffs.close(2)
    exps.close(2)
    weighed.close(2)
    rows_ok.close(1)
    p.stage_end()

    seg = p.plan["moe"][0]
    kt, nu = D_FFE // P, len(seg.units)
    act_unit, gate_dve = gated_hidden(p, hidden, silu, prod, kt, combine)
    def act_fn(act, i, u, j, bank):
        if j < kt:
            act_unit(act, i, i * kt + j, j, bank)

    def dve_fn(dve, i, u, j, bank):
        if j < kt:
            gate_dve(dve, i, i * kt + j, j, bank)
        else:
            m = j - kt
            dve.tensor_tensor(p.h[:, m, 0:T], bank[:, 0], p.h[:, m, 0:T], ALU.add).then_inc(p.unit_free, 1)

    def before(pe, i, j, k):
        if j == kt and k >= kt - 2:
            pe.wait_ge(p.unit_free, i * nu + (seg.unit_base + k + 1))

    n = kt * N_EXPERTS
    gemm(p, "moe", [x[0], hidden], T, act_fn, dve_fn, [("gate_ready", n), ("product_ready", n), ("high_ready", n), ("up_ready", n)],
         pair=lambda j: moe_pair(j, kt, nu), before=before)
    p.stage_end()


def moe_pair(j, kt, nu):
    return 2 if j == nu - 1 else j % 2


def layer_two(p, l):
    T = L2
    xs, at = p.area(p.a0, 32, T)
    rows, at = p.area(at, 2, T)
    at_q = at
    x = norm(p, p.h, "norm1", KD * l, T)
    small_ok = p.counted("small_ready")
    H = SSD_HEADS
    dt, acum = rows[0:H, 0], rows[0:H, 1]
    tmp, _ = p.area(at_q + 8 * T + 16, 5, T)
    t = [tmp[0:H, 0], dt, tmp[0:H, 1], tmp[0:H, 2], tmp[0:H, 3]]
    na = tmp[0:H, 4, 0:1]

    @p.block.tensor
    def _(pe):
        for k in range(KD):
            mm = pe.matmul(p.ps[0:H, 7, 0:T], p.par("w_dt", (l * KD + k) * H, H), p.u[:, k, 0:T], start=(k == 0), stop=(k == KD - 1))
        mm.then_inc(small_ok.sem, 1)

    def decays():
        softplus_rows(p, p.ps[0:H, 7, 0:T], p.par("dt_bias", l)[0:H], p.par("a_log", l)[0:H], t, na)

        @p.block.vector
        def _(dve):
            p.dve_steps.link(dve, dve.tensor_scalar(t[0], dt, na, -1.0, ALU.mult, ALU.mult))
            for o, n in CHUNKS2:
                dve.tensor_tensor_scan(acum[:, o:o + n], t[0][:, o:o + n], t[0][:, o:o + n], 0.0, ALU.add, ALU.bypass)

    conv = conv_silu(p, f"xbc{l}", xs, T, "conv_w", l * CONV2 * 32, 32, "conv_b", l * 32, 16, at_q)
    first_round, rest = split_segment(p.plan[f"xbc{l}"][0], 1)
    rest.unit0 = len(rest.units)
    p.plan[f"xbc{l}"] = [first_round, rest]
    gemm(p, f"xbc{l}", x, T, **conv, beside=decays)
    p.stage_end()
    ssd(p, l, xs, dt, acum, at_q)
    y = xs[:, 0:16]
    z, at = p.area(p.a0 + 16 * T, 16, T)
    q, at = p.area(p.a0 + 48 * T, 8, T)
    kv, at = p.area(at, 4, T)
    gates, at = p.area(at, 16, T)
    gemm(p, f"z{l}", x, T, act_unit=take_copy(p, z, T, func=ACT.Silu), dve_unit=gate_in(p, f"z{l}", y, z, T))
    gemm(p, f"q{l}", x, T, act_unit=take_copy(p, q, T))
    gemm(p, f"kv{l}", x, T, act_unit=take_copy(p, kv, T))

    def gate_unit(act, i, u, j, bank):
        for c in range(2):
            ins = act.activation(at_dyn(gates, 2 * u + c, 1)[:, 0], bank[:, c], ACT.Sigmoid, bias=p.par_dyn("b_gate", 2 * u + (l * 16 + c)))
        ins.then_inc(p.unit_free, 1)

    gemm(p, f"gate{l}", x, T, act_unit=gate_unit)
    p.stage_end()
    y_split, _ = p.split_area(p.a0 + 16 * T, 16, T)
    head_norm(p, y, [p.par("ssd_norm", l * 16 + c) for c in range(16)], T, 1, 1.0 / 256, EPS, group=2, split=y_split)
    x = [y_split]
    merged, _ = p.area(p.a0, 8, T)

    def gated_unit(dve, i, u, j, bank):
        dve.tensor_tensor(at_dyn(merged, u, 1), bank, at_dyn(gates, u, 1), ALU.mult).then_inc(p.unit_free, 1)

    gemm(p, f"ssd_down{l}", x, T, dve_unit=gated_unit)
    p.stage_end()

    at = p.a0 + 8 * T
    kd, at = p.area(at, 4, T)
    v_tok, at = p.area(at, 3, 256)
    rot, at = p.area(at, 2, T)
    k = kv[:, 0:2]
    qk, _ = p.area(p.a0 + 48 * T, 10, T)
    head_norm(p, qk, [p.par("q_norm", l)] * 8 + [p.par("k_norm", l)] * 2, T, 2, 1.0 / 64, EPS)
    rotary(p, qk, 10, T)

    @p.block.scalar
    def _(act):
        for h in range(KV_HEADS):
            lo = 64 * (h % 2)
            for half in range(2):
                act.activation(kd[64 * half:64 * half + 64, h], k[lo:lo + 64, h // 2], ACT.Copy)

    to_tokens(p, kv[:, 2:4], 2, CHUNKS2, v_tok)
    items = []
    for h in range(ATTN_HEADS):
        lo, g = 64 * (h % 2), h // 4
        for i, (first, nq) in enumerate(CHUNKS2):
            nk = first + nq
            items.append(dict(
                nq=nq, nk=nk, tiles=CHUNKS2[:i + 1], part=lo, sink=p.par("sinks", l * 16 + h)[0:nq],
                mask=p.con("window", i * L2, nk, rows=nq), q=q[lo:lo + 64, h // 2, first:first + nq], k=kd[lo:lo + 64, g, 0:nk],
                v=[v_tok[0:m, n, 64 * g:64 * g + 64] for n, (_, m) in enumerate(CHUNKS2[:i + 1])],
                out=[o[lo:lo + 64, h // 2, first:first + nq] for o in (p.high, p.low)]))
    attention(p, items, ATTN_DIM ** -0.5, at)
    product = p.counted("gated_product_ready")

    def merge_unit(dve, i, u, j, bank):
        dve.tensor_tensor(rot, bank, gates[:, 2 * u + 8:2 * u + 10], ALU.mult).then_inc(product.sem, 1)
        dve.wait_ge(product.sem, product.at(u + 1))
        m = merged[:, 2 * u:2 * u + 2]
        dve.tensor_tensor(m, m, rot, ALU.add).then_inc(p.unit_free, 1)
        dve.wait_ge(p.unit_free, p.plan[f"attn_down{l}"][0].unit_base + u + 1)

    gemm(p, f"attn_down{l}", [(p.high, p.low)], T, dve_unit=merge_unit, signals=[("gated_product_ready", 4)])
    p.stage_end()
    x = split_activations(p, merged, 8, T)
    gemm(p, f"w_o{l}", x, T, dve_unit=take_add(p, p.h, T, 2))
    p.stage_end()


def rotary(p, x, n, T):
    swapped, rotated = p.counted("swapped"), p.counted("rotated")
    tmp = p.work[:, 0:4 * T].rearrange("p (k t) -> p k t", t=T)
    pairs = n // 2

    @p.block.tensor
    def _(pe):
        for b in range(pairs):
            if b >= 4:
                pe.wait_ge(rotated.sem, rotated.at(b - 3))
            for c in range(2):
                mm = pe.matmul(p.ps[:, 2 * (b % 4) + c, 0:T], p.con("swap"), x[:, 2 * b + c], start=True, stop=True)
            mm.then_inc(swapped.sem, 1)

    @p.block.vector
    def _(dve):
        wide = lambda name: p.con(name)[:, None, :].to_broadcast([P, 2, T])
        for b in range(pairs):
            pair = x[:, 2 * b:2 * b + 2]
            dve.wait_ge(swapped.sem, swapped.at(b + 1))
            t = tmp[:, 2 * (b % 2):2 * (b % 2) + 2]
            dve.tensor_tensor(t, p.ps[:, 2 * (b % 4):2 * (b % 4) + 2, 0:T], wide("sin"), ALU.mult).then_inc(rotated.sem, 1)
            p.dve_steps.link(dve, dve.tensor_tensor(pair, pair, wide("cos"), ALU.mult))
            dve.tensor_tensor(pair, pair, t, ALU.add)

    swapped.close(pairs)
    rotated.close(pairs)
    p.stage_end()


def ssd(p, l, xs, dt, acum, at):
    H, R, G = SSD_HEADS, SSD_R, SSD_GROUPS
    state, at = p.area(at, H * SSD_P)
    xdt, at = p.area(at, H * SSD_P)
    xdec = p.work[:, 0:H * SSD_P]
    b_tok, at = p.area(at, G * P)
    cols, at = p.area(at, 5, H)
    arg, at = p.area(at, 2, R, P)
    eR, at = p.area(at, 2, R, P)
    mt, at = p.area(at, 2, R, P)
    dt_t, ac_t, dec, gl, dd = (cols[:, i] for i in range(5))
    B, C = xs[:, 16:24], xs[:, 24:32]
    pe_ok, act_ok, dve_ok = p.counted("products_ready"), p.counted("scalar_ready"), p.counted("vector_ready")

    for ci, (o, n) in enumerate(CHUNKS2):
        last = ci == 2
        @p.block.tensor
        def _(pe):
            pe.transpose(p.ps[0:n, 0, 0:H], dt[:, o:o + n], p.con("ident", n=H, rows=H))
            pe.transpose(p.ps[0:n, 0, H:2 * H], acum[:, o:o + n], p.con("ident", n=H, rows=H))
            pe.matmul(p.ps[:, 1, 0:H], acum[:, o + n - 1:o + n].to_broadcast([H, P]), p.con("ident", n=H, rows=H), start=True, stop=True).then_inc(pe_ok.sem, 1)
            for b in range(4):
                for c in range(4):
                    mm = pe.transpose(p.ps[0:n, 2 + b, c * P:(c + 1) * P], xs[:, 4 * b + c, o:o + n], p.con("ident"))
            mm.then_inc(pe_ok.sem, 1)
            for b in range(2):
                for c in range(4):
                    mm = pe.transpose(p.ps[0:n, 6 + b, c * P:(c + 1) * P], B[:, 4 * b + c, o:o + n], p.con("ident"))
            mm.then_inc(pe_ok.sem, 1)

        @p.block.vector
        def _(dve):
            link = p.dve_steps.link
            dve.wait_ge(pe_ok.sem, pe_ok.at(1))
            dve.tensor_copy(dt_t[0:n], p.ps[0:n, 0, 0:H])
            dve.tensor_copy(ac_t[0:n], p.ps[0:n, 0, H:2 * H])
            link(dve, dve.tensor_copy(gl, p.ps[:, 1, 0:H]))
            dve.tensor_tensor(dec[0:n], gl[0:n], ac_t[0:n], ALU.subtract).then_inc(dve_ok.sem, 1)
            dve.wait_ge(pe_ok.sem, pe_ok.at(2))
            wide = lambda x: x[:, :, None].to_broadcast([n, H, SSD_P])
            rows = lambda x: x[0:n].rearrange("p (h d) -> p h d", d=SSD_P)
            link(dve, dve.tensor_tensor(rows(xdt), p.ps[0:n, 2:6, :].rearrange("p b (h d) -> p (b h) d", d=SSD_P), wide(dt_t[0:n]), ALU.mult))
            if not last:
                dve.wait_ge(act_ok.sem, act_ok.at(1))
                dve.tensor_tensor(rows(xdec), rows(xdt), wide(dec[0:n]), ALU.mult)

        @p.block.scalar
        def _(act):
            act.wait_ge(dve_ok.sem, dve_ok.at(1))
            act.activation(dec[0:n], dec[0:n], ACT.Exp).then_inc(act_ok.sem, 1)
            act.activation(gl, gl, ACT.Exp)
            act.wait_ge(pe_ok.sem, pe_ok.at(3))
            act.activation(b_tok[0:n].rearrange("p (b t) -> p b t", t=512), p.ps[0:n, 6:8, :], ACT.Copy)

        pe_ok.close(3)
        dve_ok.close(1)
        act_ok.close(1)
        p.stage_end()
        decays, cbs, ys, sts = (p.counted(s) for s in ("decay_rows_ready", "cb_ready", "y_ready", "state_ready"))
        args, exps, mts, ctaken, ytaken = (p.counted(s) for s in ("decay_args_ready", "decay_exp_ready", "mt_ready", "c_scaled_ready", "y_taken"))

        @p.block.tensor
        def _(pe):
            def first(g):
                if g >= 2:
                    pe.wait_ge(exps.sem, exps.at(g - 1))
                    pe.wait_ge(mts.sem, mts.at(g - 1))
                for r in range(R):
                    mm = pe.matmul(p.ps[:, g % 2, r * P:r * P + n], p.con("ident", first=4 * g + r, n=1, rows=H).to_broadcast([H, P]),
                                   acum[:, o:o + n], start=True, stop=True)
                mm.then_inc(decays.sem, 1)
                pe.matmul(p.ps[0:n, 2 + g % 2, 0:n], B[:, g, o:o + n], C[:, g, o:o + n], start=True, stop=True).then_inc(cbs.sem, 1)

            def second(g):
                pe.wait_ge(mts.sem, mts.at(g + 1))
                if ci:
                    pe.wait_ge(ctaken.sem, ctaken.at(g + 1))
                if g >= 2:
                    pe.wait_ge(ytaken.sem, ytaken.at(g - 1))
                for r in range(R):
                    h = 4 * g + r
                    lo = 64 * (r % 2)
                    out = p.ps[lo:lo + 64, 4 + g % 2, (r // 2) * P:(r // 2) * P + n]
                    mm = pe.matmul(out, xdt[0:n, h * 64:(h + 1) * 64], mt[0:n, g % 2, r, 0:n], start=True, stop=(ci == 0))
                    if ci:
                        mm = pe.matmul(out, state[:, h * 64:(h + 1) * 64], eR[:, g % 2, r, 0:n], start=False, stop=True)
                if not last:
                    mm = pe.matmul(p.ps[:, 6 + g % 2, 0:256], b_tok[0:n, g * P:(g + 1) * P], xdec[0:n, g * 256:(g + 1) * 256], start=True, stop=True)
                mm.then_inc(ys.sem, 1)

            for g in range(G + 2):
                if g < G:
                    first(g)
                if g >= 2:
                    second(g - 2)

        @p.block.scalar
        def _(act):
            def early(g):
                act.wait_ge(decays.sem, decays.at(g + 1))
                if g >= 2:
                    act.wait_ge(ys.sem, ys.at(g - 1))
                bank = p.ps[:, g % 2, :].rearrange("p (r t) -> p r t", t=P)[:, :, 0:n]
                act.wait_ge(args.sem, args.at(g + 1))
                if ci:
                    act.activation(eR[:, g % 2, :, 0:n], bank, ACT.Exp)
                act.activation(arg[0:n, g % 2, :, 0:n], arg[0:n, g % 2, :, 0:n], ACT.Exp).then_inc(exps.sem, 1)

            for g in range(G):
                early(g)

        @p.block.vector
        def _(dve):
            def early(g):
                dve.wait_ge(decays.sem, decays.at(g + 1))
                bank = p.ps[0:n, g % 2, :].rearrange("p (r t) -> p r t", t=P)
                for r in range(R):
                    ins = dve.scalar_tensor_tensor(arg[0:n, g % 2, r, 0:n], bank[:, r, 0:n], ac_t[0:n, 4 * g + r:4 * g + r + 1],
                                                   p.con("below")[0:n, 0:n], ALU.subtract, ALU.add)
                ins.then_inc(args.sem, 1)

            def middle(g):
                dve.wait_ge(exps.sem, exps.at(g + 1))
                dve.wait_ge(cbs.sem, cbs.at(g + 1))
                cb = p.ps[0:n, 2 + g % 2, 0:n][:, None, :].to_broadcast([n, R, n])
                dve.tensor_tensor(mt[0:n, g % 2, :, 0:n], arg[0:n, g % 2, :, 0:n], cb, ALU.mult).then_inc(mts.sem, 1)
                if ci:
                    dve.tensor_tensor(eR[:, g % 2, :, 0:n], eR[:, g % 2, :, 0:n], C[:, g, o:o + n][:, None, :].to_broadcast([P, R, n]),
                                      ALU.mult).then_inc(ctaken.sem, 1)

            def late(g):
                dve.wait_ge(ys.sem, ys.at(g + 1))
                for c in range(2):
                    x = xs[:, 2 * g + c, o:o + n]
                    ins = dve.scalar_tensor_tensor(x, x, p.par("d_skip", l * 16 + 2 * g + c), p.ps[:, 4 + g % 2, c * P:c * P + n], ALU.mult, ALU.add)
                if not last:
                    st = state[:, g * 256:(g + 1) * 256]
                    new = p.ps[:, 6 + g % 2, 0:256]
                    if ci:
                        s4 = st.rearrange("p (r d) -> p r d", d=SSD_P)
                        p.dve_steps.link(dve, dve.tensor_tensor(s4, s4, gl[:, 4 * g:4 * g + 4][:, :, None].to_broadcast([P, R, SSD_P]), ALU.mult))
                        ins = dve.tensor_tensor(st, st, new, ALU.add)
                    else:
                        ins = dve.tensor_copy(st, new)
                ins.then_inc(ytaken.sem, 1)

            for g in range(G + 2):
                if 1 <= g <= G:
                    middle(g - 1)
                if g < G:
                    early(g)
                if g >= 2:
                    late(g - 2)

        for s in (decays, cbs, ys, args, exps, mts, ytaken):
            s.close(G)
        if ci:
            ctaken.close(G)
        if not last:
            p.stage_end()


def mlp_two(p, l):
    T = L2
    hidden, at = p.split_area(p.a0, FF2 // P, T)
    relu, at = p.area(at, 2, T)
    square, at = p.area(at, 4, T)
    x = norm(p, p.h, "norm2", KD * l, T)
    seg = p.plan[f"up{l}"][0]
    squared, high = p.counted("squares_ready"), p.counted("high_ready")

    def act_unit(act, i, u, j, bank):
        b = 2 * (j % 2)
        act.activation(relu, bank, ACT.Relu).then_inc(p.unit_free, 1)
        act.wait_ge(squared.sem, u + squared.at(1))
        act.activation(at_dyn(hidden[0], 2 * u, 2), square[:, b:b + 2], ACT.Copy).then_inc(high.sem, 1)

    def dve_unit(dve, i, u, j, bank):
        b = 2 * (j % 2)
        dve.wait_ge(p.unit_free, u + (seg.unit_base + 1))
        dve.tensor_tensor(square[:, b:b + 2], relu, relu, ALU.mult).then_inc(squared.sem, 1)
        dve.wait_ge(high.sem, u + high.at(1))
        dve.tensor_tensor(at_dyn(hidden[1], 2 * u, 2), square[:, b:b + 2], at_dyn(hidden[0], 2 * u, 2).bitcast(F32), ALU.subtract)

    gemm(p, f"up{l}", x, T, act_unit, dve_unit, [("squares_ready", 16), ("high_ready", 16)])
    p.stage_end()
    gemm(p, f"down{l}", [hidden], T, dve_unit=take_add(p, p.h, T, 1))
    p.stage_end()


def build(nc, weights, params, consts, x, mem, meta, out):
    with ExitStack() as ctx:
        p = Program(nc, ctx)
        p.mem_k, at = p.area(0, 4, SEQ)
        p.mem_v, at = p.area(at, 4, SEQ)
        first_a0 = at
        _, at = p.area(at, 4, SEQ)
        tok_in, at = p.area(at, 2, D)
        mem_in, at = p.area(at, 2, D)
        meta_tok, at = p.area(at, 1, D)
        p.mem, at = p.area(at, KD, SEQ)
        p.block = ctx.enter_context(nc.Block())
        n_small = p.con_at["dilated"][0]

        @p.block.sync
        def _(sp):
            sp.dma_start(mem_in, mem[0].rearrange("(i p) d -> p i d", p=P)).then_inc(p.mem_loaded, 16)
            sp.dma_start(p.consts[:, 0:n_small], consts[:, 0:n_small]).then_inc(p.mem_loaded, 16)
            sp.dma_start(p.params[:], params).then_inc(p.mem_loaded, 16)
            for seg in p.order[0:2]:
                for j, cols in enumerate(seg.slots):
                    sp.dma_start(p.ring[:, seg.ring[j], 0:cols], weights[seg.slot_base + j][:, 0:cols]).then_inc(p.full[seg.ring[j]], 16)
            sp.dma_start(tok_in, x[0].rearrange("(i p) d -> p i d", p=P)).then_inc(p.loaded, 16)
            sp.dma_start(meta_tok[0:N_META, 0], meta).then_inc(p.loaded, 16)
            sp.dma_start(p.consts[:, n_small:], consts[:, n_small:]).then_inc(p.loaded, 16)
            for seg in p.order[2:]:
                def body(i):
                    n = len(seg.slots)
                    for j, cols in enumerate(seg.slots):
                        s = seg.ring[j]
                        if seg.ring_free0[j] > 0:
                            sp.wait_ge(p.split, i * n + seg.ring_free0[j])
                        index = i * n + (seg.slot_base + j)
                        src = weights[index] if isinstance(index, int) else weights[bass.ds(index, 1)].rearrange("a p c -> (a p) c")
                        sp.dma_start(p.ring[:, s, 0:cols], src[:, 0:cols]).then_inc(p.full[s], 16)
                repeat(sp, seg.iters, body)

        first = p.order[0]

        @p.block.scalar
        def _(act):
            round_slot(p, act, first, 0, 0)

        @p.block.vector
        def _(dve):
            rest_slot(p, dve, first, 0, 0)

        x_tiles = ((0, P), (P, P))
        from_tokens(p, mem_in, p.mem, x_tiles, p.mem_loaded, 3)
        p.a0 = first_a0
        meta_h = ctx.enter_context(nc.sbuf_tensor("meta_h", [P, KD, N_META], F32))
        for layer in range(2):
            memory_heads(p, layer)
        from_tokens(p, tok_in, p.h, x_tiles, p.loaded, 3)
        from_tokens(p, meta_tok, meta_h, ((0, N_META),), p.loaded, 3)
        stages = [
            lambda: layer_even(p), lambda: cross_attention(p, 0), lambda: dense_ffn(p),
            lambda: layer_odd(p), lambda: cross_attention(p, 1), lambda: moe(p),
        ]
        for stage in stages:
            stage()
        @p.block.vector
        def _(dve):
            p.dve_steps.link(dve, dve.tensor_copy(p.u[:, :, 0:SEQ], p.h[:, :, 0:SEQ]))
            dve.tensor_copy(p.h[:, :, N_META:L2], p.u[:, :, 0:SEQ])
            dve.tensor_copy(p.h[:, :, 0:N_META], meta_h[:])

        p.stage_end()
        p.a0 = 0
        for layer in range(2):
            layer_two(p, layer)
            mlp_two(p, layer)
        res, _ = p.area(0, 2, D)
        to_tokens(p, p.h, KD, ((N_META, P), (N_META + P, P)), res)

        @p.block.sync
        def _(sp):
            sp.wait_ge(p.stage_done, 3 * p.stages)
            sp.dma_start(out[0].rearrange("(i p) d -> p i d", p=P), res).then_inc(p.stored, 16)
            sp.wait_ge(p.stored, 16)


def pack_weights(a):
    _, order, n_slots = plan_stream()
    w = np.zeros((n_slots, P, SLOT), np.asarray(a["x"]).dtype)
    at = 0

    def wide(m):
        nonlocal at
        m = np.asarray(m)
        n = m.shape[1] // 256
        w[at:at + n] = m.reshape(KD, P, n, 256).transpose(2, 1, 0, 3).reshape(n, P, SLOT)
        at += n

    def deep(m):
        nonlocal at
        m = np.asarray(m)
        kt = m.shape[0] // P
        parts = 1 if kt <= 16 else 2
        c = m.reshape(parts, kt // parts, P, 8, P).transpose(3, 0, 2, 1, 4).reshape(8 * parts, P, kt // parts * P)
        w[at:at + 8 * parts, :, 0:c.shape[2]] = c
        at += 8 * parts

    def flat(m):
        nonlocal at
        w[at] = np.asarray(m).reshape(2, P, D).transpose(1, 0, 2).reshape(P, SLOT)
        at += 1

    def pairs(m):
        m = np.asarray(m)
        f = m.shape[1] // 2 // P
        wide(m.reshape(D, 2, f, P).transpose(0, 2, 1, 3).reshape(D, 2 * f * P))

    wide(a["xa_w_kv"][0])
    wide(a["xa_w_kv"][1])
    wide(a["ev_w_in"][0])
    wide(a["ev_w_out"][0])
    wide(a["xa_w_q"][0])
    flat(a["xa_w_o"][0])
    pairs(a["ff_w_gu"][0])
    deep(a["ff_w_down"][0])
    wide(a["od_w_in"][0][:, 0:4 * D])
    wide(a["od_w_out"][0])
    wide(a["xa_w_q"][1])
    flat(a["xa_w_o"][1])
    for e in range(N_EXPERTS):
        first = at
        at += 1
        pairs(a["moe_w_gu"][0, e])
        w[first, :, 0:SLOT // 2] = w[first + 1, :, 0:SLOT // 2]
        w[first + 1, :, 0:SLOT // 2] = w[first + 1, :, SLOT // 2:]
        deep(a["moe_w_down"][0, e])
    for l in range(2):
        m = np.asarray(a["w_in_2"][l])
        wide(m[:, 2048:6144])
        wide(m[:, 0:2048])
        wide(m[:, 6176:7200])
        wide(m[:, 7200:7712])
        wide(m[:, 7712:9760])
        deep(a["w_ssd_down_2"][l])
        wide(a["w_attn_down_2"][l])
        wide(a["w_o_2"][l])
        wide(a["w_mlp_up_2"][l])
        deep(a["w_mlp_down_2"][l])
    assert at == n_slots
    return w


def pack_params(a):
    ch = lambda v: np.asarray(v).reshape(-1, P).T
    twice = lambda v: np.concatenate([np.asarray(v), np.asarray(v)], axis=-1).reshape(-1, P).T
    tiles = lambda m: np.asarray(m).reshape(KD, P, -1).transpose(1, 0, 2).reshape(P, -1)

    def rows(v):
        v = np.asarray(v)
        v = v.reshape(-1, v.shape[-1])
        out = np.zeros((P, v.shape[0]), np.float32)
        out[0:v.shape[1]] = v.T
        return out

    skip = np.asarray(a["d_skip_2"])
    parts = {
        "norm_mix": ch(a["norm_mix"]), "norm_xattn": ch(a["norm_xattn"]), "norm_mem": ch(a["norm_mem"]),
        "norm_ffn": ch(a["norm_ffn"]), "ev_conv": ch(a["ev_conv"]), "ev_q_norm": twice(a["ev_q_norm"]),
        "ev_k_norm": twice(a["ev_k_norm"]), "od_conv": ch(a["od_conv"]), "od_o_norm": ch(a["od_o_norm"]),
        "od_a_log": rows(a["od_a_log"]), "od_dt_bias": rows(a["od_dt_bias"]),
        "xa_q_norm": twice(a["xa_q_norm"]), "xa_k_norm": twice(a["xa_k_norm"]),
        "od_small": tiles(np.asarray(a["od_w_in"])[0][:, 4 * D:]), "router": tiles(a["moe_router"][0]),
        "norm1": ch(a["norm1_g_2"]), "norm2": ch(a["norm2_g_2"]), "conv_w": ch(a["conv_w_2"]), "conv_b": ch(a["conv_b_2"]),
        "b_gate": ch(a["b_gate_2"]), "d_skip": ch(np.repeat(skip, 64, axis=-1)), "ssd_norm": ch(a["ssd_norm_g_2"]),
        "q_norm": twice(a["q_norm_g_2"]), "k_norm": twice(a["k_norm_g_2"]),
        "dt_bias": rows(a["dt_bias_2"]), "a_log": rows(a["a_log_2"]),
        "w_dt": np.concatenate([tiles(np.asarray(a["w_in_2"])[l][:, 6144:6176]) for l in range(2)], axis=1),
        "sinks": np.broadcast_to(np.asarray(a["sinks_2"]).reshape(1, 32), (P, 32)),
    }
    for name, n in PARAMS:
        assert parts[name].shape == (P, n), (name, parts[name].shape, n)
    return np.concatenate([parts[name] for name, _ in PARAMS], axis=1).astype(np.float32)


def make_consts():
    f = np.float32
    i = np.arange(P)
    out = {"ident": np.eye(P), "ones": np.ones((P, P))}
    out["whole_col"] = np.zeros((P, 31))
    out["whole_col"][:, 15] = 1
    out["half_cols"] = np.zeros((P, 38))
    out["half_cols"][0:64, 18] = 1
    out["half_cols"][64:, 19] = 1
    s = np.zeros((P, P))
    for r in range(P):
        if r % 64 < 32:
            s[r + 32, r] = -1
        else:
            s[r - 32, r] = 1
    out["swap"] = s
    t, j = np.arange(SEQ)[:, None], np.arange(SEQ)[None]
    count = np.zeros((SEQ, SEQ))
    for window, d in ((128, 1), (512, 4), (2048, 16)):
        count += (j <= t) & ((t - j) % d == 0) & ((t - j) // d <= window // d)
    m = np.where(count > 0, np.log(np.maximum(count, 1)), NEG)
    out["dilated"] = np.concatenate([m[0:P], m[P:]], axis=1)
    w = np.zeros((P, 3 * L2))
    for n, (first, rows) in enumerate(CHUNKS2):
        q, k = np.arange(first, first + rows)[:, None], np.arange(L2)[None]
        w[0:rows, n * L2:(n + 1) * L2] = np.where((k <= q) & ((k < N_META) | (q - k < WINDOW)), 0.0, NEG)
    out["window"] = w
    inv = f(10000.0) ** (-np.arange(32, dtype=f) / f(32))
    ang = np.arange(L2, dtype=f)[:, None] * inv[None, :].astype(f)
    out["cos"] = np.cos(ang).astype(f)[:, i % 32].T
    out["sin"] = np.sin(ang).astype(f)[:, i % 32].T
    lv = []
    for l in range(DELTA_LEVELS):
        b = 2 << l
        jj, ii = i[:, None], i[None]
        lv.append((jj // b == ii // b) & (ii % b >= b // 2) & (jj % b < b // 2))
    out["levels"] = np.concatenate(lv, axis=1)
    out["below"] = np.where(i[None] >= i[:, None], 0.0, NEG)
    out["iota"] = np.broadcast_to(np.arange(8), (P, 8))
    return np.concatenate([out[name].astype(f) for name, _ in CONSTS], axis=1)


def kernel(**inputs):
    import concourse.bacc as bacc
    from concourse.bass_utils import run_bass_kernel_spmd

    a = {k: np.asarray(v) for k, v in inputs.items()}
    arrays = {
        "in_weights": pack_weights(a), "in_params": pack_params(a), "in_consts": make_consts(),
        "in_x": np.ascontiguousarray(a["x"]), "in_mem": np.ascontiguousarray(a["mem"]),
        "in_meta": np.ascontiguousarray(a["meta_tokens_2"]),
    }
    nc = bacc.Bacc("TRN2", target_bir_lowering=False, num_devices=1)
    aps = [nc.dram_tensor(n, v.shape, F32, kind="ExternalInput").ap() for n, v in arrays.items()]
    out = nc.dram_tensor("out_h", (1, SEQ, D), F32, kind="ExternalOutput").ap()
    build(nc, *aps, out)
    r = run_bass_kernel_spmd(nc, [arrays], core_ids=[0])
    return r.results[0]["out_h"]
```
